# Optimizing a Trainium2 kernel written in Bass

```python
import math
import jax
import jax.numpy as jnp
from jax import lax
import numpy as np

D_MODEL = 1024
BATCH = 1
SEQ = 512
DEPTH = 2
DEC_BATCH = 8
DEC_SEQ = 1
PAST_LEN = 1024
PAGE_SIZE = 128

HEAD_DIM = 64
A_HEADS = 4
A_KV_HEADS = 2
IDX_HEADS = 4
IDX_DIM = 64
TOPK_MAX = 256
B_HEADS = 4
C_HEADS = 4
D_HEADS = 4
D_GROUPS = 2
D_STATE = 128
D_CONV = 4
D_FF = 2816
FFN_CONV = 3
N_BRANCH = 4
ROPE_THETA = 10000.0
Q_BLOCK = 128
CHUNK = 128
EPS = 1e-6
NEG = -1e30

A_Q = A_HEADS * HEAD_DIM
A_KV = A_KV_HEADS * HEAD_DIM
A_IQ = IDX_HEADS * IDX_DIM
B_W = B_HEADS * HEAD_DIM
C_W = C_HEADS * HEAD_DIM
D_W = D_HEADS * HEAD_DIM
D_BC = D_GROUPS * D_STATE
D_CONV_CH = D_W + 2 * D_BC
IN_SPLITS = (A_Q, A_KV, A_KV, A_IQ, IDX_DIM, IDX_HEADS, B_W, B_W, B_W, C_W, C_W, C_W, C_HEADS, C_HEADS, C_W, D_W, D_CONV_CH, D_HEADS, N_BRANCH * D_MODEL)
IN_W = sum(IN_SPLITS)

kernel_name = 'hybrid_dsa_stickbreak_mlstm_ssd_convffn_step'

f32 = jnp.float32

def rms_norm(x, w):
    xf = x.astype(f32)
    y = xf * lax.rsqrt(jnp.mean(xf * xf, axis=-1, keepdims=True) + EPS)
    return (y * w.astype(f32)).astype(x.dtype)

def rope(x, pos):
    half = x.shape[-1] // 2
    inv = jnp.power(ROPE_THETA, -jnp.arange(half, dtype=f32) / half)
    ang = pos.astype(f32)[:, None] * inv[None, :]
    cos = jnp.cos(ang)[None, :, None, :]
    sin = jnp.sin(ang)[None, :, None, :]
    xf = x.astype(f32)
    x1, x2 = xf[..., :half], xf[..., half:]
    return jnp.concatenate([x1 * cos - x2 * sin, x2 * cos + x1 * sin], axis=-1).astype(x.dtype)

def causal_dwconv(x, buf, w, b):
    width, t = w.shape[0], x.shape[1]
    xx = jnp.concatenate([buf.astype(x.dtype), x], axis=1)
    y = b + xx[:, 0:t] * w[0]
    for j in range(1, width):
        y = y + xx[:, j:j + t] * w[j]
    return y, xx[:, t:]

def to_chunks(a, c):
    return jnp.moveaxis(a.reshape((a.shape[0], a.shape[1] // c, c) + a.shape[2:]), 1, 0)

def from_chunks(a):
    a = jnp.moveaxis(a, 0, 1)
    return a.reshape((a.shape[0], a.shape[1] * a.shape[2]) + a.shape[3:])

def sweep_query_blocks(fn, batched, pos):
    t = pos.shape[0]
    blk = min(Q_BLOCK, t)
    xs = tuple(to_chunks(a, blk) for a in batched) + (pos.reshape(t // blk, blk),)
    return from_chunks(lax.map(lambda args: fn(*args), xs))

def take_rows(rows, idx):
    return jax.vmap(lambda r, i: r[i])(rows, idx)

def gather_past(pool, page_table):
    g = pool[page_table]
    return g.reshape((g.shape[0], g.shape[1] * g.shape[2]) + g.shape[3:])

def gather_rows(pool, page_table, new_rows, idx):
    ps = pool.shape[1]
    past = page_table.shape[1] * ps
    is_past = idx < past
    lp = jnp.minimum(idx, past - 1)
    phys = jax.vmap(lambda pt, l: pt[l // ps])(page_table, lp)
    from_pool = pool[phys, lp % ps]
    from_new = take_rows(new_rows, jnp.clip(idx - past, 0, new_rows.shape[1] - 1))
    sel = is_past.reshape(is_past.shape + (1,) * (pool.ndim - 2))
    return jnp.where(sel, from_pool.astype(from_new.dtype), from_new)

def dsa_block(q, iq, iw, qpos, kidx, gather_kv, topk):
    bsz, tb = q.shape[0], q.shape[1]
    s = jnp.einsum('bthd,bld->bthl', iq.astype(f32), kidx.astype(f32))
    score = jnp.einsum('bth,bthl->btl', iw.astype(f32), jax.nn.relu(s))
    admissible = jnp.arange(kidx.shape[1])[None, :] <= qpos[:, None]
    score = jnp.where(admissible[None], score, NEG)
    _, idx = lax.top_k(score, topk)
    valid = idx <= qpos[None, :, None]
    k_sel, v_sel = gather_kv(idx)
    qg = q.reshape(bsz, tb, A_KV_HEADS, A_HEADS // A_KV_HEADS, HEAD_DIM).astype(f32)
    logits = jnp.einsum('btjgd,btnjd->btjgn', qg, k_sel.astype(f32)) * (HEAD_DIM ** -0.5)
    logits = jnp.where(valid[:, :, None, None, :], logits, NEG)
    p = jax.nn.softmax(logits, axis=-1)
    o = jnp.einsum('btjgn,btnjd->btjgd', p, v_sel.astype(f32))
    return o.reshape(bsz, tb, A_Q).astype(q.dtype)

def stickbreak_block(q, qpos, k, v):
    bsz, tb = q.shape[0], q.shape[1]
    z = jnp.einsum('bthd,blhd->bhtl', q.astype(f32), k.astype(f32)) * (HEAD_DIM ** -0.5)
    mask = (jnp.arange(k.shape[1])[None, :] < qpos[:, None])[None, None]
    log_keep = jnp.where(mask, jax.nn.log_sigmoid(-z), 0.0)
    after = lax.cumsum(log_keep, axis=3, reverse=True) - log_keep
    a = jnp.where(mask, jnp.exp(jax.nn.log_sigmoid(z) + after), 0.0)
    o = jnp.einsum('bhtl,blhd->bthd', a, v.astype(f32))
    return o.reshape(bsz, tb, B_W).astype(q.dtype)

def mlstm_scan(q, k, v, ig, lf, c0, n0, m0):
    c = min(CHUNK, q.shape[1])
    causal = jnp.tril(jnp.ones((c, c), dtype=bool))[None, :, :, None]

    def step(carry, xs):
        cm, nv, m = carry
        qc, kc, vc, ic, fc = xs
        b = jnp.cumsum(fc, axis=1)
        logw = jnp.where(causal, b[:, :, None, :] - b[:, None, :, :] + ic[:, None, :, :], -jnp.inf)
        log_inter = b + m[:, None, :]
        mt = jnp.maximum(log_inter, jnp.max(logw, axis=2))
        sc = jnp.einsum('bthd,bshd->btsh', qc, kc) * jnp.exp(logw - mt[:, :, None, :])
        w_inter = jnp.exp(log_inter - mt)
        num = jnp.einsum('btsh,bshe->bthe', sc, vc) + w_inter[..., None] * jnp.einsum('bhed,bthd->bthe', cm, qc)
        den = jnp.sum(sc, axis=2) + w_inter * jnp.einsum('bhd,bthd->bth', nv, qc)
        h = num / jnp.maximum(jnp.abs(den), jnp.exp(-mt))[..., None]
        b_end = b[:, -1, :]
        log_u = b_end[:, None, :] - b + ic
        m_new = jnp.maximum(b_end + m, jnp.max(log_u, axis=1))
        u = jnp.exp(log_u - m_new[:, None, :])
        decay = jnp.exp(b_end + m - m_new)
        cm_new = decay[..., None, None] * cm + jnp.einsum('bsh,bshe,bshd->bhed', u, vc, kc)
        nv_new = decay[..., None] * nv + jnp.einsum('bsh,bshd->bhd', u, kc)
        return (cm_new, nv_new, m_new), h

    (c1, n1, m1), h = lax.scan(step, (c0, n0, m0), tuple(to_chunks(a, c) for a in (q, k, v, ig, lf)))
    return from_chunks(h), c1, n1, m1

def ssd_scan(x, dt, a_neg, bm, cm, h0):
    c = min(CHUNK, x.shape[1])
    causal = jnp.tril(jnp.ones((c, c), dtype=bool))[None, :, :, None]

    def step(h, xs):
        xc, dtc, bc, cc = xs
        acum = jnp.cumsum(dtc * a_neg, axis=1)
        decay = jnp.exp(jnp.where(causal, acum[:, :, None, :] - acum[:, None, :, :], -jnp.inf))
        sc = jnp.einsum('bthn,bshn->btsh', cc, bc) * decay
        y = jnp.einsum('btsh,bsh,bshp->bthp', sc, dtc, xc) + jnp.exp(acum)[..., None] * jnp.einsum('bthn,bhpn->bthp', cc, h)
        a_end = acum[:, -1, :]
        wts = jnp.exp(a_end[:, None, :] - acum) * dtc
        h_new = jnp.exp(a_end)[..., None, None] * h + jnp.einsum('bsh,bshn,bshp->bhpn', wts, bc, xc)
        return h_new, y

    h1, y = lax.scan(step, h0, tuple(to_chunks(a, c) for a in (x, dt, bm, cm)))
    return from_chunks(y), h1

def token_mix(xn, pos, w, st):
    bsz, t = xn.shape[0], xn.shape[1]
    offs = np.cumsum(IN_SPLITS)[:-1].tolist()
    (a_q, a_k, a_v, a_iq, a_ik, a_iw, b_q, b_k, b_v, c_q, c_k, c_v, c_i, c_f, c_o,
     d_z, d_xbc, d_dt, gate) = jnp.split(xn @ w['w_in'], offs, axis=-1)

    qa = rope(a_q.reshape(bsz, t, A_HEADS, HEAD_DIM), pos)
    ka = rope(a_k.reshape(bsz, t, A_KV_HEADS, HEAD_DIM), pos)
    va = a_v.reshape(bsz, t, A_KV_HEADS, HEAD_DIM)
    iq = rope(a_iq.reshape(bsz, t, IDX_HEADS, IDX_DIM), pos)
    ik = rope(a_ik[:, :, None, :], pos)[:, :, 0, :]
    iw = a_iw * (IDX_HEADS ** -0.5 * IDX_DIM ** -0.5)
    if st is None:
        kidx_all = ik

        def gather_kv(idx):
            return take_rows(ka, idx), take_rows(va, idx)
    else:
        pt = st['page_table']
        kidx_all = jnp.concatenate([gather_past(st['a_kidx'], pt).astype(ik.dtype), ik], axis=1)

        def gather_kv(idx):
            return gather_rows(st['a_k'], pt, ka, idx), gather_rows(st['a_v'], pt, va, idx)
    topk = min(TOPK_MAX, kidx_all.shape[1] // 4)
    o_a = sweep_query_blocks(lambda q_, iq_, iw_, qp: dsa_block(q_, iq_, iw_, qp, kidx_all, gather_kv, topk), (qa, iq, iw), pos)

    qb = b_q.reshape(bsz, t, B_HEADS, HEAD_DIM)
    kb = b_k.reshape(bsz, t, B_HEADS, HEAD_DIM)
    vb = b_v.reshape(bsz, t, B_HEADS, HEAD_DIM)
    if st is None:
        kb_all, vb_all = kb, vb
    else:
        kb_all = jnp.concatenate([gather_past(st['b_k'], pt).astype(kb.dtype), kb], axis=1)
        vb_all = jnp.concatenate([gather_past(st['b_v'], pt).astype(vb.dtype), vb], axis=1)
    o_b = sweep_query_blocks(lambda q_, qp: stickbreak_block(q_, qp, kb_all, vb_all), (qb,), pos)

    qc = c_q.reshape(bsz, t, C_HEADS, HEAD_DIM).astype(f32)
    kc = c_k.reshape(bsz, t, C_HEADS, HEAD_DIM).astype(f32) * (HEAD_DIM ** -0.5)
    vc = c_v.reshape(bsz, t, C_HEADS, HEAD_DIM).astype(f32)
    ig = (c_i + w['c_b_i']).astype(f32)
    lf = jax.nn.log_sigmoid((c_f + w['c_b_f']).astype(f32))
    if st is None:
        c0 = jnp.zeros((bsz, C_HEADS, HEAD_DIM, HEAD_DIM), f32)
        n0 = jnp.zeros((bsz, C_HEADS, HEAD_DIM), f32)
        m0 = jnp.zeros((bsz, C_HEADS), f32)
    else:
        c0, n0, m0 = st['c_C'].astype(f32), st['c_n'].astype(f32), st['c_m'].astype(f32)
    hc, c1, n1, m1 = mlstm_scan(qc, kc, vc, ig, lf, c0, n0, m0)
    hc = hc * lax.rsqrt(jnp.mean(hc * hc, axis=-1, keepdims=True) + EPS)
    o_c = (jax.nn.sigmoid(c_o.astype(f32)) * hc.reshape(bsz, t, C_W) * w['c_norm'].astype(f32)).astype(xn.dtype)

    conv_buf = jnp.zeros((bsz, D_CONV - 1, D_CONV_CH), xn.dtype) if st is None else st['d_conv']
    xbc, conv_new = causal_dwconv(d_xbc, conv_buf, w['d_conv_w'], w['d_conv_b'])
    xbc = jax.nn.silu(xbc)
    dx, dbm, dcm = jnp.split(xbc, [D_W, D_W + D_BC], axis=-1)
    rep = D_HEADS // D_GROUPS
    dx = dx.reshape(bsz, t, D_HEADS, HEAD_DIM).astype(f32)
    dbm = jnp.repeat(dbm.reshape(bsz, t, D_GROUPS, D_STATE), rep, axis=2).astype(f32)
    dcm = jnp.repeat(dcm.reshape(bsz, t, D_GROUPS, D_STATE), rep, axis=2).astype(f32)
    dt = jax.nn.softplus((d_dt + w['d_dt_bias']).astype(f32))
    a_neg = -jnp.exp(w['d_A_log'].astype(f32))
    h0 = jnp.zeros((bsz, D_HEADS, HEAD_DIM, D_STATE), f32) if st is None else st['d_ssm'].astype(f32)
    yd, h1 = ssd_scan(dx, dt, a_neg, dbm, dcm, h0)
    yd = yd + w['d_D'].astype(f32)[:, None] * dx
    o_d = rms_norm(yd.reshape(bsz, t, D_W) * jax.nn.silu(d_z.astype(f32)), w['d_norm']).astype(xn.dtype)

    g = jax.nn.sigmoid(gate.reshape(bsz, t, N_BRANCH, D_MODEL))
    merged = (g[:, :, 0] * (o_a @ w['w_br_a']) + g[:, :, 1] * (o_b @ w['w_br_b'])
              + g[:, :, 2] * (o_c @ w['w_br_c']) + g[:, :, 3] * (o_d @ w['w_br_d']))
    return merged @ w['w_out'], (ka, va, ik, kb, vb, c1, n1, m1, conv_new, h1)

def layer(x, pos, w, st):
    mix, new_state = token_mix(rms_norm(x, w['norm_mix_pre']), pos, w, st)
    x = x + rms_norm(mix, w['norm_mix_post'])
    u = rms_norm(x, w['norm_ffn_pre']) @ w['ffn_up']
    buf = jnp.zeros((x.shape[0], FFN_CONV - 1, 2 * D_FF), x.dtype) if st is None else st['ffn_conv']
    u, ffn_buf = causal_dwconv(u, buf, w['ffn_conv_w'], w['ffn_conv_b'])
    val, gte = jnp.split(u, 2, axis=-1)
    f = (val * jax.nn.gelu(gte, approximate=True)) @ w['ffn_down']
    x = x + rms_norm(f, w['norm_ffn_post'])
    return x, new_state + (ffn_buf,)

def setup_inputs(seed: int = 0) -> dict:
    key = jax.random.key(seed)
    keys = jax.random.split(key, 48)
    counter = [0]

    def nk():
        counter[0] += 1
        return keys[counter[0] - 1]

    def nrm(shape, scale=1.0):
        return scale * jax.random.normal(nk(), shape, f32)

    n_pages = PAST_LEN // PAGE_SIZE
    n_used = DEC_BATCH * n_pages
    n_pool = (5 * n_used + 3) // 4
    page_table = jax.random.permutation(nk(), n_pool)[:n_used].reshape(DEC_BATCH, n_pages).astype(jnp.int32)
    dt0 = jnp.exp(jax.random.uniform(nk(), (DEPTH, D_HEADS), f32, math.log(1e-3), math.log(1e-1)))
    return {
        'x_prompt': nrm((BATCH, SEQ, D_MODEL)),
        'x_sample': nrm((DEC_BATCH, DEC_SEQ, D_MODEL)),
        'cache_a_k': nrm((DEPTH, n_pool, PAGE_SIZE, A_KV_HEADS, HEAD_DIM)),
        'cache_a_v': nrm((DEPTH, n_pool, PAGE_SIZE, A_KV_HEADS, HEAD_DIM)),
        'cache_a_kidx': nrm((DEPTH, n_pool, PAGE_SIZE, IDX_DIM)),
        'cache_b_k': nrm((DEPTH, n_pool, PAGE_SIZE, B_HEADS, HEAD_DIM)),
        'cache_b_v': nrm((DEPTH, n_pool, PAGE_SIZE, B_HEADS, HEAD_DIM)),
        'state_c_C': nrm((DEPTH, DEC_BATCH, C_HEADS, HEAD_DIM, HEAD_DIM)),
        'state_c_n': nrm((DEPTH, DEC_BATCH, C_HEADS, HEAD_DIM)),
        'state_c_m': nrm((DEPTH, DEC_BATCH, C_HEADS), 0.5),
        'state_d_conv': nrm((DEPTH, DEC_BATCH, D_CONV - 1, D_CONV_CH)),
        'state_d_ssm': nrm((DEPTH, DEC_BATCH, D_HEADS, HEAD_DIM, D_STATE), 0.5),
        'state_ffn_conv': nrm((DEPTH, DEC_BATCH, FFN_CONV - 1, 2 * D_FF)),
        'page_table': page_table,
        'norm_mix_pre': 1.0 + nrm((DEPTH, D_MODEL), 0.05),
        'norm_mix_post': 1.0 + nrm((DEPTH, D_MODEL), 0.05),
        'w_in': nrm((DEPTH, D_MODEL, IN_W), D_MODEL ** -0.5),
        'c_b_i': nrm((DEPTH, C_HEADS), 0.1),
        'c_b_f': jnp.linspace(3.0, 6.0, C_HEADS, dtype=f32)[None, :] + nrm((DEPTH, C_HEADS), 0.1),
        'c_norm': 1.0 + nrm((DEPTH, C_W), 0.05),
        'd_conv_w': nrm((DEPTH, D_CONV, D_CONV_CH), D_CONV ** -0.5),
        'd_conv_b': nrm((DEPTH, D_CONV_CH), 0.02),
        'd_dt_bias': dt0 + jnp.log(-jnp.expm1(-dt0)),
        'd_A_log': jnp.log(jax.random.uniform(nk(), (DEPTH, D_HEADS), f32, 1.0, 16.0)),
        'd_D': 1.0 + nrm((DEPTH, D_HEADS), 0.1),
        'd_norm': 1.0 + nrm((DEPTH, D_W), 0.05),
        'w_br_a': nrm((DEPTH, A_Q, D_MODEL), A_Q ** -0.5),
        'w_br_b': nrm((DEPTH, B_W, D_MODEL), B_W ** -0.5),
        'w_br_c': nrm((DEPTH, C_W, D_MODEL), C_W ** -0.5),
        'w_br_d': nrm((DEPTH, D_W, D_MODEL), D_W ** -0.5),
        'w_out': nrm((DEPTH, D_MODEL, D_MODEL), D_MODEL ** -0.5),
        'norm_ffn_pre': 1.0 + nrm((DEPTH, D_MODEL), 0.05),
        'norm_ffn_post': 1.0 + nrm((DEPTH, D_MODEL), 0.05),
        'ffn_up': nrm((DEPTH, D_MODEL, 2 * D_FF), D_MODEL ** -0.5),
        'ffn_conv_w': nrm((DEPTH, FFN_CONV, 2 * D_FF), FFN_CONV ** -0.5),
        'ffn_conv_b': nrm((DEPTH, 2 * D_FF), 0.02),
        'ffn_down': nrm((DEPTH, D_FF, D_MODEL), D_FF ** -0.5),
    }

def reference(x_prompt, x_sample, cache_a_k, cache_a_v, cache_a_kidx, cache_b_k, cache_b_v,
              state_c_C, state_c_n, state_c_m, state_d_conv, state_d_ssm, state_ffn_conv, page_table,
              norm_mix_pre, norm_mix_post, w_in, c_b_i, c_b_f, c_norm, d_conv_w, d_conv_b, d_dt_bias,
              d_A_log, d_D, d_norm, w_br_a, w_br_b, w_br_c, w_br_d, w_out, norm_ffn_pre, norm_ffn_post,
              ffn_up, ffn_conv_w, ffn_conv_b, ffn_down):
    past = page_table.shape[1] * cache_a_k.shape[2]
    pos_p = jnp.arange(x_prompt.shape[1], dtype=jnp.int32)
    pos_s = past + jnp.arange(x_sample.shape[1], dtype=jnp.int32)
    xp, xs = x_prompt, x_sample
    p_list, s_list = [], []
    for l in range(DEPTH):
        w = {'norm_mix_pre': norm_mix_pre[l], 'norm_mix_post': norm_mix_post[l], 'w_in': w_in[l],
             'c_b_i': c_b_i[l], 'c_b_f': c_b_f[l], 'c_norm': c_norm[l], 'd_conv_w': d_conv_w[l],
             'd_conv_b': d_conv_b[l], 'd_dt_bias': d_dt_bias[l], 'd_A_log': d_A_log[l], 'd_D': d_D[l],
             'd_norm': d_norm[l], 'w_br_a': w_br_a[l], 'w_br_b': w_br_b[l], 'w_br_c': w_br_c[l],
             'w_br_d': w_br_d[l], 'w_out': w_out[l], 'norm_ffn_pre': norm_ffn_pre[l],
             'norm_ffn_post': norm_ffn_post[l], 'ffn_up': ffn_up[l], 'ffn_conv_w': ffn_conv_w[l],
             'ffn_conv_b': ffn_conv_b[l], 'ffn_down': ffn_down[l]}
        st = {'page_table': page_table, 'a_k': cache_a_k[l], 'a_v': cache_a_v[l], 'a_kidx': cache_a_kidx[l],
              'b_k': cache_b_k[l], 'b_v': cache_b_v[l], 'c_C': state_c_C[l], 'c_n': state_c_n[l],
              'c_m': state_c_m[l], 'd_conv': state_d_conv[l], 'd_ssm': state_d_ssm[l],
              'ffn_conv': state_ffn_conv[l]}
        xp, sp = layer(xp, pos_p, w, None)
        xs, ss = layer(xs, pos_s, w, st)
        p_list.append(sp)
        s_list.append(ss)
    p_st = [jnp.stack([sl[i] for sl in p_list]) for i in range(11)]
    s_st = [jnp.stack([sl[i] for sl in s_list]) for i in range(11)]
    (p_a_k, p_a_v, p_a_kidx, p_b_k, p_b_v, p_c_C, p_c_n, p_c_m, p_d_conv, p_d_ssm, p_ffn_conv) = p_st
    (s_a_k, s_a_v, s_a_kidx, s_b_k, s_b_v, s_c_C, s_c_n, s_c_m, s_d_conv, s_d_ssm, s_ffn_conv) = s_st
    return (xp, xs, p_a_k, p_a_v, p_a_kidx, p_b_k, p_b_v, p_c_C, p_c_n, p_c_m, p_d_conv, p_d_ssm, p_ffn_conv,
            s_a_k, s_a_v, s_a_kidx, s_b_k, s_b_v, s_c_C, s_c_n, s_c_m, s_d_conv, s_d_ssm, s_ffn_conv)


_drawn_inputs = setup_inputs


def setup_inputs(seed=0):
    import zlib

    import numpy as np

    out = dict(_drawn_inputs(seed))
    spreads = {}
    factors = {}
    for name, (base, spread) in spreads.items():
        noise = np.random.default_rng([zlib.crc32(name.encode()), seed]).standard_normal(out[name].shape)
        drawn = base * np.exp(spread * noise) if base else spread * noise
        out[name] = jnp.asarray(drawn.astype(out[name].dtype))
    for name, factor in factors.items():
        out[name] = (out[name] * factor).astype(out[name].dtype)
    return out
```

```python
import concourse.bass as bass
from concourse import mybir
from contextlib import ExitStack

L = 2
NPR = 512
NSM = 8
TOK = NPR + NSM
HALF = TOK // 2
DM = 1024
KD = DM // 128
DFF = 2816
JF = DFF // 128
NT = NPR // 128
PAGES = 8
PAST = 1024
POOL = 80
HD = 64
TOPK_P = 128
TOPK_S = 256
RING = 4
SLOT = 8 * 128
NEG = -1e30
TAKEN = -3e38
EPS = 1e-6

AQ, AK, AV, IQ, SM, BQ, BK, BV, CQ, CK, CV, CO, DZ, XX, XB, XC = (
    0, 2, 3, 4, 6, 7, 9, 11, 13, 15, 17, 19, 21, 23, 25, 27)
NPROJ = 29
IKD = 29
NF = 31
MERGED = 23
T_SM, T_AV, T_BV, T_CK, T_CV, T_XX, T_XB = -1, 0, 1, 3, 5, 7, 9
TO_TM = [(SM, T_SM), (AV, T_AV), (BV, T_BV), (BV + 1, T_BV + 1), (CK, T_CK), (CK + 1, T_CK + 1),
         (CV, T_CV), (CV + 1, T_CV + 1), (XX, T_XX), (XX + 1, T_XX + 1), (XB, T_XB), (XB + 1, T_XB + 1)]
V_NPRE, V_NPOST, V_FPRE, V_FPOST, V_CN, V_DN, V_DCW, V_DCB = 0, 8, 16, 24, 32, 34, 36, 60
V_FCW, V_FCB, V_D, V_BI, V_BFD, V_AL, V_SBI, V_SBF, V_SBD, V_SAL = 66, 198, 242, 244, 248, 256, 260, 262, 264, 266
NV = 268
S_N, S_M, S_DC, S_FC = 0, 16, 32, 176
NST = 880
C_ID, C_ONE, C_TRI, C_NTRI, C_NONE, C_PERM, C_DUP1, C_DUP2, C_BLK = (128 * i for i in range(9))
C_SEL = 1152
C_SELP = C_SEL + 512
C_SELS = C_SEL
C_AIW = C_SELP + 256
C_EM = C_AIW + 32
C_EB = C_EM + 8
C_SGN = C_EB + 32
C_EPS = C_SGN + 8
C_COS = C_EPS + 1
C_SIN = C_COS + TOK
NC_ = C_SIN + TOK
OFF = [0, 512, 896, 1152]
TRI_W = 1280
UNITS = ([("ki", b) for b in range(NSM)] + [(k, b) for b in range(NSM) for k in ("kb0", "kb1")]
         + [(v, b) for b in range(NSM) for v in ("vb0", "vb1")] + [("ka", b) for b in range(NSM)]
         + [("va", b) for b in range(NSM)])


class Signal:

    def __init__(self, sem, per):
        self.sem, self.per, self.n = sem, per, 0

    def nth(self, l, k):
        return self.sem, l * self.per + k + 1

    def all(self, l):
        return self.sem, (l + 1) * self.per


def trunk_kernel(nc, x_in, pages, consts, vecs, states, c_state, d_state, ki_c, ka_c, va_c, kb_c, vb_c,
                 w_proj, w_gate, w_br, w_out, w_up, w_down,
                 y_out, ka_o, va_o, ki_o, kb_o, vb_o, pc_o, pn_o, pm_o, dconv_o, dconv_s_o, pssm_o,
                 fconv_o, fconv_s_o, sc_o, sn_o, sm_o, sssm_o):
    f32 = mybir.dt.float32
    ALU = mybir.AluOpType
    ACT = mybir.ActivationFunctionType
    AX = mybir.AxisListType.X
    ctx = ExitStack()
    with ctx:
        def sb(name, shape, dt=f32):
            return ctx.enter_context(nc.sbuf_tensor(name, shape, dt))

        signals = []

        def sig(name, per):
            s = Signal(ctx.enter_context(nc.semaphore(name)), per)
            signals.append((name, s))
            return s

        X = sb("X", [128, KD, TOK])
        XN = sb("XN", [128, KD, TOK])
        F = sb("F", [128, NF, TOK])
        TM = sb("TM", [128, 11, NT, 128])
        R = sb("R", [128, RING, SLOT])
        S = sb("S", [128, 5, TOK])
        B1 = sb("B1", [128, TRI_W])
        B2 = sb("B2", [128, TRI_W])
        B3 = sb("B3", [128, TRI_W])
        K = sb("K", [128, NC_])
        V = sb("V", [128, L, NV])
        ST = sb("ST", [128, NST])
        CS = sb("CS", [128, 2, NSM, HD])
        HS = sb("HS", [128, 2, NSM, 128])
        PT = sb("PT", [1, NSM * PAGES], mybir.dt.int32)
        DO = sb("DO", [128, 6, 11])
        FO = sb("FO", [128, 2 * JF, 10])
        RT = sb("RT", [128, NT, 96])
        SMT = sb("SMT", [128, NT, 64])
        NEGA = sb("NEGA", [128, 8])
        SROW = sb("SROW", [128, 512])
        MR = sb("MR", [4, 512])
        ML = sb("ML", [4, 1])
        U4 = sb("U4", [128, NT])
        VU = sb("VU", [128, NT, HD])
        PST = sb("PST", [128, 386])
        M8 = sb("M8", [128, 8])
        MX = sb("MX", [128, 16])
        QI = sb("QI", [64, NSM, 32])
        QA = sb("QA", [128, NSM, 32])
        QB = sb("QB", [128, 2, NSM, 32])
        IWW = sb("IWW", [32, 8])
        DG = sb("DG", [32, 32])
        STM = S[0:8, 2:4, 0:512].rearrange("p a (c d) -> p a c d", d=128)
        SS = sb("SS", [128, 24, 16])
        OS = sb("OS", [128, 32])
        PS = ctx.enter_context(nc.psum_tensor("PS", [128, 8, 512], f32))

        def kc(col, n=128, p0=0, p1=128):
            return K[p0:p1, col:col + n]

        def pair(b):
            return PS[:, b:b + 2, 0:HALF]

        def halves(ap):
            return ap.rearrange("p (a t) -> p a t", a=2)

        ident = kc(C_ID)
        eps = K[:, C_EPS:C_EPS + 1]
        one = K[:, C_ONE:C_ONE + 1]

        loaded = sig("inputs_loaded", 0)
        pt_loaded = sig("page_table_loaded", 0)
        st_loaded = sig("states_loaded", 3 * 16)
        slot_full = [sig(f"slot{i}_full", 0) for i in range(RING)]
        tile_used = sig("tile_used", NPROJ + len(UNITS) + 40 + 8 + 44 + 22)
        sq_ready = sig("squares_ready", 32)
        sq_added = sig("squares_added", 32)
        sum_ready = sig("sum_of_squares_ready", 4)
        root_ready = sig("root_ready", 4)
        norm_out = sig("norm_applied", 32)
        proj_out = sig("projection_copied", NPROJ)
        scaled = sig("queries_keys_scaled", 2)
        perm_done = sig("rotated_halves_ready", 7)
        perm_used = sig("rotated_halves_used", 7)
        rope_done = sig("rope_done", 6)
        cv_init = sig("conv_started", 6)
        cv_done = sig("conv_summed", 6)
        cv_saved = sig("conv_tail_saved", 6)
        xbc_ready = sig("conv_activated", 6)
        tm_done = sig("transposed", 12)
        tm_ready = sig("token_major_ready", 12)
        sm_v = sig("gate_inputs_ready", 1)
        sm_ln = sig("gate_logs_ready", 2)
        sm_cin = sig("log_decays_ready", 1)
        sm_cum = sig("log_decays_summed", 1)
        sm_rt = sig("row_terms_ready", 1)
        sm_tr = sig("row_terms_transposed", 1)
        sm_row = sig("rows_copied", 1)
        sm_g = sig("running_max_ready", 1)
        sm_em = sig("exp_m_ready", 1)
        bc_done = sig("row_broadcast", 8)
        ex_arg = sig("decay_exponent_ready", 8)
        ex_done = sig("decay_exp_done", 8)
        ex_mask = sig("decay_masked", 8)
        st_block = sig("key_query_block_done", 32)
        w_ready = sig("weighted_block_ready", 32)
        vu_ready = sig("state_weights_ready", 8)
        num_done = sig("numerator_done", 8)
        c_em = sig("c_floor_broadcast", 2)
        c_abs = sig("c_denominator_abs", 2)
        c_h = sig("c_h_ready", 2)
        c_sq = sig("c_squares_ready", 2)
        c_sum = sig("c_sum_ready", 2)
        c_root = sig("c_root_ready", 2)
        c_sg = sig("c_output_gate_ready", 2)
        c_out = sig("c_output_ready", 2)
        d_sl = sig("d_silu_ready", 2)
        d_y = sig("d_y_ready", 2)
        d_sq = sig("d_squares_ready", 2)
        d_sum = sig("d_sum_ready", 1)
        d_root = sig("d_root_ready", 1)
        d_out = sig("d_output_ready", 2)
        pst_done = sig("prompt_state_copied", 1)
        z_done = sig("b_logits_ready", 4)
        z_ln = sig("b_log_term_ready", 4)
        sp_done = sig("b_softplus_ready", 4)
        sp_mask = sig("b_softplus_masked", 4)
        ac_done = sig("b_log_weights_ready", 4)
        a_exp = sig("b_weights_exp", 4)
        a_mask = sig("b_weights_masked", 4)
        pv_done = sig("b_values_summed", 4)
        b_out = sig("b_output_copied", 2)
        ix_done = sig("index_products_ready", NT)
        ix_relu = sig("index_relu_ready", NT)
        ix_sum = sig("index_scores_ready", NT)
        ix_mask = sig("index_scores_masked", NT)
        bias_ready = sig("selection_bias_ready", NT)
        at_qk = sig("a_logits_ready", 16)
        at_max = sig("a_max_ready", 16)
        at_exp = sig("a_exp_ready", 16)
        at_norm = sig("a_probs_ready", 16)
        at_tr = sig("a_probs_transposed", 16)
        at_trc = sig("a_probs_copied", 16)
        at_pv = sig("a_values_summed", 16)
        a_out = sig("a_output_copied", 2)
        q_pad = sig("sample_queries_placed", 1)
        sx_done = sig("sample_index_products", 2)
        sx_relu = sig("sample_index_relu", 1)
        sx_iw = sig("sample_index_weights", 1)
        sx_score = sig("sample_scores_ready", 1)
        sx_sel = sig("sample_selection_ready", 1)
        sx_bc = sig("sample_selection_broadcast", 1)
        sx_bias = sig("sample_bias_ready", 1)
        sb_zc = sig("sample_b_logits_copied", 1)
        sb_zt = sig("sample_b_logits_transposed", 1)
        sb_ln = sig("sample_b_log_term", 1)
        sb_sp = sig("sample_b_softplus", 1)
        sb_ac = sig("sample_b_log_weights", 1)
        sb_arg = sig("sample_b_exponent", 1)
        sb_a = sig("sample_b_weights", 1)
        sb_out = sig("sample_b_output", 1)
        sa_max = sig("sample_a_max", 1)
        sa_exp = sig("sample_a_exp", 1)
        sa_p = sig("sample_a_probs", 1)
        sa_tr = sig("sample_a_probs_transposed", 1)
        sa_trc = sig("sample_a_probs_copied", 1)
        sa_out = sig("sample_a_output", 1)
        r_sel = sig("sample_gates_broadcast", 1)
        r_v = sig("sample_gate_inputs", 1)
        r_ln = sig("sample_gate_logs", 1)
        r_arg = sig("sample_exponents", 1)
        r_exp = sig("sample_exps", 1)
        r_dot = sig("sample_dots_ready", 1)
        r_tr = sig("sample_rows_transposed", 1)
        r_trc = sig("sample_rows_copied", 1)
        r_md = sig("sample_diagonals_ready", 8)
        r_bc = sig("sample_rows_broadcast", 8)
        r_bcu = sig("sample_rows_used", 8)
        r_out = sig("sample_states_updated", 1)
        r_prod = sig("sample_products_ready", 1)
        g_sig = sig("gate_sigmoid", 32)
        br_done = sig("branch_done", 24)
        br_used = sig("branch_merged", 32)
        up_evac = sig("up_copied", 2 * JF)
        fcv = sig("ffn_conv_done", 2 * JF)
        gl_done = sig("gelu_done", JF)
        h_ready = sig("hidden_ready", JF)
        dn_done = sig("down_chunk_done", 8)
        stored = sig("outputs_stored", 0)
        N_STORES = {0: 0}
        act_own = sig("act_own", 0)
        dve_own = sig("dve_own", 0)
        pool_own = sig("pool_own", 0)
        tiles_per = tile_used.per
        FIRST = {"proj": 0, "units": NPROJ, "gate": NPROJ + len(UNITS), "out": NPROJ + len(UNITS) + 40,
                 "up": NPROJ + len(UNITS) + 48, "down": NPROJ + len(UNITS) + 92}
        parts_of = {"ki": 8, "kb0": 8, "kb1": 8, "vb0": 4, "vb1": 4, "ka": 8, "va": 8}
        full_at, at = [], [0] * RING
        for l in range(L):
            for n in range(tiles_per):
                u = n - FIRST["units"]
                at[(l * tiles_per + n) % RING] += 16 * (parts_of[UNITS[u][0]] if 0 <= u < len(UNITS) else 1)
                full_at.append(at[(l * tiles_per + n) % RING])

        def slot(l, n):
            return R[:, (l * tiles_per + n) % RING, :]

        def tile_done(l, n):
            return tile_used.nth(l, n)

        def full(l, n):
            m = l * tiles_per + n
            return slot_full[m % RING].sem, full_at[m]

        block = ctx.enter_context(nc.Block())

        @block.sync
        def _(sp):
            sp.dma_start(PT[:, :], pages).then_inc(pt_loaded.sem, 16)
            for dst, src in ((X[:, :, :], x_in), (K[:, :], consts), (V[:, :, :], vecs)):
                sp.dma_start(dst, src).then_inc(loaded.sem, 16)
            sp.wait_ge(pt_loaded.sem, 16)

            def room(l, n):
                m = l * tiles_per + n
                if m >= RING:
                    sp.wait_ge(tile_used.sem, m - RING + 1)

            def tile(l, n, src, width):
                room(l, n)
                sp.dma_start(slot(l, n)[:, 0:width], src).then_inc(full(l, n)[0], 16)

            for l in range(L):
                if l:
                    sp.wait_ge(stored.sem, N_STORES_UPTO[l - 1])
                sp.dma_start(ST[:, :], states[l]).then_inc(st_loaded.sem, 16)
                sp.dma_start(CS[:, :, :, :], c_state[l]).then_inc(st_loaded.sem, 16)
                sp.dma_start(HS[:, :, :, :], d_state[l]).then_inc(st_loaded.sem, 16)
                for c in range(NPROJ):
                    tile(l, c, w_proj[l, c], 1024)
                for u, (what, b) in enumerate(UNITS):
                    n = FIRST["units"] + u
                    room(l, n)
                    dst, sem = slot(l, n), full(l, n)[0]
                    lo, hi = {"vb0": (0, 4), "vb1": (4, 8)}.get(what, (0, 8))
                    for j in range(lo, hi):
                        pg = sp.value_load(PT[0:1, b * PAGES + j:b * PAGES + j + 1], min_val=0, max_val=POOL - 1)
                        if what == "ki":
                            src, d = ki_c[l, bass.ds(pg, 1)], dst[0:64, j * 128:(j + 1) * 128]
                        elif what == "ka":
                            src, d = ka_c[l, bass.ds(pg, 1)], dst[:, j * 128:(j + 1) * 128]
                        elif what == "va":
                            src, d = va_c[l, bass.ds(pg, 1)], dst[:, j * 128:(j + 1) * 128]
                        elif what in ("kb0", "kb1"):
                            src, d = kb_c[int(what[2])][l, bass.ds(pg, 1)], dst[:, j * 128:(j + 1) * 128]
                        else:
                            src, d = vb_c[l, bass.ds(pg, 1)], dst[:, (j - lo) * 256:(j - lo + 1) * 256]
                        sp.dma_start(d, src.rearrange("o p c -> (o p) c")).then_inc(sem, 16)
                for d in range(KD):
                    for br in range(4):
                        tile(l, FIRST["gate"] + 5 * d + br, w_gate[l, 4 * d + br], 1024)
                    tile(l, FIRST["gate"] + 5 * d + 4, w_br[l, d], 1024)
                for d in range(KD):
                    tile(l, FIRST["out"] + d, w_out[l, d], 1024)
                for j in range(2 * JF):
                    tile(l, FIRST["up"] + j, w_up[l, j], 1024)
                for j in range(JF):
                    tile(l, FIRST["down"] + j, w_down[l, j], SLOT)
            sp.wait_ge(norm_out.sem, L * norm_out.per)
            sp.dma_start(y_out, X[:, :, :]).then_inc(stored.sem, 16)
            sp.wait_ge(stored.sem, N_STORES_UPTO[L])

        @block.tensor
        def _(pe):
            pe.wait_ge(loaded.sem, 48)
            mm = nc.tensor.matmul

            def dense(l, n, bank, rhs, blocks, first, last):
                pe.wait_ge(*full(l, n))
                w = slot(l, n)
                for k, r in enumerate(blocks):
                    for a in range(2):
                        i = mm(PS[:, bank + a, 0:HALF], w[:, k * 128:(k + 1) * 128],
                               rhs(r)[:, a * HALF:(a + 1) * HALF],
                               start=first and k == 0, stop=last and k == len(blocks) - 1)
                return i

            def used(l, n):
                pass

            def norm_sum(l, j):
                pe.wait_ge(*sq_added.nth(l, 8 * j + 7))
                for a in range(2):
                    i = mm(PS[:, 4 + a, 0:HALF], kc(C_ONE), S[:, 2, a * HALF:(a + 1) * HALF], start=True, stop=True)
                i.then_inc(sum_ready.sem, 1)

            def finish(i, s):
                i.then_inc(s.sem, 1)

            for l in range(L):
                norm_sum(l, 0)
                for c in range(NPROJ):
                    pe.wait_ge(*norm_out.nth(l, 7))
                    if c >= 2:
                        pe.wait_ge(*proj_out.nth(l, c - 2))
                    dense(l, c, 2 * (c % 2), lambda r: XN[:, r, :], range(KD), True, True).then_inc(tile_used.sem, 1)
                for i, c in enumerate([AQ, AQ + 1, AK, IQ, IQ + 1, SM, SM]):
                    pe.wait_ge(*proj_out.nth(l, c))
                    if i >= 2:
                        pe.wait_ge(*perm_used.nth(l, i - 2))
                    if i < 2:
                        pe.wait_ge(*root_ready.nth(l, 0))
                    for a in range(2):
                        if i < 5:
                            ins = mm(PS[:, 4 + 2 * (i % 2) + a, 0:HALF], kc(C_PERM),
                                     F[:, c, a * HALF:(a + 1) * HALF], start=True, stop=True)
                        else:
                            ins = mm(PS[:, 4 + 2 * (i % 2) + a, 0:HALF], kc((C_DUP1, C_DUP2)[i - 5], 128, 0, 64),
                                     F[0:64, c, a * HALF:(a + 1) * HALF], start=True, stop=True)
                    finish(ins, perm_done)
                pe.wait_ge(*rope_done.nth(l, 5))
                for i, (src, dst) in enumerate(TO_TM):
                    if i >= 4:
                        pe.wait_ge(*tm_ready.nth(l, i - 4))
                    pe.wait_ge(*(xbc_ready.nth(l, src - XX) if src >= XX else proj_out.nth(l, src)))
                    if src == CK:
                        pe.wait_ge(*scaled.nth(l, 1))
                    for t in range(NT):
                        ins = nc.tensor.transpose(PS[:, 4 + i % 4, t * 128:(t + 1) * 128],
                                                  F[:, src, t * 128:(t + 1) * 128], ident)
                    finish(ins, tm_done)
                pe.wait_ge(*sm_cin.nth(l, 0))
                pe.wait_ge(*tm_ready.nth(l, 11))
                CIN = SMT[:, :, 16:24]
                mm(PS[:, 4, 0:32], kc(C_TRI), CIN, start=True, stop=False)
                for k in range(1, NT):
                    ins = mm(PS[:, 4, 8 * k:32], kc(C_ONE), SMT[:, 0:NT - k, 16:24], start=False, stop=k == NT - 1)
                finish(ins, sm_cum)
                pe.wait_ge(*sm_rt.nth(l, 0))
                for t in range(NT):
                    ins = nc.tensor.transpose(PS[0:96, 5, t * 128:(t + 1) * 128], RT[:, t, :], ident)
                finish(ins, sm_tr)
                pe.wait_ge(*xbc_ready.nth(l, 5))
                pe.wait_ge(*q_pad.nth(l, 0))
                for i in range(6):
                    ins = mm(PS[:, 6, 8 * i:8 * i + 8], K[64:80, C_SELS + 128 * i:C_SELS + 128 * i + 128],
                             F[64:80, SM, NPR:TOK], start=True, stop=True)
                finish(ins, r_sel)
                pe.wait_ge(*r_prod.nth(l, 0))
                mm(PS[:, 7, 0:32], kc(C_BLK), SS[:, 0:2, :], start=True, stop=True)
                finish(mm(PS[:, 7, 32:48], kc(C_ONE), SS[:, 2, :], start=True, stop=True), r_dot)
                for i, c in enumerate([CQ, CQ + 1, CK, CK + 1, XC, XC + 1, XB, XB + 1]):
                    ins = nc.tensor.transpose(PS[0:8, i // 4, (i % 4) * 128:(i % 4) * 128 + 128],
                                              F[:, c, NPR:TOK], ident)
                finish(ins, r_tr)
                for s in range(8):
                    pe.wait_ge(*r_md.nth(l, s))
                    if s >= 2:
                        pe.wait_ge(*r_bcu.nth(l, s - 2))
                    elif s == 0:
                        pe.wait_ge(*r_trc.nth(l, 0))
                    md = (B1, B2)[s % 2]
                    bank = 2 * (s % 2)
                    if s < 4:
                        for hh in range(2):
                            ins = mm(PS[64 * hh:64 * hh + 64, bank, :], K[0:8, C_ONE:C_ONE + 64],
                                     md[0:8, 512 * hh:512 * hh + 512], start=True, stop=True)
                    else:
                        for a in range(2):
                            ins = mm(PS[:, bank + a, :], K[0:8, C_ONE:C_ONE + 128],
                                     md[0:8, 512 * a:512 * a + 512], start=True, stop=True)
                    finish(ins, r_bc)
                pe.wait_ge(*sm_em.nth(l, 0))
                pe.wait_ge(*r_bcu.nth(l, 7))
                for v in range(8):
                    h, c, r0 = v % 4, (v % 4) // 2, 64 * (v % 2)
                    if v:
                        pe.wait_ge(*ex_arg.nth(l, v - 1))
                    if v < 4:
                        ins = mm(PS[:, 4, :], K[0:4, C_SEL + 128 * h:C_SEL + 128 * h + 128], SROW[0:4, :],
                                 start=True, stop=True)
                    else:
                        ins = mm(PS[:, 4, :], K[32:36, C_SEL + 128 * h:C_SEL + 128 * h + 128], SROW[32:36, :],
                                 start=True, stop=True)
                    finish(ins, bc_done)
                    if v == 2 or v == 4:
                        pe.wait_ge(*c_h.nth(l, (v - 2) // 2))
                    if v == 6:
                        pass
                    for i in range(NT):
                        n = NPR - 128 * i
                        m = 4 * v + i
                        if m >= 2:
                            pe.wait_ge(*w_ready.nth(l, m - 2))
                        if v < 4:
                            ins = mm(PS[:, 5 + m % 2, 0:n], F[r0:r0 + 64, CK + c, 128 * i:128 * i + 128],
                                     F[r0:r0 + 64, CQ + c, 128 * i:NPR], start=True, stop=True)
                        else:
                            ins = mm(PS[:, 5 + m % 2, 0:n], F[:, XB + c, 128 * i:128 * i + 128],
                                     F[:, XC + c, 128 * i:NPR], start=True, stop=True)
                        finish(ins, st_block)
                    pe.wait_ge(*vu_ready.nth(l, v))
                    for i in range(NT):
                        if v < 4:
                            mm(PS[r0:r0 + 64, 7, 64 * c:64 * c + 64], VU[:, i, :], TM[:, T_CK + c, i, r0:r0 + 64],
                               start=i == 0, stop=i == NT - 1)
                        else:
                            mm(PS[r0:r0 + 64, 7, 130 + 128 * c:258 + 128 * c], VU[:, i, :], TM[:, T_XB + c, i, :],
                               start=i == 0, stop=i == NT - 1)
                    if v < 4:
                        for i in range(NT):
                            mm(PS[r0:r0 + 64, 7, 128 + c:129 + c], TM[:, T_CK + c, i, r0:r0 + 64], U4[:, i:i + 1],
                               start=i == 0, stop=i == NT - 1)
                    nb = 0 if v < 4 else c
                    for i in range(NT):
                        n = NPR - 128 * i
                        pe.wait_ge(*w_ready.nth(l, 4 * v + i))
                        wv = (TM[:, T_CV + c, i, r0:r0 + 64] if v < 4 else TM[:, T_XX + c, i, r0:r0 + 64])
                        ins = mm(PS[r0:r0 + 64, nb, 128 * i:NPR], wv, B1[:, OFF[i]:OFF[i] + n],
                                 start=i == 0, stop=i == NT - 1)
                    if v < 4:
                        for i in range(NT):
                            n = NPR - 128 * i
                            ins = mm(PS[r0:r0 + 64, 2, 128 * i:NPR], K[:, C_ONE:C_ONE + 64],
                                     B1[:, OFF[i]:OFF[i] + n], start=i == 0, stop=i == NT - 1)
                    finish(ins, num_done)
                    if v in (1, 3):
                        finish(mm(PS[:, 3, :], K[0:4, C_SELP + 128 * c:C_SELP + 128 * c + 128], MR[:, :],
                                  start=True, stop=True), c_em)
                        pe.wait_ge(*c_sq.nth(l, c))
                        for a in range(2):
                            ins = mm(PS[:, 2 + a, 0:HALF], kc(C_BLK), S[:, 2, a * HALF:(a + 1) * HALF],
                                     start=True, stop=True)
                        finish(ins, c_sum)
                        pe.wait_ge(*c_root.nth(l, c))
                pe.wait_ge(*d_sq.nth(l, 1))
                for a in range(2):
                    for c in range(2):
                        ins = mm(PS[:, 2 + a, 0:HALF], kc(C_ONE), S[:, 2 + c, a * HALF:(a + 1) * HALF],
                                 start=c == 0, stop=c == 1)
                finish(ins, d_sum)
                pe.wait_ge(*d_root.nth(l, 0))
                pe.wait_ge(*pst_done.nth(l, 0))
                for h in range(4):
                    c, r0 = h // 2, 64 * (h % 2)
                    if h:
                        pe.wait_ge(*a_exp.nth(l, h - 1))
                    else:
                        pe.wait_ge(*scaled.nth(l, 1))

                    def logits(i, start):
                        return mm(PS[:, 4 + i, 0:NPR - 128 * i], F[r0:r0 + 64, BK + c, 128 * i:128 * i + 128],
                                  F[r0:r0 + 64, BQ + c, 128 * i:NPR], start=start, stop=True)
                    for i in range(NT):
                        ins = logits(i, True)
                    finish(ins, z_done)
                    pe.wait_ge(*sp_mask.nth(l, h))
                    for i in range(NT):
                        mm(PS[:, 4 + i, 0:NPR - 128 * i], kc(C_NTRI), B2[:, OFF[i]:OFF[i] + NPR - 128 * i],
                           start=True, stop=False)
                        for j in range(i + 1, NT):
                            mm(PS[:, 4 + i, 128 * (j - i):NPR - 128 * i], kc(C_NONE),
                               B2[:, OFF[j]:OFF[j] + NPR - 128 * j], start=False, stop=False)
                        ins = logits(i, False)
                    finish(ins, ac_done)
                    pe.wait_ge(*a_mask.nth(l, h))
                    if h == 2:
                        pe.wait_ge(*b_out.nth(l, 0))
                    for i in range(NT):
                        ins = mm(PS[r0:r0 + 64, 0, 128 * i:NPR], TM[:, T_BV + c, i, r0:r0 + 64],
                                 B3[:, OFF[i]:OFF[i] + NPR - 128 * i], start=i == 0, stop=i == NT - 1)
                    finish(ins, pv_done)
                pe.wait_ge(*b_out.nth(l, 1))
                for i in range(NT):
                    w = 128 * (i + 1)
                    if i:
                        pe.wait_ge(*at_trc.nth(l, 4 * i - 1))
                    for h in range(4):
                        r0 = 64 * (h % 2)
                        ins = mm(PS[:, 4 + h, 0:w], F[r0:r0 + 64, IQ + h // 2, 128 * i:128 * i + 128],
                                 F[r0:r0 + 64, IKD, 0:w], start=True, stop=True)
                    finish(ins, ix_done)
                    pe.wait_ge(*ix_relu.nth(l, i))
                    for h in range(4):
                        r0 = 64 * (h // 2)
                        finish(mm(PS[:, 4 + h, 0:w], F[r0:r0 + 64, AQ + h % 2, 128 * i:128 * i + 128],
                                  F[r0:r0 + 64, AK, 0:w], start=True, stop=True), at_qk)
                    for h in range(4):
                        r0 = 64 * (h // 2)
                        pe.wait_ge(*at_norm.nth(l, 4 * i + h))
                        for j in range(i + 1):
                            ins = nc.tensor.transpose(PS[:, 4 + h, 128 * j:128 * j + 128],
                                                      S[:, h, 128 * j:128 * j + 128], ident)
                        finish(ins, at_tr)
                        pe.wait_ge(*at_trc.nth(l, 4 * i + h))
                        for j in range(i + 1):
                            ins = mm(PS[r0:r0 + 64, h % 2, 128 * i:128 * i + 128], TM[:, T_AV, j, r0:r0 + 64],
                                     B3[:, 512 * (h % 2) + 128 * j:512 * (h % 2) + 128 * j + 128],
                                     start=j == 0, stop=j == i)
                        finish(ins, at_pv)
                pe.wait_ge(*at_trc.nth(l, 15))
                n0 = FIRST["units"]
                for b in range(NSM):
                    pe.wait_ge(*full(l, n0 + b))
                    for a in range(2):
                        mm(PS[0:32, 4 + a, :], QI[:, b, :], slot(l, n0 + b)[0:64, 512 * a:512 * a + 512],
                           start=b == 0, stop=b == 7)
                    mm(PS[0:32, 6, 0:1], QI[:, b, :], F[0:64, IKD, NPR + b:NPR + b + 1],
                       start=b == 0, stop=b == 7).then_inc(tile_used.sem, 1)
                finish(mm(PS[0:32, 7, 0:8], K[64:68, C_AIW:C_AIW + 32], F[64:68, SM, NPR:TOK],
                          start=True, stop=True), sx_done)
                pe.wait_ge(*sx_relu.nth(l, 0))
                pe.wait_ge(*sx_iw.nth(l, 0))
                mm(PS[0:8, 4, :], IWW[:, :], B1[0:32, 0:512], start=True, stop=True)
                mm(PS[0:8, 5, :], IWW[:, :], B1[0:32, 512:1024], start=True, stop=True)
                finish(mm(PS[0:8, 6, 0:1], IWW[:, :], B1[0:32, 1024:1025], start=True, stop=True), sx_done)
                n0 += NSM
                pe.wait_ge(*a_out.nth(l, 1))
                for b in range(NSM):
                    for c in range(2):
                        n = n0 + 2 * b + c
                        pe.wait_ge(*full(l, n))
                        for a in range(2):
                            ins = mm(PS[0:32, a, :], QB[:, c, b, :], slot(l, n)[:, 512 * a:512 * a + 512],
                                     start=b == 0 and c == 0, stop=b == 7 and c == 1)
                        ins.then_inc(tile_used.sem, 1)
                pe.wait_ge(*sb_zc.nth(l, 0))
                for j in range(PAGES):
                    ins = nc.tensor.transpose(PS[:, 2, 32 * j:32 * j + 32], B1[0:32, 128 * j:128 * j + 128],
                                              K[0:32, C_ID:C_ID + 32])
                finish(ins, sb_zt)
                pe.wait_ge(*sb_sp.nth(l, 0))
                mm(PS[:, 3, 0:256], kc(C_NTRI), S[:, 2, 0:256], start=True, stop=False)
                for k in range(1, PAGES):
                    ins = mm(PS[:, 3, 0:256 - 32 * k], kc(C_NONE), S[:, 2, 32 * k:256], start=False, stop=k == 7)
                finish(ins, sb_ac)
                pe.wait_ge(*sb_a.nth(l, 0))
                n0 += 2 * NSM
                for b in range(NSM):
                    for hf in range(2):
                        n = n0 + 2 * b + hf
                        pe.wait_ge(*full(l, n))
                        for jj in range(4):
                            j = 4 * hf + jj
                            for c in range(2):
                                ins = mm(PS[:, c, 2 * b:2 * b + 2],
                                         slot(l, n)[:, 256 * jj + 128 * c:256 * jj + 128 * c + 128],
                                         S[:, 3, 32 * j + 4 * b + 2 * c:32 * j + 4 * b + 2 * c + 2],
                                         start=j == 0, stop=j == 7)
                        ins.then_inc(tile_used.sem, 1)
                pe.wait_ge(*sx_sel.nth(l, 0))
                for a, (lo, hi) in enumerate(((0, 512), (512, 1024), (1024, 1025))):
                    ins = mm(PS[0:32, 4 + a, 0:hi - lo], K[0:8, C_EB:C_EB + 32], B2[0:8, lo:hi],
                             start=True, stop=True)
                finish(ins, sx_bc)
                pe.wait_ge(*sb_out.nth(l, 0))
                n0 += 2 * NSM
                for b in range(NSM):
                    pe.wait_ge(*full(l, n0 + b))
                    for a in range(2):
                        mm(PS[0:32, a, :], QA[:, b, :], slot(l, n0 + b)[:, 512 * a:512 * a + 512],
                           start=b == 0, stop=b == 7)
                    mm(PS[0:32, 2, 0:1], QA[:, b, :], F[:, AK, NPR + b:NPR + b + 1],
                       start=b == 0, stop=b == 7).then_inc(tile_used.sem, 1)
                pe.wait_ge(*sa_p.nth(l, 0))
                for j in range(PAGES):
                    nc.tensor.transpose(PS[:, 3, 32 * j:32 * j + 32], B1[0:32, 128 * j:128 * j + 128],
                                        K[0:32, C_ID:C_ID + 32])
                finish(mm(PS[:, 7, 0:32], K[0:32, C_ONE:C_ONE + 128], DG[:, :], start=True, stop=True), sa_tr)
                pe.wait_ge(*sa_trc.nth(l, 0))
                n0 += NSM
                for b in range(NSM):
                    pe.wait_ge(*full(l, n0 + b))
                    for j in range(PAGES):
                        ins = mm(PS[:, 6, 4 * b:4 * b + 4], slot(l, n0 + b)[:, 128 * j:128 * j + 128],
                                 S[:, 2, 32 * j + 4 * b:32 * j + 4 * b + 4], start=j == 0, stop=j == 7)
                    ins.then_inc(tile_used.sem, 1)
                pe.wait_ge(*sa_out.nth(l, 0))
                for s in (c_out, d_out, b_out):
                    pe.wait_ge(*s.nth(l, 1))
                for d in range(KD):
                    nb = FIRST["gate"] + 5 * d + 4
                    for br, o in enumerate((AQ, BQ, CQ, DZ)):
                        q = 4 * d + br
                        if q >= 2:
                            pe.wait_ge(*g_sig.nth(l, q - 2))
                        dense(l, nb - 4 + br, 2 * (q % 2), lambda r: XN[:, r, :], range(KD), True, True)\
                            .then_inc(tile_used.sem, 1)
                    pe.wait_ge(*full(l, nb))
                    for br, o in enumerate((AQ, BQ, CQ, DZ)):
                        q = 4 * d + br
                        if q >= 2:
                            pe.wait_ge(*br_used.nth(l, q - 2))
                        for k in range(2):
                            for a in range(2):
                                ins = mm(PS[:, 4 + 2 * (q % 2) + a, 0:HALF],
                                         slot(l, nb)[:, 256 * br + 128 * k:256 * br + 128 * k + 128],
                                         F[:, o + k, a * HALF:(a + 1) * HALF], start=k == 0, stop=k == 1)
                        finish(ins, tile_used if br == 3 else br_done)
                pe.wait_ge(*br_used.nth(l, 31))
                for d in range(KD):
                    if d >= 2:
                        pe.wait_ge(*sq_ready.nth(l, 8 + d - 2))
                    else:
                        pe.wait_ge(*g_sig.nth(l, 30 + d))
                    dense(l, FIRST["out"] + d, 2 * (d % 2), lambda r: F[:, MERGED + r, :], range(KD), True, True)\
                        .then_inc(tile_used.sem, 1)
                norm_sum(l, 1)
                norm_sum(l, 2)
                pe.wait_ge(*norm_out.nth(l, 23))
                for j in range(2 * JF):
                    if j >= 4:
                        pe.wait_ge(*up_evac.nth(l, j - 4))
                    dense(l, FIRST["up"] + j, 2 * (j % 4), lambda r: XN[:, r, :], range(KD), True, True)\
                        .then_inc(tile_used.sem, 1)
                for d in range(KD):
                    if d >= 2:
                        pe.wait_ge(*sq_ready.nth(l, 24 + d - 2))
                    else:
                        pe.wait_ge(*up_evac.nth(l, 2 * JF - 1))
                        pe.wait_ge(*h_ready.nth(l, JF - 1))
                    for k in range(JF):
                        t, e = divmod(JF * d + k, 8)
                        n = FIRST["down"] + t
                        if e == 0 or k == 0:
                            pe.wait_ge(*full(l, n))
                        for a in range(2):
                            ins = mm(PS[:, 2 * (d % 2) + a, 0:HALF], slot(l, n)[:, 128 * e:128 * e + 128],
                                     F[:, k, a * HALF:(a + 1) * HALF], start=k == 0, stop=k == JF - 1)
                        if k == JF - 1:
                            ins.then_inc(dn_done.sem, 1)
                            if e == 7:
                                pe.wait_ge(*dn_done.nth(l, d))
                                pe.sem_inc(tile_used.sem, 1)
                        elif e == 7:
                            ins.then_inc(tile_used.sem, 1)
                norm_sum(l, 3)

        @block.scalar
        def _(act):
            A = nc.scalar.activation

            def do(ins, s=act_own):
                ins.then_inc(s.sem, 1)
                s.n += 1
                act.wait_ge(s.sem, s.n)

            stores = [0]

            def store(dst, src):
                act.dma_start(dst, src).then_inc(stored.sem, 16)

            act.wait_ge(loaded.sem, 48)

            def squares(l, j, src):
                for k in range(KD):
                    m = 8 * j + k
                    if k >= 2:
                        act.wait_ge(*sq_added.nth(l, m - 2))
                    do(A(S[:, k % 2, :], src(k), ACT.Square), sq_ready)

            def root(l, j):
                act.wait_ge(*sum_ready.nth(l, j))
                do(A(halves(S[:, 3, :]), pair(4), ACT.Sqrt, bias=eps, scale=1.0 / DM), root_ready)

            for l in range(L):
                squares(l, 0, lambda k: X[:, k, :]) if l == 0 else None
                if l:
                    for k in range(KD):
                        act.wait_ge(*norm_out.nth(l - 1, 31))
                        if k >= 2:
                            act.wait_ge(*sq_added.nth(l, k - 2))
                        do(A(S[:, k % 2, :], X[:, k, :], ACT.Square), sq_ready)
                root(l, 0)
                for c in range(NPROJ):
                    act.wait_ge(*tile_done(l, c))
                    do(A(halves(F[:, c, :]), pair(2 * (c % 2)), ACT.Copy), proj_out)
                if l:
                    act.wait_ge(stored.sem, N_STORES_UPTO[l - 1])
                for c in range(7):
                    if c < 6:
                        if c >= 2:
                            pass
                        else:
                            act.wait_ge(*rope_done.nth(l, 5))
                        do(A(S[:, c % 2, :], F[:, XX + c, :], ACT.Identity,
                             bias=V[:, l, V_DCB + c:V_DCB + c + 1],
                             scale=V[:, l, V_DCW + 4 * c + 3:V_DCW + 4 * c + 4]), cv_init)
                    if c >= 1:
                        act.wait_ge(*cv_done.nth(l, c - 1))
                        do(A(DO[:, c - 1, :], F[:, XX + c - 1, NPR - 3:TOK], ACT.Copy), cv_saved)
                        do(A(F[:, XX + c - 1, :], S[:, (c - 1) % 2, :], ACT.Silu), xbc_ready)
                for i, (src, dst) in enumerate(TO_TM):
                    act.wait_ge(*tm_done.nth(l, i))
                    src_t = PS[:, 4 + i % 4, :].rearrange("p (t c) -> p t c", c=128)
                    if dst == T_SM:
                        do(A(SMT[:, :, 48:64], src_t[:, :, 64:80], ACT.Copy), tm_ready)
                    else:
                        do(A(TM[:, dst, :, :], src_t, ACT.Copy), tm_ready)
                act.wait_ge(*sm_v.nth(l, 0))
                do(A(SMT[:, :, 8:16], SMT[:, :, 0:8], ACT.Abs))
                do(A(SMT[:, :, 8:16], SMT[:, :, 8:16], ACT.Exp, scale=-1.0))
                do(A(SMT[:, :, 8:16], SMT[:, :, 8:16], ACT.Ln, bias=one), sm_ln)
                do(A(NEGA[:, 4:8], V[:, l, V_AL:V_AL + 4], ACT.Exp), sm_ln)
                act.wait_ge(*sm_tr.nth(l, 0))
                do(A(SROW[0:96, :], PS[0:96, 5, :], ACT.Copy), sm_row)
                act.wait_ge(*sm_g.nth(l, 0))
                do(A(SROW[0:4, :], SROW[0:4, :], ACT.Copy, scale=-1.0))
                do(A(ML[:, :], MR[:, NPR - 1:NPR], ACT.Copy))
                do(A(MR[:, :], MR[:, :], ACT.Exp, scale=-1.0), sm_em)
                store(pm_o[l], ML[:, :])
                act.wait_ge(*rope_done.nth(l, 5))
                store(ka_o[l], F[:, AK, :])
                store(va_o[l], F[:, AV, :])
                store(ki_o[l], F[0:64, IKD, :])
                store(kb_o[l], F[:, BK:BK + 2, :])
                store(vb_o[l], F[:, BV:BV + 2, :])
                store(dconv_o[l], DO[:, :, :])
                act.wait_ge(st_loaded.sem, 48 * (l + 1))
                store(dconv_s_o[l], ST[:, S_DC:S_DC + 144])
                act.wait_ge(*r_v.nth(l, 0))
                do(A(SS[:, 5:7, :], SS[:, 3:5, :], ACT.Abs))
                do(A(SS[:, 5:7, :], SS[:, 5:7, :], ACT.Exp, scale=-1.0))
                do(A(SS[:, 5:7, :], SS[:, 5:7, :], ACT.Ln, bias=one))
                do(A(SS[:, 17, 0:2], V[:, l, V_SAL:V_SAL + 2], ACT.Exp), r_ln)
                act.wait_ge(*r_arg.nth(l, 0))
                do(A(SS[:, 11:15, :], SS[:, 7:11, :], ACT.Exp), r_exp)
                act.wait_ge(*r_tr.nth(l, 0))
                do(A(S[0:8, 2:4, 0:512], PS[0:8, 0:2, :], ACT.Copy), r_trc)
                for c in range(2):
                    do(A(F[:, CO + c, :], F[:, CO + c, :], ACT.Sigmoid), c_sg)
                for c in range(2):
                    do(A(F[:, DZ + c, :], F[:, DZ + c, :], ACT.Silu), d_sl)
                for v in range(8):
                    act.wait_ge(*ex_arg.nth(l, v))
                    do(A(B1[:, :], B1[:, :], ACT.Exp), ex_done)
                    if v in (1, 3):
                        c = v // 2
                        act.wait_ge(*num_done.nth(l, v))
                        do(A(S[:, 0, 0:NPR], PS[:, 2, :], ACT.Abs), c_abs)
                        act.wait_ge(*c_h.nth(l, c))
                        do(A(S[:, 2, :], S[:, 1, :], ACT.Square), c_sq)
                        act.wait_ge(*c_sum.nth(l, c))
                        do(A(halves(S[:, 3, :]), pair(2), ACT.Sqrt, bias=eps, scale=1.0 / HD), c_root)
                for c in range(2):
                    act.wait_ge(*d_y.nth(l, c))
                    do(A(S[:, 2 + c, :], S[:, c, :], ACT.Square), d_sq)
                act.wait_ge(*d_sum.nth(l, 0))
                do(A(halves(S[:, 4, :]), pair(2), ACT.Sqrt, bias=eps, scale=1.0 / 256), d_root)
                do(A(PST[:, :], PS[:, 7, 0:386], ACT.Copy), pst_done)
                store(pc_o[l], PST[:, 0:128])
                store(pn_o[l], PST[:, 128:130])
                store(pssm_o[l], PST[:, 130:386])
                act.wait_ge(*r_out.nth(l, 0))
                store(sc_o[l], CS[:, :, :, :])
                store(sssm_o[l], HS[:, :, :, :])
                store(sn_o[l], SS[:, 22, :])
                store(sm_o[l], SS[:, 21, :])
                for h in range(4):
                    act.wait_ge(*z_done.nth(l, h))
                    for i in range(NT):
                        n = NPR - 128 * i
                        do(A(B1[:, OFF[i]:OFF[i] + n], PS[:, 4 + i, 0:n], ACT.Abs))
                    do(A(B1[:, :], B1[:, :], ACT.Exp, scale=-1.0))
                    do(A(B1[:, :], B1[:, :], ACT.Ln, bias=one), z_ln)
                    act.wait_ge(*ac_done.nth(l, h))
                    for i in range(NT):
                        n = NPR - 128 * i
                        if i == NT - 1:
                            do(A(B3[:, OFF[i]:OFF[i] + n], PS[:, 4 + i, 0:n], ACT.Exp), a_exp)
                        else:
                            do(A(B3[:, OFF[i]:OFF[i] + n], PS[:, 4 + i, 0:n], ACT.Exp))
                    if h % 2:
                        act.wait_ge(*pv_done.nth(l, h))
                        do(A(F[:, BQ + h // 2, 0:NPR], PS[:, 0, :], ACT.Copy), b_out)
                for i in range(NT):
                    w = 128 * (i + 1)
                    act.wait_ge(*ix_done.nth(l, i))
                    for h in range(4):
                        if h < 3:
                            do(A(S[:, h, 0:w], PS[:, 4 + h, 0:w], ACT.Relu))
                        else:
                            do(A(S[:, h, 0:w], PS[:, 4 + h, 0:w], ACT.Relu), ix_relu)
                    for h in range(4):
                        m = 4 * i + h
                        act.wait_ge(*at_max.nth(l, m))
                        do(A(S[:, h, 0:w], S[:, h, 0:w], ACT.Exp, bias=MX[:, h:h + 1], scale=0.125,
                             accum_out=MX[:, 4 + h:5 + h]), at_exp)
                    for h in range(4):
                        m = 4 * i + h
                        act.wait_ge(*at_tr.nth(l, m))
                        if m >= 2:
                            act.wait_ge(*at_pv.nth(l, m - 2))
                        do(A(B3[:, 512 * (h % 2):512 * (h % 2) + w], PS[:, 4 + h, 0:w], ACT.Copy), at_trc)
                act.wait_ge(*at_pv.nth(l, 15))
                for c in range(2):
                    do(A(F[:, AQ + c, 0:NPR], PS[:, c, :], ACT.Copy), a_out)
                act.wait_ge(*sx_done.nth(l, 0))
                do(A(B1[0:32, 0:1024].rearrange("p (a c) -> p a c", a=2), PS[0:32, 4:6, :], ACT.Relu))
                do(A(B1[0:32, 1024:1025], PS[0:32, 6, 0:1], ACT.Relu), sx_relu)
                act.wait_ge(*sx_done.nth(l, 1))
                do(A(B2[0:8, 0:1024].rearrange("p (a c) -> p a c", a=2), PS[0:8, 4:6, :], ACT.Copy))
                do(A(B2[0:8, 1024:1025], PS[0:8, 6, 0:1], ACT.Copy), sx_score)
                act.wait_ge(*tile_done(l, FIRST["units"] + 3 * NSM - 1))
                do(A(B1[0:32, 0:1024].rearrange("p (a c) -> p a c", a=2), PS[0:32, 0:2, :], ACT.Copy), sb_zc)
                act.wait_ge(*sb_zt.nth(l, 0))
                do(A(S[:, 1, 0:256], PS[:, 2, 0:256], ACT.Copy))
                do(A(S[:, 0, 0:256], S[:, 1, 0:256], ACT.Abs))
                do(A(S[:, 0, 0:256], S[:, 0, 0:256], ACT.Exp, scale=-1.0))
                do(A(S[:, 0, 0:256], S[:, 0, 0:256], ACT.Ln, bias=one), sb_ln)
                act.wait_ge(*sb_arg.nth(l, 0))
                do(A(S[:, 3, 0:256], S[:, 1, 0:256], ACT.Exp), sb_a)
                act.wait_ge(*sx_bc.nth(l, 0))
                act.wait_ge(*sa_max.nth(l, 0))
                do(A(B1[0:32, 0:1025], B1[0:32, 0:1025], ACT.Exp, bias=MX[0:32, 8:9], scale=0.125,
                     accum_out=MX[0:32, 9:10]), sa_exp)
                act.wait_ge(*sa_tr.nth(l, 0))
                do(A(S[:, 2, 0:256], PS[:, 3, 0:256], ACT.Copy), sa_trc)
                for q in range(32):
                    act.wait_ge(*tile_done(l, FIRST["gate"] + 5 * (q // 4) + q % 4))
                    if q >= 4:
                        act.wait_ge(*br_used.nth(l, q - 4))
                    do(A(halves(S[:, q % 4, :]), pair(2 * (q % 2)), ACT.Sigmoid), g_sig)

                def evac(l, j, done):
                    for d in range(KD):
                        act.wait_ge(*done(d))
                        do(A(halves(XN[:, d, :]), pair(2 * (d % 2)), ACT.Copy))
                        if d >= 2:
                            act.wait_ge(*sq_added.nth(l, 8 * j + d - 2))
                        else:
                            act.wait_ge(*(br_used.nth(l, 31) if j == 1 else h_ready.nth(l, JF - 1)))
                        do(A(halves(S[:, d % 2, :]), pair(2 * (d % 2)), ACT.Square), sq_ready)
                    root(l, j)

                evac(l, 1, lambda d: tile_done(l, FIRST["out"] + d))
                for k in range(KD):
                    act.wait_ge(*norm_out.nth(l, 8 + k))
                    if k >= 2:
                        act.wait_ge(*sq_added.nth(l, 16 + k - 2))
                    do(A(S[:, k % 2, :], X[:, k, :], ACT.Square), sq_ready)
                root(l, 2)
                for j in range(JF):
                    for g in range(2):
                        m = 2 * j + g
                        ch = g * JF + j
                        act.wait_ge(*tile_done(l, FIRST["up"] + m))
                        if m >= 2:
                            act.wait_ge(*fcv.nth(l, m - 2))
                        else:
                            act.wait_ge(*norm_out.nth(l, 23))
                        do(A(halves(S[:, g, :]), pair(2 * (m % 4)), ACT.Copy))
                        do(A(FO[:, ch, :], S[:, g, NPR - 2:TOK], ACT.Copy))
                        if j:
                            act.wait_ge(*h_ready.nth(l, j - 1))
                        do(A(halves(S[:, 2 + g, :]), pair(2 * (m % 4)), ACT.Identity,
                             bias=V[:, l, V_FCB + ch:V_FCB + ch + 1],
                             scale=V[:, l, V_FCW + 3 * ch + 2:V_FCW + 3 * ch + 3]), up_evac)
                    act.wait_ge(*fcv.nth(l, 2 * j + 1))
                    do(A(S[:, 4, :], S[:, 3, :], ACT.Gelu_apprx_tanh), gl_done)
                store(fconv_o[l], FO[:, :, :])
                store(fconv_s_o[l], ST[:, S_FC:S_FC + 4 * JF * 8])
                evac(l, 3, lambda d: dn_done.nth(l, d))

        @block.vector
        def _(dve):
            v_ = nc.vector

            def do(ins, s=dve_own):
                ins.then_inc(s.sem, 1)
                s.n += 1
                dve.wait_ge(s.sem, s.n)

            def tt(out, a, b, op, s=dve_own):
                do(v_.tensor_tensor(out, a, b, op), s)

            def stt(out, a, sc, b, o0, o1, s=dve_own):
                do(v_.scalar_tensor_tensor(out, a, sc, b, o0, o1), s)

            def ts(out, a, s1, s2, o0, o1, s=dve_own):
                do(v_.tensor_scalar(out, a, s1, s2, o0, o1), s)

            for t in (QI, QA, RT, QB):
                do(v_.memset(t[:], 0.0))
            dve.wait_ge(loaded.sem, 48)

            def add_squares(l, j):
                for k in range(KD):
                    dve.wait_ge(*sq_ready.nth(l, 8 * j + k))
                    if k == 0:
                        do(v_.tensor_copy(S[:, 2, :], S[:, 0, :]), sq_added)
                    else:
                        tt(S[:, 2, :], S[:, 2, :], S[:, k % 2, :], ALU.add, sq_added)
                dve.wait_ge(*root_ready.nth(l, j))
                do(v_.reciprocal(S[:, 3, :], S[:, 3, :]))

            def pre_norm(l, j, col):
                add_squares(l, j)
                for k in range(KD):
                    stt(XN[:, k, :], X[:, k, :], V[:, l, col + k:col + k + 1], S[:, 3, :], ALU.mult, ALU.mult,
                        norm_out)

            def post_norm(l, j, col):
                add_squares(l, j)
                for k in range(KD):
                    stt(S[:, 4, :], XN[:, k, :], V[:, l, col + k:col + k + 1], S[:, 3, :], ALU.mult, ALU.mult)
                    tt(X[:, k, :], X[:, k, :], S[:, 4, :], ALU.add, norm_out)

            for l in range(L):
                def vc(col, n=1, p0=0, p1=128):
                    return V[p0:p1, l, col:col + n]

                pre_norm(l, 0, V_NPRE)
                for i, c in enumerate([AQ, AQ + 1, AK, IQ, IQ + 1]):
                    dve.wait_ge(*proj_out.nth(l, c))
                    tt(S[:, 0, :], F[:, c, :], kc(C_COS, TOK), ALU.mult)
                    dve.wait_ge(*perm_done.nth(l, i))
                    tt(halves(S[:, 1, :]), pair(4 + 2 * (i % 2)), halves(kc(C_SIN, TOK)), ALU.mult, perm_used)
                    tt(F[:, c, :], S[:, 0, :], S[:, 1, :], ALU.add, rope_done)
                dve.wait_ge(*perm_done.nth(l, 5))
                tt(halves(S[:, 0, :]), pair(6), halves(kc(C_COS, TOK)), ALU.mult, perm_used)
                dve.wait_ge(*perm_done.nth(l, 6))
                tt(halves(S[:, 1, :]), pair(4), halves(kc(C_SIN, TOK)), ALU.mult, perm_used)
                tt(F[:, IKD, :], S[:, 0, :], S[:, 1, :], ALU.add, rope_done)
                dve.wait_ge(st_loaded.sem, 48 * (l + 1))
                for c in range(6):
                    dve.wait_ge(*cv_init.nth(l, c))
                    y, x = S[:, c % 2, :], F[:, XX + c, :]
                    for k in range(3):
                        w = vc(V_DCW + 4 * c + k)
                        d = 3 - k
                        stt(y[:, d:NPR], x[:, 0:NPR - d], w, y[:, d:NPR], ALU.mult, ALU.add)
                        o = S_DC + 24 * c + 8 * k
                        stt(y[:, NPR:TOK], ST[:, o:o + 8], w, y[:, NPR:TOK], ALU.mult, ALU.add,
                            cv_done if k == 2 else dve_own)
                dve.wait_ge(*scaled.nth(l, 1))

                def place(t, h):
                    return t.rearrange("p b c -> p (b c)")[:, h:h + 36 * 7 + 1:36]
                for h in range(4):
                    r0 = 64 * (h % 2)
                    do(v_.tensor_copy(place(QI[:, :, :], h), F[r0:r0 + 64, IQ + h // 2, NPR:TOK]))
                    do(v_.tensor_copy(place(QB[r0:r0 + 64, h // 2, :, :], h), F[r0:r0 + 64, BQ + h // 2, NPR:TOK]))
                    r0 = 64 * (h // 2)
                    do(v_.tensor_copy(place(QA[r0:r0 + 64, :, :], h), F[r0:r0 + 64, AQ + h % 2, NPR:TOK]),
                       q_pad if h == 3 else dve_own)
                dve.wait_ge(*tm_ready.nth(l, 0))
                t0 = SMT[:, :, 48:64]

                def bc3(ap, n, axis_len):
                    return ap.unsqueeze(1).to_broadcast([128, n, axis_len])
                tt(SMT[:, :, 0:8], t0[:, :, 8:16], bc3(vc(V_BFD, 8), NT, 8), ALU.add)
                tt(SMT[:, :, 0:8], SMT[:, :, 0:8], bc3(kc(C_SGN, 8), NT, 8), ALU.mult, sm_v)
                tt(SMT[:, :, 32:36], t0[:, :, 4:8], bc3(vc(V_BI, 4), NT, 4), ALU.add)
                ts(SMT[:, :, 36:40], t0[:, :, 0:4], 1.0 / 16, None, ALU.mult, ALU.bypass)
                dve.wait_ge(*sm_ln.nth(l, 1))
                stt(SMT[:, :, 24:32], SMT[:, :, 0:8], 0.0, SMT[:, :, 8:16], ALU.max, ALU.add)
                do(v_.memset(NEGA[:, 0:4], -1.0))
                ts(NEGA[:, 4:8], NEGA[:, 4:8], -1.0, None, ALU.mult, ALU.bypass)
                tt(SMT[:, :, 16:24], SMT[:, :, 24:32], bc3(NEGA[:, :], NT, 8), ALU.mult, sm_cin)
                dve.wait_ge(*sm_cum.nth(l, 0))
                cum = PS[:, 4, 0:32].rearrange("p (t c) -> p t c", t=NT)
                tt(RT[:, :, 0:4], SMT[:, :, 32:36], cum[:, :, 0:4], ALU.subtract)
                do(v_.tensor_copy(RT[:, :, 32:36], cum[:, :, 4:8]))
                do(v_.tensor_copy(RT[:, :, 64:68], cum[:, :, 0:4]), sm_rt)
                ts(SMT[:, :, 40:44], RT[:, :, 32:36], -1.0, None, ALU.mult, ALU.bypass)
                dve.wait_ge(*sm_row.nth(l, 0))
                do(v_.tensor_tensor_scan(SROW[0:4, :], SROW[0:4, :], SROW[0:4, :], 0.0, ALU.max, ALU.max))
                tt(MR[:, :], SROW[0:4, :], PS[64:68, 5, :], ALU.add, sm_g)
                dve.wait_ge(*tm_ready.nth(l, 9))
                for c in range(2):
                    x4 = TM[:, T_XX + c, :, :].rearrange("p t (h d) -> p t h d", h=2)
                    tt(x4, x4, SMT[:, :, 28 + 2 * c:30 + 2 * c].unsqueeze(3).to_broadcast([128, NT, 2, HD]), ALU.mult)
                def fs(c0):
                    return F[:, c0:c0 + 2, NPR:TOK]

                def ss(i):
                    return SS[:, i, :].rearrange("p (c b) -> p c b", c=2)

                def bb(col):
                    return vc(col, 2).unsqueeze(2).to_broadcast([128, 2, NSM])
                dve.wait_ge(*xbc_ready.nth(l, 5))
                tt(ss(0), fs(CQ), fs(CK), ALU.mult)
                tt(ss(1), fs(CQ), ST[:, S_N:S_N + 16].rearrange("p (c b) -> p c b", c=2), ALU.mult)
                tt(ss(2), fs(XB), fs(XC), ALU.mult, r_prod)
                dve.wait_ge(*r_sel.nth(l, 0))
                sel = PS[:, 6, 0:48].rearrange("p (k c b) -> p k c b", k=3, c=2)
                tt(ss(15), sel[:, 0], bb(V_SBI), ALU.add)
                tt(ss(16), sel[:, 1], bb(V_SBF), ALU.add)
                ts(ss(3), ss(16), -1.0, None, ALU.mult, ALU.bypass)
                tt(ss(4), sel[:, 2], bb(V_SBD), ALU.add, r_v)
                dve.wait_ge(*r_ln.nth(l, 0))
                stt(SS[:, 5:7, :], SS[:, 3:5, :], 0.0, SS[:, 5:7, :], ALU.max, ALU.add)
                tt(ss(16), ST[:, S_M:S_M + 16].rearrange("p (c b) -> p c b", c=2), ss(5), ALU.subtract)
                tt(ss(21), ss(16), ss(15), ALU.max)
                tt(ss(7), ss(16), ss(21), ALU.subtract)
                tt(ss(8), ss(15), ss(21), ALU.subtract)
                ts(ss(9), ss(21), -1.0, None, ALU.mult, ALU.bypass)
                stt(ss(10), ss(6), -1.0, SS[:, 17, 0:2].unsqueeze(2).to_broadcast([128, 2, NSM]),
                    ALU.mult, ALU.mult, r_arg)
                dve.wait_ge(*r_exp.nth(l, 0))
                dve.wait_ge(*r_dot.nth(l, 0))
                dots = PS[:, 7, 0:48].rearrange("p (k c b) -> p k c b", k=3, c=2)
                tt(ss(18), dots[:, 0], ss(12), ALU.mult)
                tt(ss(19), dots[:, 1], ss(11), ALU.mult)
                tt(ss(19), ss(19), ss(18), ALU.add)
                tt(ss(22), ss(11), ST[:, S_N:S_N + 16].rearrange("p (c b) -> p c b", c=2), ALU.mult)
                tt(ss(20), ss(12), fs(CK), ALU.mult)
                tt(ss(22), ss(22), ss(20), ALU.add)
                tt(ss(20), ss(12), fs(CV), ALU.mult)
                tt(ss(23), ss(6), fs(XX), ALU.mult)
                tt(ss(0), dots[:, 2], ss(23), ALU.mult)
                for s in range(8):
                    dve.wait_ge(*r_bc.nth(l, s))
                    bank = 2 * (s % 2)
                    c = s % 2
                    wide = HD if s < 4 else 128
                    if s < 4:
                        p = PS[:, bank, :].rearrange("p (b d) -> p b d", b=NSM)
                        stt_, t = CS[:, c], B3[:, 0:512].rearrange("p (b d) -> p b d", b=NSM)
                    else:
                        p = PS[:, bank:bank + 2, :].rearrange("p a (b d) -> p (a b) d", d=128)
                        stt_, t = HS[:, c], B3[:, 0:1024].rearrange("p (b d) -> p b d", b=NSM)

                    def over(i):
                        return SS[:, i, 8 * c:8 * c + 8].unsqueeze(2).to_broadcast([128, NSM, wide])
                    if s in (0, 1, 4, 5):
                        tt(t, stt_, p, ALU.mult, r_bcu)
                        do(v_.tensor_reduce(SS[:, 1 if s < 4 else 2, 8 * c:8 * c + 8], t, AX, ALU.add))
                    else:
                        tt(t, p, over(20 if s < 4 else 23), ALU.mult, r_bcu)
                        tt(stt_, stt_, over(11 if s < 4 else 14), ALU.mult)
                        tt(stt_, stt_, t, ALU.add)
                tt(ss(1), ss(1), ss(11), ALU.mult)
                tt(ss(3), ss(18), fs(CV), ALU.mult)
                tt(ss(1), ss(1), ss(3), ALU.add)
                ts(ss(4), ss(19), -1.0, None, ALU.mult, ALU.bypass)
                tt(ss(19), ss(19), ss(4), ALU.max)
                tt(ss(19), ss(19), ss(13), ALU.max)
                do(v_.reciprocal(ss(19), ss(19)))
                tt(ss(1), ss(1), ss(19), ALU.mult)
                tt(ss(2), ss(2), ss(14), ALU.mult)
                tt(ss(2), ss(2), ss(0), ALU.add, r_out)
                for v in range(8):
                    h, c, r0 = v % 4, (v % 4) // 2, 64 * (v % 2)
                    dve.wait_ge(*bc_done.nth(l, v))
                    if v:
                        dve.wait_ge(*num_done.nth(l, v - 1))
                    for i in range(NT):
                        n = NPR - 128 * i
                        col = RT[:, i, h:h + 1] if v < 4 else SMT[:, i, 40 + h:41 + h]
                        ts(B1[:, OFF[i]:OFF[i] + n], PS[:, 4, 128 * i:NPR], col, 0.0, ALU.add, ALU.min,
                           ex_arg if i == NT - 1 else dve_own)
                    dve.wait_ge(*ex_mask.nth(l, v))
                    src = TM[:, T_CV + c, :, r0:r0 + 64] if v < 4 else TM[:, T_XX + c, :, r0:r0 + 64]
                    for i in range(NT):
                        last = OFF[i] + NPR - 128 * i - 1
                        do(v_.tensor_copy(U4[:, i:i + 1], B1[:, last:last + 1]))
                        ts(VU[:, i, :], src[:, i, :], B1[:, last:last + 1], None, ALU.mult, ALU.bypass,
                           vu_ready if i == NT - 1 else dve_own)
                    for i in range(NT):
                        n = NPR - 128 * i
                        m = 4 * v + i
                        dve.wait_ge(*st_block.nth(l, m))
                        tt(B1[:, OFF[i]:OFF[i] + n], B1[:, OFF[i]:OFF[i] + n], PS[:, 5 + m % 2, 0:n], ALU.mult,
                           w_ready)
                    if v in (1, 3):
                        dve.wait_ge(*c_em.nth(l, c))
                        dve.wait_ge(*c_abs.nth(l, c))
                        tt(S[:, 0, 0:NPR], S[:, 0, 0:NPR], PS[:, 3, :], ALU.max)
                        do(v_.reciprocal(S[:, 0, 0:NPR], S[:, 0, 0:NPR]))
                        do(v_.tensor_copy(S[:, 1, NPR:TOK], SS[:, 1, 8 * c:8 * c + 8]))
                        tt(S[:, 1, 0:NPR], PS[:, 0, :], S[:, 0, 0:NPR], ALU.mult, c_h)
                        dve.wait_ge(*c_root.nth(l, c))
                        do(v_.reciprocal(S[:, 3, :], S[:, 3, :]))
                        tt(S[:, 1, :], S[:, 1, :], S[:, 3, :], ALU.mult)
                        dve.wait_ge(*c_sg.nth(l, c))
                        stt(F[:, CQ + c, :], S[:, 1, :], vc(V_CN + c), F[:, CO + c, :], ALU.mult, ALU.mult, c_out)
                dve.wait_ge(*num_done.nth(l, 7))
                for c in range(2):
                    do(v_.tensor_copy(S[:, 4, NPR:TOK], SS[:, 2, 8 * c:8 * c + 8]))
                    do(v_.tensor_copy(S[:, 4, 0:NPR], PS[:, c, :]))
                    stt(S[:, c, :], F[:, XX + c, :], vc(V_D + c), S[:, 4, :], ALU.mult, ALU.add)
                    dve.wait_ge(*d_sl.nth(l, c))
                    tt(S[:, c, :], S[:, c, :], F[:, DZ + c, :], ALU.mult, d_y)
                dve.wait_ge(*d_root.nth(l, 0))
                do(v_.reciprocal(S[:, 4, :], S[:, 4, :]))
                for c in range(2):
                    stt(F[:, DZ + c, :], S[:, c, :], vc(V_DN + c), S[:, 4, :], ALU.mult, ALU.mult, d_out)
                for h in range(4):
                    dve.wait_ge(*z_ln.nth(l, h))
                    for i in range(NT):
                        n = NPR - 128 * i
                        stt(B2[:, OFF[i]:OFF[i] + n], PS[:, 4 + i, 0:n], 0.0, B1[:, OFF[i]:OFF[i] + n],
                            ALU.max, ALU.add, sp_done if i == NT - 1 else dve_own)
                dve.wait_ge(*b_out.nth(l, 1))
                for i in range(NT):
                    w = 128 * (i + 1)
                    dve.wait_ge(*ix_relu.nth(l, i))
                    ts(B1[:, 0:w], S[:, 0, 0:w], SMT[:, i, 36:37], None, ALU.mult, ALU.bypass)
                    for h in range(1, 4):
                        stt(B1[:, 0:w], S[:, h, 0:w], SMT[:, i, 36 + h:37 + h], B1[:, 0:w], ALU.mult, ALU.add,
                            ix_sum if h == 3 else dve_own)
                    dve.wait_ge(*ix_mask.nth(l, i))
                    if w <= TOPK_P:
                        ts(B2[:, 0:w], B1[:, 0:w], NEG / 2, NEG, ALU.is_le, ALU.mult, bias_ready)
                    else:
                        for _ in range(TOPK_P // 8):
                            do(v_.max(M8[:, :], B1[:, 0:w]))
                            do(v_.match_replace(B1[:, 0:w], M8[:, :], B1[:, 0:w], TAKEN))
                        ts(B2[:, 0:w], B1[:, 0:w], TAKEN / 2, NEG, ALU.is_gt, ALU.mult, bias_ready)
                    for h in range(4):
                        dve.wait_ge(*at_qk.nth(l, 4 * i + h))
                        tt(S[:, h, 0:w], PS[:, 4 + h, 0:w], B2[:, 0:w], ALU.add)
                        do(v_.reduce_max(MX[:, h:h + 1], S[:, h, 0:w], AX))
                        ts(MX[:, h:h + 1], MX[:, h:h + 1], -0.125, None, ALU.mult, ALU.bypass, at_max)
                    for h in range(4):
                        dve.wait_ge(*at_exp.nth(l, 4 * i + h))
                        do(v_.reciprocal(MX[:, 4 + h:5 + h], MX[:, 4 + h:5 + h]))
                        ts(S[:, h, 0:w], S[:, h, 0:w], MX[:, 4 + h:5 + h], None, ALU.mult, ALU.bypass, at_norm)
                dve.wait_ge(*sx_done.nth(l, 0))
                stt(IWW[:, :], PS[0:32, 7, 0:8], 1.0 / 16, K[0:32, C_EM:C_EM + 8], ALU.mult, ALU.mult, sx_iw)
                dve.wait_ge(*sx_score.nth(l, 0))
                for _ in range(TOPK_S // 8):
                    do(v_.max(M8[0:8, :], B2[0:8, 0:PAST + 1]))
                    do(v_.match_replace(B2[0:8, 0:PAST + 1], M8[0:8, :], B2[0:8, 0:PAST + 1], TAKEN))
                ts(B2[0:8, 0:PAST + 1], B2[0:8, 0:PAST + 1], TAKEN / 2, None, ALU.is_le, ALU.bypass, sx_sel)
                dve.wait_ge(*sb_ln.nth(l, 0))
                stt(S[:, 2, 0:256], S[:, 1, 0:256], 0.0, S[:, 0, 0:256], ALU.max, ALU.add, sb_sp)
                dve.wait_ge(*sb_ac.nth(l, 0))
                tt(S[:, 1, 0:256], S[:, 1, 0:256], PS[:, 3, 0:256], ALU.add, sb_arg)
                dve.wait_ge(*tile_done(l, FIRST["units"] + 5 * NSM - 1))
                for h in range(4):
                    r0, c = 64 * (h % 2), h // 2
                    do(v_.tensor_copy(F[r0:r0 + 64, BQ + c, NPR:TOK], PS[r0:r0 + 64, c, h % 2:16:2]),
                       sb_out if h == 3 else dve_own)
                dve.wait_ge(*sx_bc.nth(l, 0))
                ts(B3[0:32, 0:1024].rearrange("p (a c) -> p a c", a=2), PS[0:32, 4:6, :], -NEG, NEG,
                   ALU.mult, ALU.add)
                ts(B3[0:32, 1024:1025], PS[0:32, 6, 0:1], -NEG, NEG, ALU.mult, ALU.add, sx_bias)
                dve.wait_ge(*tile_done(l, FIRST["units"] + 6 * NSM - 1))
                tt(B1[0:32, 0:1024].rearrange("p (a c) -> p a c", a=2), PS[0:32, 0:2, :],
                   B3[0:32, 0:1024].rearrange("p (a c) -> p a c", a=2), ALU.add)
                tt(B1[0:32, 1024:1025], PS[0:32, 2, 0:1], B3[0:32, 1024:1025], ALU.add)
                do(v_.reduce_max(MX[0:32, 8:9], B1[0:32, 0:1025], AX))
                ts(MX[0:32, 8:9], MX[0:32, 8:9], -0.125, None, ALU.mult, ALU.bypass, sa_max)
                dve.wait_ge(*sa_exp.nth(l, 0))
                do(v_.reciprocal(MX[0:32, 9:10], MX[0:32, 9:10]))
                ts(B1[0:32, 0:1025], B1[0:32, 0:1025], MX[0:32, 9:10], None, ALU.mult, ALU.bypass)
                ts(DG[:, :], K[0:32, C_ID:C_ID + 32], B1[0:32, 1024:1025], None, ALU.mult, ALU.bypass, sa_p)
                dve.wait_ge(*sa_tr.nth(l, 0))
                tt(OS[:, :].rearrange("p (b h) -> p b h", h=4), PS[:, 7, 0:32].rearrange("p (b h) -> p b h", h=4),
                   F[:, AV, NPR:TOK].unsqueeze(2).to_broadcast([128, NSM, 4]), ALU.mult)
                dve.wait_ge(*tile_done(l, FIRST["units"] + 7 * NSM - 1))
                tt(OS[:, :], OS[:, :], PS[:, 6, 0:32], ALU.add)
                for h in range(4):
                    r0 = 64 * (h // 2)
                    do(v_.tensor_copy(F[r0:r0 + 64, AQ + h % 2, NPR:TOK], OS[r0:r0 + 64, h:32:4]),
                       sa_out if h == 3 else dve_own)
                dve.wait_ge(stored.sem, N_STORES_MID[l])
                for d in range(KD):
                    for br in range(4):
                        q = 4 * d + br
                        dve.wait_ge(*g_sig.nth(l, q))
                        dve.wait_ge(*(tile_done(l, FIRST["gate"] + 5 * d + 4) if br == 3
                                      else br_done.nth(l, 3 * d + br)))
                        p = pair(4 + 2 * (q % 2))
                        if br == 0:
                            tt(halves(F[:, MERGED + d, :]), halves(S[:, q % 4, :]), p, ALU.mult, br_used)
                        else:
                            tt(halves(S[:, 4, :]), halves(S[:, q % 4, :]), p, ALU.mult)
                            tt(F[:, MERGED + d, :], F[:, MERGED + d, :], S[:, 4, :], ALU.add, br_used)
                post_norm(l, 1, V_NPOST)
                pre_norm(l, 2, V_FPRE)
                for j in range(JF):
                    for g in range(2):
                        m, ch = 2 * j + g, g * JF + j
                        dve.wait_ge(*up_evac.nth(l, m))
                        u, y = S[:, g, :], S[:, 2 + g, :]
                        for k in range(2):
                            w = vc(V_FCW + 3 * ch + k)
                            d = 2 - k
                            stt(y[:, d:NPR], u[:, 0:NPR - d], w, y[:, d:NPR], ALU.mult, ALU.add)
                            o = S_FC + 16 * ch + 8 * k
                            stt(y[:, NPR:TOK], ST[:, o:o + 8], w, y[:, NPR:TOK], ALU.mult, ALU.add,
                                fcv if k == 1 else dve_own)
                    dve.wait_ge(*gl_done.nth(l, j))
                    tt(F[:, j, :], S[:, 2, :], S[:, 4, :], ALU.mult, h_ready)
                post_norm(l, 3, V_FPOST)

        @block.gpsimd
        def _(pool):
            g_ = nc.gpsimd

            def do(ins, s=pool_own):
                ins.then_inc(s.sem, 1)
                s.n += 1
                pool.wait_ge(s.sem, s.n)

            def diagonal(buf, i, base):
                return g_.affine_select(out=buf[:, OFF[i]:OFF[i] + 128], in_=buf[:, OFF[i]:OFF[i] + 128],
                                        pattern=[[1, 128]], compare_op=ALU.is_ge, fill=0.0, base=base,
                                        channel_multiplier=-1)
            pool.wait_ge(loaded.sem, 48)
            for l in range(L):
                pool.wait_ge(*proj_out.nth(l, CK + 1))
                do(g_.tensor_scalar(F[:, BQ:BQ + 2, :], F[:, BQ:BQ + 2, :], 0.125, None, ALU.mult), scaled)
                do(g_.tensor_scalar(F[:, CK:CK + 2, :], F[:, CK:CK + 2, :], 0.125, None, ALU.mult), scaled)
                pool.wait_ge(*r_trc.nth(l, 0))
                for s in range(8):
                    if s >= 2:
                        pool.wait_ge(*r_bc.nth(l, s - 2))
                    md = (B1, B2)[s % 2]
                    id8 = K[0:8, C_ID:C_ID + 8]
                    if s < 4:
                        out = md[0:8, 0:1024].rearrange("p (h b d) -> p h b d", h=2, b=NSM)
                        for hh in range(2):
                            do(g_.tensor_tensor(out[:, hh], STM[:, s // 4, s % 4, 64 * hh:64 * hh + 64].unsqueeze(1)
                                                .to_broadcast([8, NSM, HD]),
                                                id8.unsqueeze(2).to_broadcast([8, NSM, HD]), ALU.mult),
                               r_md if hh else pool_own)
                    else:
                        out = md[0:8, 0:1024].rearrange("p (b d) -> p b d", b=NSM)
                        do(g_.tensor_tensor(out, STM[:, s // 4, s % 4, :].unsqueeze(1).to_broadcast([8, NSM, 128]),
                                            id8.unsqueeze(2).to_broadcast([8, NSM, 128]), ALU.mult), r_md)
                for v in range(8):
                    pool.wait_ge(*ex_done.nth(l, v))
                    for i in range(NT):
                        do(diagonal(B1, i, 0), ex_mask if i == NT - 1 else pool_own)
                for h in range(4):
                    pool.wait_ge(*sp_done.nth(l, h))
                    for i in range(NT):
                        do(diagonal(B2, i, -1), sp_mask if i == NT - 1 else pool_own)
                    pool.wait_ge(*a_exp.nth(l, h))
                    for i in range(NT):
                        do(diagonal(B3, i, -1), a_mask if i == NT - 1 else pool_own)
                for i in range(NT):
                    pool.wait_ge(*ix_sum.nth(l, i))
                    blk = B1[:, 128 * i:128 * i + 128]
                    do(g_.affine_select(out=blk, in_=blk, pattern=[[-1, 128]], compare_op=ALU.is_ge, fill=NEG,
                                        base=0, channel_multiplier=1), ix_mask)


N_MID, N_END, N_ALL = 15, 17, 17
N_STORES_MID = [16 * (N_ALL * l + N_MID) for l in range(L)]
N_STORES_UPTO = [16 * N_ALL * (l + 1) for l in range(L)] + [16 * (N_ALL * L + 1)]


def _f(a, *order):
    return a


def kernel(**inputs):
    import numpy as np
    import concourse.bacc as bacc
    from concourse.bass_utils import run_bass_kernel_spmd

    g = {k: np.asarray(v) for k, v in inputs.items()}
    x = np.concatenate([g["x_prompt"][0], g["x_sample"][:, 0]], 0)
    arr = {}
    arr["x"] = x.T.reshape(KD, 128, TOK).transpose(1, 0, 2)
    arr["pages"] = g["page_table"].reshape(1, -1)
    a = {}
    offs = np.cumsum([0, 256, 128, 128, 256, 64, 4, 256, 256, 256, 256, 256, 256, 4, 4, 256, 256, 768, 4, 4096])
    (o_aq, o_ak, o_av, o_iq, o_ik, o_iw, o_bq, o_bk, o_bv, o_cq, o_ck, o_cv, o_ci, o_cf, o_co, o_dz, o_x, o_dt,
     o_g) = offs[:19]
    w = g["w_in"]
    r = np.arange
    zero = np.zeros((L, DM, 48), w.dtype)
    aq = np.concatenate([o_aq + 64 * h + r(64) for h in (0, 2, 1, 3)])
    cols = [w[:, :, aq], w[:, :, o_ak:o_ak + 128], w[:, :, o_av:o_av + 128], w[:, :, o_iq:o_iq + 256],
            w[:, :, o_ik:o_ik + 64], w[:, :, o_iw:o_iw + 4], w[:, :, o_ci:o_ci + 4], w[:, :, o_cf:o_cf + 4],
            w[:, :, o_dt:o_dt + 4], zero, w[:, :, o_bq:o_bq + 768], w[:, :, o_cq:o_cq + 768],
            w[:, :, o_co:o_co + 256], w[:, :, o_dz:o_dz + 256], w[:, :, o_x:o_x + 768]]
    wp = np.concatenate(cols, 2)

    def tiles(m, kk, nn):
        return m.reshape(L, kk, 128, nn, 128).transpose(0, 3, 2, 1, 4).reshape(L, nn, 128, kk * 128)
    arr["w_proj"] = tiles(wp, KD, NPROJ)
    wg = tiles(w[:, :, o_g:], KD, 32).reshape(L, 4, 8, 128, 1024).transpose(0, 2, 1, 3, 4)
    arr["w_gate"] = wg.reshape(L, 32, 128, 1024)
    ra = np.concatenate([64 * h + r(64) for h in (0, 2, 1, 3)])
    brs = [tiles(m, 2, KD) for m in (g["w_br_a"][:, ra], g["w_br_b"], g["w_br_c"], g["w_br_d"])]
    arr["w_br"] = np.concatenate(brs, 3)
    arr["w_out"] = tiles(g["w_out"], KD, KD)
    up = tiles(g["ffn_up"], KD, 2 * JF).reshape(L, 2, JF, 128, 1024).transpose(0, 2, 1, 3, 4)
    arr["w_up"] = up.reshape(L, 2 * JF, 128, 1024)
    dn = tiles(g["ffn_down"], JF, KD).reshape(L, KD, 128, JF, 128).transpose(0, 1, 3, 2, 4)
    arr["w_down"] = dn.reshape(L, JF, 8, 128, 128).transpose(0, 1, 3, 2, 4).reshape(L, JF, 128, SLOT)

    def fm(v, n):
        return v.reshape(L, n, 128).transpose(0, 2, 1)

    def bcast(v):
        return np.broadcast_to(v[:, None, :], (L, 128, v.shape[1]))

    def heads(v):
        return np.repeat(v.reshape(L, 2, 2), 64, 2).transpose(0, 2, 1)
    packs = [fm(g["norm_mix_pre"], 8), fm(g["norm_mix_post"], 8), fm(g["norm_ffn_pre"], 8),
             fm(g["norm_ffn_post"], 8), fm(g["c_norm"], 2), fm(g["d_norm"], 2),
             g["d_conv_w"].reshape(L, 4, 6, 128).transpose(0, 3, 2, 1).reshape(L, 128, 24), fm(g["d_conv_b"], 6),
             g["ffn_conv_w"].reshape(L, 3, 44, 128).transpose(0, 3, 2, 1).reshape(L, 128, 132),
             fm(g["ffn_conv_b"], 44), heads(g["d_D"]), bcast(g["c_b_i"]), bcast(g["c_b_f"]),
             bcast(g["d_dt_bias"]), bcast(g["d_A_log"]), heads(g["c_b_i"]), heads(g["c_b_f"]),
             heads(g["d_dt_bias"]), heads(g["d_A_log"])]
    vec = np.concatenate(packs, 2)
    assert vec.shape[2] == NV
    arr["vecs"] = vec.transpose(1, 0, 2)
    n_ = g["state_c_n"].reshape(L, 8, 2, 128).transpose(0, 3, 2, 1).reshape(L, 128, 16)
    m_ = np.repeat(g["state_c_m"].reshape(L, 8, 2, 2), 64, 3).transpose(0, 3, 2, 1).reshape(L, 128, 16)
    dc = g["state_d_conv"].reshape(L, 8, 3, 6, 128).transpose(0, 4, 3, 2, 1).reshape(L, 128, 144)
    fc = g["state_ffn_conv"].reshape(L, 8, 2, 44, 128).transpose(0, 4, 3, 2, 1).reshape(L, 128, 704)
    arr["states"] = np.concatenate([n_, m_, dc, fc], 2)
    arr["c_state"] = g["state_c_C"].reshape(L, 8, 2, 128, 64).transpose(0, 3, 2, 1, 4)
    arr["d_state"] = g["state_d_ssm"].reshape(L, 8, 2, 128, 128).transpose(0, 3, 2, 1, 4)
    arr["ki_c"] = g["cache_a_kidx"].transpose(0, 1, 3, 2)
    arr["ka_c"] = g["cache_a_k"].reshape(L, POOL, 128, 128).transpose(0, 1, 3, 2)
    arr["va_c"] = g["cache_a_v"].reshape(L, POOL, 128, 128)
    kb = g["cache_b_k"].reshape(L, POOL, 128, 2, 128).transpose(3, 0, 1, 4, 2)
    arr["kb0_c"], arr["kb1_c"] = kb[0], kb[1]
    arr["vb_c"] = g["cache_b_v"].reshape(L, POOL, 128, 256)

    k_ = np.zeros((128, NC_), np.float32)
    i = r(128)
    k_[:, C_ID:C_ID + 128] = np.eye(128)
    k_[:, C_ONE:C_ONE + 128] = 1
    k_[:, C_TRI:C_TRI + 128] = i[:, None] <= i[None]
    k_[:, C_NTRI:C_NTRI + 128] = -1.0 * (i[:, None] >= i[None])
    k_[:, C_NONE:C_NONE + 128] = -1
    swap = (i // 64) * 64 + (i % 64 + 32) % 64
    k_[swap, C_PERM + i] = 1
    k_[i % 64, C_DUP1 + i] = 1
    k_[(i % 64 + 32) % 64, C_DUP2 + i] = 1
    k_[:, C_BLK:C_BLK + 128] = (i[:, None] // 64) == (i[None] // 64)
    for h in range(4):
        k_[[h, 32 + h], C_SEL + 128 * h:C_SEL + 128 * h + 128] = 1
        k_[h, C_SELP + 128 * (h // 2) + 64 * (h % 2):C_SELP + 128 * (h // 2) + 64 * (h % 2) + 64] = 1
        for what in range(3):
            col = C_SELS + 128 * (2 * what + h // 2) + 64 * (h % 2)
            k_[64 + 4 * (what + 1) + h, col:col + 64] = 1
        k_[64 + h, C_AIW + h:C_AIW + 32:4] = 1
    for b in range(8):
        k_[4 * b:4 * b + 4, C_EM + b] = 1
        k_[b, C_EB + 4 * b:C_EB + 4 * b + 4] = 1
    k_[:, C_SGN:C_SGN + 4] = -1
    k_[:, C_SGN + 4:C_SGN + 8] = 1
    k_[:, C_EPS] = EPS
    inv = np.power(np.float32(10000.0), -r(32).astype(np.float32) / np.float32(32)).astype(np.float32)
    pos = np.concatenate([r(NPR), np.full(NSM, PAST)]).astype(np.float32)
    ang = (inv[i % 32][:, None] * pos[None]).astype(np.float32)
    k_[:, C_COS:C_COS + TOK] = np.cos(ang)
    k_[:, C_SIN:C_SIN + TOK] = np.sin(ang) * np.where(i % 64 < 32, -1.0, 1.0)[:, None]
    arr["consts"] = k_

    nc = bacc.Bacc("TRN2", target_bir_lowering=False, num_devices=1)
    dt_of = mybir.dt.from_np

    def dram(name):
        arr[name] = np.ascontiguousarray(arr[name])
        return nc.dram_tensor(name, arr[name].shape, dt_of(arr[name].dtype), kind="ExternalInput").ap()
    shapes = {"y_o": (128, KD, TOK), "ka_o": (L, 128, TOK), "va_o": (L, 128, TOK), "ki_o": (L, 64, TOK),
              "kb_o": (L, 128, 2, TOK), "vb_o": (L, 128, 2, TOK), "pc_o": (L, 128, 128), "pn_o": (L, 128, 2),
              "pm_o": (L, 4, 1), "dconv_o": (L, 128, 6, 11), "dconv_s_o": (L, 128, 144), "pssm_o": (L, 128, 256),
              "fconv_o": (L, 128, 44, 10), "fconv_s_o": (L, 128, 704), "sc_o": (L, 128, 2, 8, 64),
              "sn_o": (L, 128, 16), "sm_o": (L, 128, 16), "sssm_o": (L, 128, 2, 8, 128)}
    outs = {n: nc.dram_tensor(n, s, mybir.dt.float32, kind="ExternalOutput").ap() for n, s in shapes.items()}
    kb_aps = (dram("kb0_c"), dram("kb1_c"))
    trunk_kernel(nc, *[dram(n) for n in ("x", "pages", "consts", "vecs", "states", "c_state", "d_state",
                                         "ki_c", "ka_c", "va_c")], kb_aps,
                 *[dram(n) for n in ("vb_c", "w_proj", "w_gate", "w_br", "w_out", "w_up", "w_down")],
                 *outs.values())
    res = run_bass_kernel_spmd(nc, [arr], core_ids=[0]).results[0]
    o = {n: np.asarray(res[n]) for n in shapes}

    y = o["y_o"].transpose(2, 1, 0).reshape(TOK, DM)

    def rows(t, c):
        return t.reshape(L, -1, c, TOK).transpose(0, 3, 2, 1).reshape(L, TOK, -1)
    both = {}
    for name, t, c, tail in (("a_k", o["ka_o"], 1, (2, 64)), ("a_v", o["va_o"], 1, (2, 64)),
                             ("kidx", o["ki_o"], 1, (64,)), ("b_k", o["kb_o"], 2, (4, 64)),
                             ("b_v", o["vb_o"], 2, (4, 64))):
        t = rows(t, c)
        both["p_" + name] = t[:, None, :NPR].reshape((L, 1, NPR) + tail)
        both["s_" + name] = t[:, NPR:, None].reshape((L, NSM, 1) + tail)
    p_c = o["pc_o"].reshape(L, 2, 64, 2, 64).transpose(0, 3, 1, 2, 4).reshape(L, 1, 4, 64, 64)
    p_n = o["pn_o"].reshape(L, 2, 64, 2).transpose(0, 3, 1, 2).reshape(L, 1, 4, 64)
    p_m = o["pm_o"].reshape(L, 1, 4)
    dco = o["dconv_o"]
    p_dc = dco[..., :3].transpose(0, 3, 2, 1).reshape(L, 1, 3, 768)
    s_old = o["dconv_s_o"].reshape(L, 128, 6, 3, 8)[:, :, :, 1:]
    s_dc = np.concatenate([s_old, dco[:, :, :, None, 3:]], 3).transpose(0, 4, 3, 2, 1).reshape(L, 8, 3, 768)
    p_h = o["pssm_o"].reshape(L, 2, 64, 2, 128).transpose(0, 3, 1, 2, 4).reshape(L, 1, 4, 64, 128)
    fco = o["fconv_o"]
    p_fc = fco[..., :2].transpose(0, 3, 2, 1).reshape(L, 1, 2, 2 * DFF)
    f_old = o["fconv_s_o"].reshape(L, 128, 44, 2, 8)[:, :, :, 1:]
    s_fc = np.concatenate([f_old, fco[:, :, :, None, 2:]], 3).transpose(0, 4, 3, 2, 1).reshape(L, 8, 2, 2 * DFF)
    s_c = o["sc_o"].reshape(L, 2, 64, 2, 8, 64).transpose(0, 4, 3, 1, 2, 5).reshape(L, 8, 4, 64, 64)
    s_n = o["sn_o"].reshape(L, 2, 64, 2, 8).transpose(0, 4, 3, 1, 2).reshape(L, 8, 4, 64)
    s_m = o["sm_o"].reshape(L, 2, 64, 2, 8)[:, :, 0].transpose(0, 3, 2, 1).reshape(L, 8, 4)
    s_h = o["sssm_o"].reshape(L, 2, 64, 2, 8, 128).transpose(0, 4, 3, 1, 2, 5).reshape(L, 8, 4, 64, 128)
    out = (y[None, :NPR], y[NPR:, None], both["p_a_k"], both["p_a_v"], both["p_kidx"], both["p_b_k"],
           both["p_b_v"], p_c, p_n, p_m, p_dc, p_h, p_fc, both["s_a_k"], both["s_a_v"], both["s_kidx"],
           both["s_b_k"], both["s_b_v"], s_c, s_n, s_m, s_dc, s_h, s_fc)
    return tuple(np.ascontiguousarray(t) for t in out)
```

```python
import concourse.bass as bass
from concourse import mybir
from contextlib import ExitStack

L = 2
NPR = 512
NSM = 8
TOK = NPR + NSM
HALF = TOK // 2
DM = 1024
KD = DM // 128
DFF = 2816
JF = DFF // 128
NT = NPR // 128
PAGES = 8
PAST = 1024
POOL = 80
HD = 64
TOPK_P = 128
TOPK_S = 256
RING = 4
SLOT = 8 * 128
NEG = -1e30
TAKEN = -3e38
EPS = 1e-6

AQ, AK, AV, IQ, SM, BQ, BK, BV, CQ, CK, CV, CO, DZ, XX, XB, XC = (
    0, 2, 3, 4, 6, 7, 9, 11, 13, 15, 17, 19, 21, 23, 25, 27)
NPROJ = 29
IKD = 29
NF = 31
MERGED = 23
T_SM, T_AV, T_BV, T_CK, T_CV, T_XX, T_XB = -1, 0, 1, 3, 5, 7, 9
TO_TM = [(SM, T_SM), (AV, T_AV), (BV, T_BV), (BV + 1, T_BV + 1), (CK, T_CK), (CK + 1, T_CK + 1),
         (CV, T_CV), (CV + 1, T_CV + 1), (XX, T_XX), (XX + 1, T_XX + 1), (XB, T_XB), (XB + 1, T_XB + 1)]
V_NPRE, V_NPOST, V_FPRE, V_FPOST, V_CN, V_DN, V_DCW, V_DCB = 0, 8, 16, 24, 32, 34, 36, 60
V_FCW, V_FCB, V_D, V_BI, V_BFD, V_AL, V_SBI, V_SBF, V_SBD, V_SAL = 66, 198, 242, 244, 248, 256, 260, 262, 264, 266
NV = 268
S_N, S_M, S_DC, S_FC = 0, 16, 32, 176
NST = 880
C_ID, C_ONE, C_TRI, C_NTRI, C_NONE, C_PERM, C_DUP1, C_DUP2, C_BLK = (128 * i for i in range(9))
C_SEL = 1152
C_SELP = C_SEL + 512
C_SELS = C_SEL
C_AIW = C_SELP + 256
C_EM = C_AIW + 32
C_EB = C_EM + 8
C_SGN = C_EB + 32
C_EPS = C_SGN + 8
C_COS = C_EPS + 1
C_SIN = C_COS + TOK
NC_ = C_SIN + TOK
OFF = [0, 512, 896, 1152]
TRI_W = 1280
K_REC, V_REC = 512, 384
UPS = PAGES // 2
NU = NSM * UPS


class Signal:

    def __init__(self, sem, per):
        self.sem, self.per, self.n = sem, per, 0

    def nth(self, l, k):
        return self.sem, l * self.per + k + 1

    def all(self, l):
        return self.sem, (l + 1) * self.per


def trunk_kernel(nc, x_in, pages, consts, vecs, states, c_state, d_state, k_c, v_c,
                 w_proj, w_gate, w_br, w_out, w_up, w_down,
                 y_out, ka_o, va_o, ki_o, kb_o, vb_o, pc_o, pn_o, pm_o, dconv_o, dconv_s_o, pssm_o,
                 fconv_o, fconv_s_o, sc_o, sn_o, sm_o, sssm_o):
    f32 = mybir.dt.float32
    f32r = mybir.dt.float32r
    ALU = mybir.AluOpType
    ACT = mybir.ActivationFunctionType
    AX = mybir.AxisListType.X
    ctx = ExitStack()
    with ctx:
        def sb(name, shape, dt=f32):
            return ctx.enter_context(nc.sbuf_tensor(name, shape, dt))

        signals = []

        def sig(name, per):
            s = Signal(ctx.enter_context(nc.semaphore(name)), per)
            signals.append((name, s))
            return s

        X = sb("X", [128, KD, TOK])
        XH = sb("XH", [128, KD, TOK], f32r)
        RB = sb("RB", [128, TOK])
        F = sb("F", [128, NF, TOK])
        with nc.sbuf_tensor("TM", [128, 11, NT, 128], f32) as TM:
            pass
        WH = sb("WH", [128, 2, SLOT], f32r)
        WL = sb("WL", [128, 2, SLOT], f32r)
        sb("TM_rest", [128, 11 * NT * 128 - 4 * SLOT])
        R = sb("R", [128, RING, SLOT])
        S = sb("S", [128, 5, TOK])
        with nc.sbuf_tensor("B1", [128, TRI_W], f32) as B1, nc.sbuf_tensor("B2", [128, TRI_W], f32) as B2, \
                nc.sbuf_tensor("B3", [128, TRI_W], f32) as B3:
            pass
        XL = sb("XL", [128, KD, TOK], f32r)
        K = sb("K", [128, NC_])
        V = sb("V", [128, L, NV])
        ST = sb("ST", [128, NST])
        CS = sb("CS", [128, 2, NSM, HD])
        HS = sb("HS", [128, 2, NSM, 128])
        PT = sb("PT", [1, NSM * PAGES], mybir.dt.int32)
        DO = sb("DO", [128, 6, 11])
        FO = sb("FO", [128, 2 * JF, 10])
        RT = sb("RT", [128, NT, 96])
        SMT = sb("SMT", [128, NT, 64])
        NEGA = sb("NEGA", [128, 8])
        SROW = sb("SROW", [128, 512])
        MR = sb("MR", [4, 512])
        ML = sb("ML", [4, 1])
        U4 = sb("U4", [128, 2, NT])
        VU = S[:, 4, 0:512].rearrange("p (v t d) -> p v t d", v=2, t=NT)
        PST = sb("PST", [128, 386])
        M8 = sb("M8", [128, 8])
        MX = sb("MX", [128, 16])
        QI = sb("QI", [64, NSM, 32])
        QA = sb("QA", [128, NSM, 32])
        QB = sb("QB", [128, 2, NSM, 32])
        IWW = sb("IWW", [32, 8])
        DG = sb("DG", [32, 32])
        STM = S[0:8, 2:4, 0:512].rearrange("p a (c d) -> p a c d", d=128)
        SS = sb("SS", [128, 24, 16])
        OS = sb("OS", [128, 32])
        PS = ctx.enter_context(nc.psum_tensor("PS", [128, 8, 512], f32))

        def kc(col, n=128, p0=0, p1=128):
            return K[p0:p1, col:col + n]

        def pair(b):
            return PS[:, b:b + 2, 0:HALF]

        def halves(ap):
            return ap.rearrange("p (a t) -> p a t", a=2)

        ident = kc(C_ID)
        eps = K[:, C_EPS:C_EPS + 1]
        one = K[:, C_ONE:C_ONE + 1]

        loaded = sig("inputs_loaded", 0)
        pt_loaded = sig("page_table_loaded", 0)
        st_loaded = sig("states_loaded", 3 * 16)
        slot_full = [sig(f"slot{i}_full", 0) for i in range(RING)]
        tile_used = sig("tile_used", NPROJ + 2 * NU + 40 + 8 + 44 + 22)
        xt_ready = sig("normalised_ready", 16)
        xh_ready = sig("leading_part_ready", 16)
        xl_again = sig("rest_part_ready_again", 8)
        w_hi = sig("weight_leading_part_ready", 105)
        w_lo = sig("weight_rest_part_ready", 105)
        sq_ready = sig("squares_ready", 32)
        sq_added = sig("squares_added", 32)
        sum_ready = sig("sum_of_squares_ready", 4)
        root_ready = sig("root_ready", 4)
        norm_out = sig("norm_applied", 32)
        proj_out = sig("projection_copied", NPROJ)
        scaled = sig("queries_keys_scaled", 2)
        perm_done = sig("rotated_halves_ready", 7)
        perm_used = sig("rotated_halves_used", 7)
        rope_done = sig("rope_done", 6)
        cv_init = sig("conv_started", 6)
        cv_done = sig("conv_summed", 6)
        cv_saved = sig("conv_tail_saved", 6)
        xbc_ready = sig("conv_activated", 6)
        tm_done = sig("transposed", 12)
        tm_ready = sig("token_major_ready", 12)
        sm_v = sig("gate_inputs_ready", 1)
        sm_ln = sig("gate_logs_ready", 2)
        sm_cin = sig("log_decays_ready", 1)
        sm_cum = sig("log_decays_summed", 1)
        sm_rt = sig("row_terms_ready", 1)
        sm_ng = sig("negated_column_terms_ready", 1)
        sm_tr = sig("row_terms_transposed", 1)
        sm_row = sig("rows_copied", 1)
        sm_g = sig("running_max_ready", 1)
        sm_em = sig("exp_m_ready", 1)
        bc_done = sig("row_broadcast", 8)
        ex_arg = sig("decay_exponent_ready", 8)
        ex_done = sig("decay_exp_done", 8)
        st_block = sig("key_query_block_done", 32)
        w_ready = sig("weighted_block_ready", 32)
        vu_ready = sig("state_weights_ready", 8)
        num_done = sig("numerator_done", 8)
        c_em = sig("c_floor_broadcast", 2)
        c_abs = sig("c_denominator_abs", 2)
        c_h = sig("c_h_ready", 2)
        c_sq = sig("c_squares_ready", 2)
        c_sum = sig("c_sum_ready", 2)
        c_root = sig("c_root_ready", 2)
        c_sg = sig("c_output_gate_ready", 2)
        c_out = sig("c_output_ready", 2)
        d_sl = sig("d_silu_ready", 2)
        d_y = sig("d_y_ready", 2)
        d_sq = sig("d_squares_ready", 2)
        d_sum = sig("d_sum_ready", 1)
        d_root = sig("d_root_ready", 1)
        d_out = sig("d_output_ready", 2)
        pst_done = sig("prompt_state_copied", 1)
        z_done = sig("b_logits_ready", 4)
        z_ln = sig("b_log_term_ready", 4)
        sp_done = sig("b_softplus_ready", 4)
        sp_mask = sig("b_softplus_masked", 4)
        ac_done = sig("b_log_weights_ready", 4)
        a_exp = sig("b_weights_exp", 4)
        a_mask = sig("b_weights_masked", 4)
        pv_done = sig("b_values_summed", 4)
        b_out = sig("b_output_copied", 2)
        ix_done = sig("index_products_ready", NT)
        ix_relu = sig("index_relu_ready", NT)
        ix_sum = sig("index_scores_ready", NT)
        ix_mask = sig("index_scores_masked", NT)
        bias_ready = sig("selection_bias_ready", NT)
        at_qk = sig("a_logits_ready", 16)
        at_max = sig("a_max_ready", 16)
        at_exp = sig("a_exp_ready", 16)
        at_norm = sig("a_probs_ready", 16)
        at_tr = sig("a_probs_transposed", 16)
        at_trc = sig("a_probs_copied", 16)
        at_pv = sig("a_values_summed", 16)
        a_out = sig("a_output_copied", 2)
        q_pad = sig("sample_queries_placed", 1)
        sx_done = sig("sample_index_products", 2)
        sx_relu = sig("sample_index_relu", 1)
        sx_iw = sig("sample_index_weights", 1)
        sx_score = sig("sample_scores_ready", 1)
        sx_sel = sig("sample_selection_ready", 1)
        sx_bc = sig("sample_selection_broadcast", 1)
        sb_zc = sig("sample_b_logits_copied", 1)
        sb_zt = sig("sample_b_logits_transposed", 1)
        sb_ln = sig("sample_b_log_term", 1)
        sb_sp = sig("sample_b_softplus", 1)
        sb_ac = sig("sample_b_log_weights", 1)
        sb_arg = sig("sample_b_exponent", 1)
        sb_a = sig("sample_b_weights", 1)
        sa_max = sig("sample_a_max", 1)
        sa_exp = sig("sample_a_exp", 1)
        sa_p = sig("sample_a_probs", 1)
        sa_tr = sig("sample_a_probs_transposed", 1)
        sa_trc = sig("sample_a_probs_copied", 1)
        sa_out = sig("sample_a_output", 1)
        r_sel = sig("sample_gates_broadcast", 1)
        r_v = sig("sample_gate_inputs", 1)
        r_ln = sig("sample_gate_logs", 1)
        r_arg = sig("sample_exponents", 1)
        r_exp = sig("sample_exps", 1)
        r_dot = sig("sample_dots_ready", 1)
        r_tr = sig("sample_rows_transposed", 1)
        r_trc = sig("sample_rows_copied", 1)
        r_md = sig("sample_diagonals_ready", 8)
        r_bc = sig("sample_rows_broadcast", 8)
        r_bcu = sig("sample_rows_used", 8)
        r_out = sig("sample_states_updated", 1)
        r_prod = sig("sample_products_ready", 1)
        g_sig = sig("gate_sigmoid", 32)
        br_done = sig("branch_done", 24)
        br_used = sig("branch_merged", 32)
        up_evac = sig("up_copied", 2 * JF)
        fcv = sig("ffn_conv_done", 2 * JF)
        gl_done = sig("gelu_done", JF)
        h_ready = sig("hidden_ready", JF)
        dn_done = sig("down_chunk_done", 8)
        stored = sig("outputs_stored", 0)
        N_STORES = {0: 0}
        act_own = sig("act_own", 0)
        dve_own = sig("dve_own", 0)
        pool_own = sig("pool_own", 0)
        tiles_per = tile_used.per
        FIRST = {"proj": 0, "K": NPROJ, "V": NPROJ + NU, "gate": NPROJ + 2 * NU, "out": NPROJ + 2 * NU + 40,
                 "up": NPROJ + 2 * NU + 48, "down": NPROJ + 2 * NU + 92}
        full_at, at = [], [0] * RING
        for l in range(L):
            for n in range(tiles_per):
                cache = FIRST["K"] <= n < FIRST["gate"]
                at[(l * tiles_per + n) % RING] += 32 if cache else 16
                full_at.append(at[(l * tiles_per + n) % RING])

        def slot(l, n):
            return R[:, (l * tiles_per + n) % RING, :]

        def tile_done(l, n):
            return tile_used.nth(l, n)

        def split_no(n):
            return (n if n < FIRST["K"] else n - FIRST["up"] + 61 if n >= FIRST["up"]
                    else NPROJ + (n - FIRST["gate"]) // 5 * 4 + (n - FIRST["gate"]) % 5)

        SPLIT = (list(range(NPROJ)) + [FIRST["gate"] + 5 * (q // 4) + q % 4 for q in range(32)]
                 + [FIRST["up"] + j for j in range(2 * JF)])

        def full(l, n):
            m = l * tiles_per + n
            return slot_full[m % RING].sem, full_at[m]

        block = ctx.enter_context(nc.Block())

        @block.sync
        def _(sp):
            sp.dma_start(PT[:, :], pages).then_inc(pt_loaded.sem, 16)
            for dst, src in ((X[:, :, :], x_in), (K[:, :], consts), (V[:, :, :], vecs)):
                sp.dma_start(dst, src).then_inc(loaded.sem, 16)
            sp.wait_ge(pt_loaded.sem, 16)

            def room(l, n):
                m = l * tiles_per + n
                if m >= RING:
                    sp.wait_ge(tile_used.sem, m - RING + 1)

            def tile(l, n, src, width):
                room(l, n)
                sp.dma_start(slot(l, n)[:, 0:width], src).then_inc(full(l, n)[0], 16)

            for l in range(L):
                if l:
                    sp.wait_ge(stored.sem, N_STORES_UPTO[l - 1])
                sp.dma_start(ST[:, :], states[l]).then_inc(st_loaded.sem, 16)
                sp.dma_start(CS[:, :, :, :], c_state[l]).then_inc(st_loaded.sem, 16)
                sp.dma_start(HS[:, :, :, :], d_state[l]).then_inc(st_loaded.sem, 16)
                for c in range(NPROJ):
                    tile(l, c, w_proj[l, c], 1024)
                for what, rec, src in (("K", K_REC, k_c), ("V", V_REC, v_c)):
                    for u in range(NU):
                        n = FIRST[what] + u
                        room(l, n)
                        for j in range(2):
                            pg = sp.value_load(PT[0:1, 2 * u + j:2 * u + j + 1], min_val=0, max_val=POOL - 1)
                            sp.dma_start(slot(l, n)[:, rec * j:rec * (j + 1)],
                                         src[l, bass.ds(pg, 1)].rearrange("o p c -> (o p) c"))\
                              .then_inc(full(l, n)[0], 16)
                for d in range(KD):
                    for br in range(4):
                        tile(l, FIRST["gate"] + 5 * d + br, w_gate[l, 4 * d + br], 1024)
                    tile(l, FIRST["gate"] + 5 * d + 4, w_br[l, d], 1024)
                for d in range(KD):
                    tile(l, FIRST["out"] + d, w_out[l, d], 1024)
                for j in range(2 * JF):
                    tile(l, FIRST["up"] + j, w_up[l, j], 1024)
                for j in range(JF):
                    tile(l, FIRST["down"] + j, w_down[l, j], SLOT)
            sp.wait_ge(norm_out.sem, L * norm_out.per)
            sp.dma_start(y_out, X[:, :, :]).then_inc(stored.sem, 16)
            sp.wait_ge(stored.sem, N_STORES_UPTO[L])

        @block.tensor
        def _(pe):
            pe.wait_ge(loaded.sem, 48)
            mm = nc.tensor.matmul

            def dense(l, n, bank, rhs, blocks, first, last):
                pe.wait_ge(*full(l, n))
                w = slot(l, n)
                for k, r in enumerate(blocks):
                    for a in range(2):
                        i = mm(PS[:, bank + a, 0:HALF], w[:, k * 128:(k + 1) * 128],
                               rhs(r)[:, a * HALF:(a + 1) * HALF],
                               start=first and k == 0, stop=last and k == len(blocks) - 1)
                return i

            def dense_split(l, n, bank):
                m = split_no(n)
                pe.wait_ge(*w_hi.nth(l, m))
                pe.wait_ge(*w_lo.nth(l, m))
                for k in range(KD):
                    for w, x in ((WH, XH), (WH, XL), (WL, XH)):
                        for a in range(2):
                            i = mm(PS[:, bank + a, 0:HALF], w[:, m % 2, k * 128:(k + 1) * 128],
                                   x[:, k, a * HALF:(a + 1) * HALF], start=k == 0 and w is WH and x is XH,
                                   stop=k == KD - 1 and w is WL)
                i.then_inc(tile_used.sem, 1)

            def norm_sum(l, j):
                pe.wait_ge(*sq_added.nth(l, 8 * j + 7))
                for a in range(2):
                    i = mm(PS[:, 4 + a, 0:HALF], kc(C_ONE), S[:, 2, a * HALF:(a + 1) * HALF], start=True, stop=True)
                i.then_inc(sum_ready.sem, 1)

            def finish(i, s):
                i.then_inc(s.sem, 1)

            for l in range(L):
                norm_sum(l, 0)
                for c in range(NPROJ):
                    pe.wait_ge(*norm_out.nth(l, 7))
                    if c >= 2:
                        pe.wait_ge(*proj_out.nth(l, c - 2))
                    dense_split(l, c, 2 * (c % 2))
                for i, c in enumerate([AQ, AQ + 1, AK, IQ, IQ + 1, SM, SM]):
                    pe.wait_ge(*proj_out.nth(l, c))
                    if i >= 2:
                        pe.wait_ge(*perm_used.nth(l, i - 2))
                    if i < 2:
                        pe.wait_ge(*root_ready.nth(l, 0))
                    for a in range(2):
                        if i < 5:
                            ins = mm(PS[:, 4 + 2 * (i % 2) + a, 0:HALF], kc(C_PERM),
                                     F[:, c, a * HALF:(a + 1) * HALF], start=True, stop=True)
                        else:
                            ins = mm(PS[:, 4 + 2 * (i % 2) + a, 0:HALF], kc((C_DUP1, C_DUP2)[i - 5], 128, 0, 64),
                                     F[0:64, c, a * HALF:(a + 1) * HALF], start=True, stop=True)
                    finish(ins, perm_done)
                pe.wait_ge(*rope_done.nth(l, 5))
                for i, (src, dst) in enumerate(TO_TM):
                    if i >= 4:
                        pe.wait_ge(*tm_ready.nth(l, i - 4))
                    pe.wait_ge(*(xbc_ready.nth(l, src - XX) if src >= XX else proj_out.nth(l, src)))
                    if src == CK:
                        pe.wait_ge(*scaled.nth(l, 1))
                    for t in range(NT):
                        ins = nc.tensor.transpose(PS[:, 4 + i % 4, t * 128:(t + 1) * 128],
                                                  F[:, src, t * 128:(t + 1) * 128], ident)
                    finish(ins, tm_done)
                pe.wait_ge(*sm_cin.nth(l, 0))
                pe.wait_ge(*tm_ready.nth(l, 11))
                CIN = SMT[:, :, 16:24]
                mm(PS[:, 4, 0:32], kc(C_TRI), CIN, start=True, stop=False)
                for k in range(1, NT):
                    ins = mm(PS[:, 4, 8 * k:32], kc(C_ONE), SMT[:, 0:NT - k, 16:24], start=False, stop=k == NT - 1)
                finish(ins, sm_cum)
                pe.wait_ge(*sm_rt.nth(l, 0))
                for t in range(NT):
                    ins = nc.tensor.transpose(PS[0:96, 5, t * 128:(t + 1) * 128], RT[:, t, :], ident)
                finish(ins, sm_tr)
                pe.wait_ge(*xbc_ready.nth(l, 5))
                pe.wait_ge(*q_pad.nth(l, 0))
                for i in range(6):
                    ins = mm(PS[:, 6, 8 * i:8 * i + 8], K[64:80, C_SELS + 128 * i:C_SELS + 128 * i + 128],
                             F[64:80, SM, NPR:TOK], start=True, stop=True)
                finish(ins, r_sel)
                pe.wait_ge(*r_prod.nth(l, 0))
                mm(PS[:, 7, 0:32], kc(C_BLK), SS[:, 0:2, :], start=True, stop=True)
                finish(mm(PS[:, 7, 32:48], kc(C_ONE), SS[:, 2, :], start=True, stop=True), r_dot)
                for i, c in enumerate([CQ, CQ + 1, CK, CK + 1, XC, XC + 1, XB, XB + 1]):
                    ins = nc.tensor.transpose(PS[0:8, i // 4, (i % 4) * 128:(i % 4) * 128 + 128],
                                              F[:, c, NPR:TOK], ident)
                finish(ins, r_tr)
                for s in range(8):
                    pe.wait_ge(*r_md.nth(l, s))
                    if s >= 2:
                        pe.wait_ge(*r_bcu.nth(l, s - 2))
                    elif s == 0:
                        pe.wait_ge(*r_trc.nth(l, 0))
                    md = (B1, B2)[s % 2]
                    bank = 2 * (s % 2)
                    if s < 4:
                        for hh in range(2):
                            ins = mm(PS[64 * hh:64 * hh + 64, bank, :], K[0:8, C_ONE:C_ONE + 64],
                                     md[0:8, 512 * hh:512 * hh + 512], start=True, stop=True)
                    else:
                        for a in range(2):
                            ins = mm(PS[:, bank + a, :], K[0:8, C_ONE:C_ONE + 128],
                                     md[0:8, 512 * a:512 * a + 512], start=True, stop=True)
                    finish(ins, r_bc)
                pe.wait_ge(*sm_em.nth(l, 0))
                pe.wait_ge(*r_bcu.nth(l, 7))
                def broadcast(v):
                    if v:
                        pe.wait_ge(*ex_arg.nth(l, v - 1))
                    p0 = 0 if v < 4 else 32
                    col = C_SEL + 128 * (v % 4)
                    finish(mm(PS[:, 4, :], K[p0:p0 + 4, col:col + 128], SROW[p0:p0 + 4, :],
                              start=True, stop=True), bc_done)
                broadcast(0)
                for v in range(8):
                    h, c, r0 = v % 4, (v % 4) // 2, 64 * (v % 2)
                    E = (B1, B2)[v % 2]
                    if v == 2 or v == 4:
                        pe.wait_ge(*c_h.nth(l, (v - 2) // 2))
                    for i in range(NT):
                        if i == 2 and v < 7:
                            broadcast(v + 1)
                        n = NPR - 128 * i
                        m = 4 * v + i
                        if m >= 2:
                            pe.wait_ge(*w_ready.nth(l, m - 2))
                        if v < 4:
                            ins = mm(PS[:, 5 + m % 2, 0:n], F[r0:r0 + 64, CK + c, 128 * i:128 * i + 128],
                                     F[r0:r0 + 64, CQ + c, 128 * i:NPR], start=True, stop=True)
                        else:
                            ins = mm(PS[:, 5 + m % 2, 0:n], F[:, XB + c, 128 * i:128 * i + 128],
                                     F[:, XC + c, 128 * i:NPR], start=True, stop=True)
                        finish(ins, st_block)
                    pe.wait_ge(*vu_ready.nth(l, v))
                    for i in range(NT):
                        if v < 4:
                            mm(PS[r0:r0 + 64, 7, 64 * c:64 * c + 64], VU[:, v % 2, i, :], TM[:, T_CK + c, i, r0:r0 + 64],
                               start=i == 0, stop=i == NT - 1)
                        else:
                            mm(PS[r0:r0 + 64, 7, 130 + 128 * c:258 + 128 * c], VU[:, v % 2, i, :], TM[:, T_XB + c, i, :],
                               start=i == 0, stop=i == NT - 1)
                    if v < 4:
                        for i in range(NT):
                            mm(PS[r0:r0 + 64, 7, 128 + c:129 + c], TM[:, T_CK + c, i, r0:r0 + 64], U4[:, v % 2, i:i + 1],
                               start=i == 0, stop=i == NT - 1)
                    nb = 0 if v < 4 else c
                    for i in range(NT):
                        n = NPR - 128 * i
                        pe.wait_ge(*w_ready.nth(l, 4 * v + i))
                        wv = (TM[:, T_CV + c, i, r0:r0 + 64] if v < 4 else TM[:, T_XX + c, i, r0:r0 + 64])
                        ins = mm(PS[r0:r0 + 64, nb, 128 * i:NPR], wv, E[:, OFF[i]:OFF[i] + n],
                                 start=i == 0, stop=i == NT - 1)
                    if v < 4:
                        for i in range(NT):
                            n = NPR - 128 * i
                            ins = mm(PS[r0:r0 + 64, 2, 128 * i:NPR], K[:, C_ONE:C_ONE + 64],
                                     E[:, OFF[i]:OFF[i] + n], start=i == 0, stop=i == NT - 1)
                    finish(ins, num_done)
                    if v in (1, 3):
                        finish(mm(PS[:, 3, :], K[0:4, C_SELP + 128 * c:C_SELP + 128 * c + 128], MR[:, :],
                                  start=True, stop=True), c_em)
                        pe.wait_ge(*c_sq.nth(l, c))
                        for a in range(2):
                            ins = mm(PS[:, 2 + a, 0:HALF], kc(C_BLK), S[:, 2, a * HALF:(a + 1) * HALF],
                                     start=True, stop=True)
                        finish(ins, c_sum)
                        pe.wait_ge(*c_root.nth(l, c))
                pe.wait_ge(*d_sq.nth(l, 1))
                for a in range(2):
                    for c in range(2):
                        ins = mm(PS[:, 2 + a, 0:HALF], kc(C_ONE), S[:, 2 + c, a * HALF:(a + 1) * HALF],
                                 start=c == 0, stop=c == 1)
                finish(ins, d_sum)
                pe.wait_ge(*d_root.nth(l, 0))
                pe.wait_ge(*pst_done.nth(l, 0))
                for h in range(4):
                    c, r0 = h // 2, 64 * (h % 2)
                    if h:
                        pe.wait_ge(*a_exp.nth(l, h - 1))
                    else:
                        pe.wait_ge(*scaled.nth(l, 1))

                    def logits(i, start):
                        return mm(PS[:, 4 + i, 0:NPR - 128 * i], F[r0:r0 + 64, BK + c, 128 * i:128 * i + 128],
                                  F[r0:r0 + 64, BQ + c, 128 * i:NPR], start=start, stop=True)
                    for i in range(NT):
                        ins = logits(i, True)
                    finish(ins, z_done)
                    pe.wait_ge(*sp_mask.nth(l, h))
                    for i in range(NT):
                        mm(PS[:, 4 + i, 0:NPR - 128 * i], kc(C_NTRI), B2[:, OFF[i]:OFF[i] + NPR - 128 * i],
                           start=True, stop=False)
                        for j in range(i + 1, NT):
                            mm(PS[:, 4 + i, 128 * (j - i):NPR - 128 * i], kc(C_NONE),
                               B2[:, OFF[j]:OFF[j] + NPR - 128 * j], start=False, stop=False)
                        ins = logits(i, False)
                    finish(ins, ac_done)
                    pe.wait_ge(*a_mask.nth(l, h))
                    if h == 2:
                        pe.wait_ge(*b_out.nth(l, 0))
                    for i in range(NT):
                        ins = mm(PS[r0:r0 + 64, 0, 128 * i:NPR], TM[:, T_BV + c, i, r0:r0 + 64],
                                 B3[:, OFF[i]:OFF[i] + NPR - 128 * i], start=i == 0, stop=i == NT - 1)
                    finish(ins, pv_done)
                pe.wait_ge(*b_out.nth(l, 1))
                for i in range(NT):
                    w = 128 * (i + 1)
                    if i:
                        pe.wait_ge(*at_trc.nth(l, 4 * i - 1))
                    for h in range(4):
                        r0 = 64 * (h % 2)
                        ins = mm(PS[:, 4 + h, 0:w], F[r0:r0 + 64, IQ + h // 2, 128 * i:128 * i + 128],
                                 F[r0:r0 + 64, IKD, 0:w], start=True, stop=True)
                    finish(ins, ix_done)
                    pe.wait_ge(*ix_relu.nth(l, i))
                    for h in range(4):
                        r0 = 64 * (h // 2)
                        finish(mm(PS[:, 4 + h, 0:w], F[r0:r0 + 64, AQ + h % 2, 128 * i:128 * i + 128],
                                  F[r0:r0 + 64, AK, 0:w], start=True, stop=True), at_qk)
                    for h in range(4):
                        r0 = 64 * (h // 2)
                        pe.wait_ge(*at_norm.nth(l, 4 * i + h))
                        for j in range(i + 1):
                            ins = nc.tensor.transpose(PS[:, 4 + h, 128 * j:128 * j + 128],
                                                      S[:, h, 128 * j:128 * j + 128], ident)
                        finish(ins, at_tr)
                        pe.wait_ge(*at_trc.nth(l, 4 * i + h))
                        for j in range(i + 1):
                            ins = mm(PS[r0:r0 + 64, h % 2, 128 * i:128 * i + 128], TM[:, T_AV, j, r0:r0 + 64],
                                     B3[:, 512 * (h % 2) + 128 * j:512 * (h % 2) + 128 * j + 128],
                                     start=j == 0, stop=j == i)
                        finish(ins, at_pv)
                pe.wait_ge(*at_trc.nth(l, 15))
                pe.wait_ge(*a_out.nth(l, 1))
                for u in range(NU):
                    b, t = divmod(u, UPS)
                    n = FIRST["K"] + u
                    pe.wait_ge(*full(l, n))
                    rec = slot(l, n).rearrange("p (j k c) -> p k j c", j=2, k=4)
                    bank, col = t // 2, 256 * (t % 2)
                    st = b == 0 and t % 2 == 0
                    end = b == NSM - 1
                    mm(PS[0:32, 4 + bank, col:col + 256], QI[:, b, :], rec[0:64, 3], start=st, stop=end,
                       skip_group_check=True)
                    mm(PS[0:32, bank, col:col + 256], QA[:, b, :], rec[:, 0], start=st, stop=end,
                       skip_group_check=True)
                    if t == 0:
                        mm(PS[0:32, 6, 0:1], QI[:, b, :], F[0:64, IKD, NPR + b:NPR + b + 1], start=b == 0,
                           stop=end, skip_group_check=True)
                        mm(PS[0:32, 6, 1:2], QA[:, b, :], F[:, AK, NPR + b:NPR + b + 1], start=False,
                           stop=end, skip_group_check=True)
                    for c in range(2):
                        ins = mm(PS[0:32, 2 + bank, col:col + 256], QB[:, c, b, :], rec[:, 1 + c],
                                 start=st and c == 0, stop=end and c == 1, skip_group_check=True)
                    ins.then_inc(tile_used.sem, 1)
                finish(mm(PS[0:32, 7, 0:8], K[64:68, C_AIW:C_AIW + 32], F[64:68, SM, NPR:TOK],
                          start=True, stop=True), sx_done)
                pe.wait_ge(*sx_relu.nth(l, 0))
                pe.wait_ge(*sx_iw.nth(l, 0))
                mm(PS[0:8, 4, :], IWW[:, :], B3[0:32, 0:512], start=True, stop=True)
                mm(PS[0:8, 5, :], IWW[:, :], B3[0:32, 512:1024], start=True, stop=True)
                finish(mm(PS[0:8, 7, 0:1], IWW[:, :], B3[0:32, 1024:1025], start=True, stop=True), sx_done)
                pe.wait_ge(*sb_zc.nth(l, 0))
                for j in range(PAGES):
                    ins = nc.tensor.transpose(PS[:, 2, 32 * j:32 * j + 32], B1[0:32, 128 * j:128 * j + 128],
                                              K[0:32, C_ID:C_ID + 32])
                finish(ins, sb_zt)
                pe.wait_ge(*sb_sp.nth(l, 0))
                mm(PS[:, 3, 0:256], kc(C_NTRI), S[:, 2, 0:256], start=True, stop=False)
                for k in range(1, PAGES):
                    ins = mm(PS[:, 3, 0:256 - 32 * k], kc(C_NONE), S[:, 2, 32 * k:256], start=False, stop=k == 7)
                finish(ins, sb_ac)
                pe.wait_ge(*sx_sel.nth(l, 0))
                for a, (bank, lo, hi) in enumerate(((4, 0, 512), (5, 512, 1024), (7, 1024, 1025))):
                    ins = mm(PS[0:32, bank, 0:hi - lo], K[0:8, C_EB:C_EB + 32], B2[0:8, lo:hi],
                             start=True, stop=True)
                finish(ins, sx_bc)
                pe.wait_ge(*sa_p.nth(l, 0))
                for j in range(PAGES):
                    nc.tensor.transpose(PS[:, 4, 32 * j:32 * j + 32], B1[0:32, 128 * j:128 * j + 128],
                                        K[0:32, C_ID:C_ID + 32])
                finish(mm(PS[:, 7, 0:32], K[0:32, C_ONE:C_ONE + 128], DG[:, :], start=True, stop=True), sa_tr)
                pe.wait_ge(*sb_a.nth(l, 0))
                pe.wait_ge(*sa_trc.nth(l, 0))
                for u in range(NU):
                    b, t = divmod(u, UPS)
                    n = FIRST["V"] + u
                    pe.wait_ge(*full(l, n))
                    for jj in range(2):
                        j, v0 = 2 * t + jj, V_REC * jj
                        mm(PS[:, 6, 4 * b:4 * b + 4], slot(l, n)[:, v0:v0 + 128],
                           S[:, 2, 32 * j + 4 * b:32 * j + 4 * b + 4], start=j == 0, stop=j == 7)
                        for c in range(2):
                            ins = mm(PS[:, 2 + c, 2 * b:2 * b + 2],
                                     slot(l, n)[:, v0 + 128 + 128 * c:v0 + 256 + 128 * c],
                                     S[:, 3, 32 * j + 4 * b + 2 * c:32 * j + 4 * b + 2 * c + 2],
                                     start=j == 0, stop=j == 7)
                    ins.then_inc(tile_used.sem, 1)
                pe.wait_ge(*sa_out.nth(l, 0))
                for s in (c_out, d_out):
                    pe.wait_ge(*s.nth(l, 1))
                pe.wait_ge(*xl_again.nth(l, 7))
                for d in range(KD):
                    nb = FIRST["gate"] + 5 * d + 4
                    for br, o in enumerate((AQ, BQ, CQ, DZ)):
                        q = 4 * d + br
                        if q >= 2:
                            pe.wait_ge(*g_sig.nth(l, q - 2))
                        dense_split(l, nb - 4 + br, 2 * (q % 2))
                    pe.wait_ge(*full(l, nb))
                    for br, o in enumerate((AQ, BQ, CQ, DZ)):
                        q = 4 * d + br
                        if q >= 2:
                            pe.wait_ge(*br_used.nth(l, q - 2))
                        for k in range(2):
                            for a in range(2):
                                ins = mm(PS[:, 4 + 2 * (q % 2) + a, 0:HALF],
                                         slot(l, nb)[:, 256 * br + 128 * k:256 * br + 128 * k + 128],
                                         F[:, o + k, a * HALF:(a + 1) * HALF], start=k == 0, stop=k == 1)
                        finish(ins, tile_used if br == 3 else br_done)
                pe.wait_ge(*br_used.nth(l, 31))
                for d in range(KD):
                    if d >= 2:
                        pe.wait_ge(*sq_ready.nth(l, 8 + d - 2))
                    else:
                        pe.wait_ge(*g_sig.nth(l, 30 + d))
                    dense(l, FIRST["out"] + d, 2 * (d % 2), lambda r: F[:, MERGED + r, :], range(KD), True, True)\
                        .then_inc(tile_used.sem, 1)
                norm_sum(l, 1)
                norm_sum(l, 2)
                pe.wait_ge(*norm_out.nth(l, 23))
                for j in range(2 * JF):
                    if j >= 4:
                        pe.wait_ge(*up_evac.nth(l, j - 4))
                    dense_split(l, FIRST["up"] + j, 2 * (j % 4))
                for d in range(KD):
                    if d >= 2:
                        pe.wait_ge(*sq_ready.nth(l, 24 + d - 2))
                    else:
                        pe.wait_ge(*up_evac.nth(l, 2 * JF - 1))
                        pe.wait_ge(*h_ready.nth(l, JF - 1))
                    for k in range(JF):
                        t, e = divmod(JF * d + k, 8)
                        n = FIRST["down"] + t
                        if e == 0 or k == 0:
                            pe.wait_ge(*full(l, n))
                        for a in range(2):
                            ins = mm(PS[:, 2 * (d % 2) + a, 0:HALF], slot(l, n)[:, 128 * e:128 * e + 128],
                                     F[:, k, a * HALF:(a + 1) * HALF], start=k == 0, stop=k == JF - 1)
                        if k == JF - 1:
                            ins.then_inc(dn_done.sem, 1)
                            if e == 7:
                                pe.wait_ge(*dn_done.nth(l, d))
                                pe.sem_inc(tile_used.sem, 1)
                        elif e == 7:
                            ins.then_inc(tile_used.sem, 1)
                norm_sum(l, 3)

        @block.scalar
        def _(act):
            A = nc.scalar.activation

            def do(ins, s=act_own):
                ins.then_inc(s.sem, 1)
                s.n += 1
                act.wait_ge(s.sem, s.n)

            stores = [0]

            def store(dst, src):
                act.dma_start(dst, src).then_inc(stored.sem, 16)

            act.wait_ge(loaded.sem, 48)

            def squares(l, j, src):
                for k in range(KD):
                    m = 8 * j + k
                    if k >= 2:
                        act.wait_ge(*sq_added.nth(l, m - 2))
                    do(A(S[:, k % 2, :], src(k), ACT.Square), sq_ready)

            def split(l, m):
                if m < 105:
                    act.wait_ge(*full(l, SPLIT[m]))
                    if m >= 2:
                        act.wait_ge(*tile_done(l, SPLIT[m - 2]))
                    elif l:
                        act.wait_ge(*tile_done(l - 1, SPLIT[103 + m]))
                    do(A(WH[:, m % 2, :], slot(l, SPLIT[m]), ACT.Copy), w_hi)

            def leading(l, half):
                for k in range(KD):
                    act.wait_ge(*xt_ready.nth(l, 8 * half + k))
                    do(A(XH[:, k, :], S[:, k % 2, :], ACT.Copy), xh_ready)

            def root(l, j):
                act.wait_ge(*sum_ready.nth(l, j))
                do(A(halves(S[:, 3, :]), pair(4), ACT.Sqrt, bias=eps, scale=1.0 / DM), root_ready)

            for l in range(L):
                squares(l, 0, lambda k: X[:, k, :]) if l == 0 else None
                if l:
                    for k in range(KD):
                        act.wait_ge(*norm_out.nth(l - 1, 31))
                        if k >= 2:
                            act.wait_ge(*sq_added.nth(l, k - 2))
                        do(A(S[:, k % 2, :], X[:, k, :], ACT.Square), sq_ready)
                split(l, 0)
                split(l, 1)
                root(l, 0)
                leading(l, 0)
                for c in range(NPROJ):
                    act.wait_ge(*tile_done(l, c))
                    if c + 2 < NPROJ:
                        split(l, c + 2)
                    do(A(halves(F[:, c, :]), pair(2 * (c % 2)), ACT.Copy), proj_out)
                if l:
                    act.wait_ge(stored.sem, N_STORES_UPTO[l - 1])
                for c in range(7):
                    if c < 6:
                        if c >= 2:
                            pass
                        else:
                            act.wait_ge(*rope_done.nth(l, 5))
                        do(A(S[:, c % 2, :], F[:, XX + c, :], ACT.Identity,
                             bias=V[:, l, V_DCB + c:V_DCB + c + 1],
                             scale=V[:, l, V_DCW + 4 * c + 3:V_DCW + 4 * c + 4]), cv_init)
                    if c >= 1:
                        act.wait_ge(*cv_done.nth(l, c - 1))
                        do(A(DO[:, c - 1, :], F[:, XX + c - 1, NPR - 3:TOK], ACT.Copy), cv_saved)
                        do(A(F[:, XX + c - 1, :], S[:, (c - 1) % 2, :], ACT.Silu), xbc_ready)
                for i, (src, dst) in enumerate(TO_TM):
                    act.wait_ge(*tm_done.nth(l, i))
                    src_t = PS[:, 4 + i % 4, :].rearrange("p (t c) -> p t c", c=128)
                    if dst == T_SM:
                        do(A(SMT[:, :, 48:64], src_t[:, :, 64:80], ACT.Copy), tm_ready)
                    else:
                        do(A(TM[:, dst, :, :], src_t, ACT.Copy), tm_ready)
                act.wait_ge(*sm_v.nth(l, 0))
                do(A(SMT[:, :, 8:16], SMT[:, :, 0:8], ACT.Abs))
                do(A(SMT[:, :, 8:16], SMT[:, :, 8:16], ACT.Exp, scale=-1.0))
                do(A(SMT[:, :, 8:16], SMT[:, :, 8:16], ACT.Ln, bias=one), sm_ln)
                do(A(NEGA[:, 4:8], V[:, l, V_AL:V_AL + 4], ACT.Exp), sm_ln)
                act.wait_ge(*sm_tr.nth(l, 0))
                do(A(SROW[0:96, :], PS[0:96, 5, :], ACT.Copy), sm_row)
                act.wait_ge(*sm_g.nth(l, 0))
                do(A(SROW[0:4, :], SROW[0:4, :], ACT.Copy, scale=-1.0))
                do(A(ML[:, :], MR[:, NPR - 1:NPR], ACT.Copy))
                do(A(MR[:, :], MR[:, :], ACT.Exp, scale=-1.0), sm_em)
                store(pm_o[l], ML[:, :])
                act.wait_ge(*rope_done.nth(l, 5))
                store(ka_o[l], F[:, AK, :])
                store(va_o[l], F[:, AV, :])
                store(ki_o[l], F[0:64, IKD, :])
                store(kb_o[l], F[:, BK:BK + 2, :])
                store(vb_o[l], F[:, BV:BV + 2, :])
                store(dconv_o[l], DO[:, :, :])
                act.wait_ge(st_loaded.sem, 48 * (l + 1))
                store(dconv_s_o[l], ST[:, S_DC:S_DC + 144])
                act.wait_ge(*r_v.nth(l, 0))
                do(A(SS[:, 5:7, :], SS[:, 3:5, :], ACT.Abs))
                do(A(SS[:, 5:7, :], SS[:, 5:7, :], ACT.Exp, scale=-1.0))
                do(A(SS[:, 5:7, :], SS[:, 5:7, :], ACT.Ln, bias=one))
                do(A(SS[:, 17, 0:2], V[:, l, V_SAL:V_SAL + 2], ACT.Exp), r_ln)
                act.wait_ge(*r_arg.nth(l, 0))
                do(A(SS[:, 11:15, :], SS[:, 7:11, :], ACT.Exp), r_exp)
                act.wait_ge(*r_tr.nth(l, 0))
                do(A(S[0:8, 2:4, 0:512], PS[0:8, 0:2, :], ACT.Copy), r_trc)
                for c in range(2):
                    do(A(F[:, CO + c, :], F[:, CO + c, :], ACT.Sigmoid), c_sg)
                for c in range(2):
                    do(A(F[:, DZ + c, :], F[:, DZ + c, :], ACT.Silu), d_sl)
                def decays(v):
                    h, E = v % 4, (B1, B2)[v % 2]
                    act.wait_ge(*bc_done.nth(l, v))
                    if v >= 2:
                        act.wait_ge(*num_done.nth(l, v - 2))
                    for i in range(NT):
                        col = SMT[:, i, 40 + h:41 + h] if v < 4 else RT[:, i, 32 + h:33 + h]
                        do(A(E[:, OFF[i]:OFF[i] + NPR - 128 * i], PS[:, 4, 128 * i:NPR], ACT.Relu, bias=col,
                             scale=-1.0), ex_arg if i == NT - 1 else act_own)
                    do(A(E[:, :], E[:, :], ACT.Exp, scale=-1.0), ex_done)
                act.wait_ge(*sm_ng.nth(l, 0))
                decays(0)
                for v in range(8):
                    if v < 7:
                        decays(v + 1)
                    if v in (1, 3):
                        c = v // 2
                        act.wait_ge(*num_done.nth(l, v))
                        do(A(S[:, 0, 0:NPR], PS[:, 2, :], ACT.Abs), c_abs)
                        act.wait_ge(*c_h.nth(l, c))
                        do(A(S[:, 2, :], S[:, 1, :], ACT.Square), c_sq)
                        act.wait_ge(*c_sum.nth(l, c))
                        do(A(halves(S[:, 3, :]), pair(2), ACT.Sqrt, bias=eps, scale=1.0 / HD), c_root)
                for c in range(2):
                    act.wait_ge(*d_y.nth(l, c))
                    do(A(S[:, 2 + c, :], S[:, c, :], ACT.Square), d_sq)
                act.wait_ge(*d_sum.nth(l, 0))
                do(A(halves(S[:, 4, :]), pair(2), ACT.Sqrt, bias=eps, scale=1.0 / 256), d_root)
                do(A(PST[:, :], PS[:, 7, 0:386], ACT.Copy), pst_done)
                store(pc_o[l], PST[:, 0:128])
                store(pn_o[l], PST[:, 128:130])
                store(pssm_o[l], PST[:, 130:386])
                act.wait_ge(*r_out.nth(l, 0))
                store(sc_o[l], CS[:, :, :, :])
                store(sssm_o[l], HS[:, :, :, :])
                store(sn_o[l], SS[:, 22, :])
                store(sm_o[l], SS[:, 21, :])
                for h in range(4):
                    act.wait_ge(*z_done.nth(l, h))
                    for i in range(NT):
                        n = NPR - 128 * i
                        do(A(B1[:, OFF[i]:OFF[i] + n], PS[:, 4 + i, 0:n], ACT.Abs))
                    do(A(B1[:, :], B1[:, :], ACT.Exp, scale=-1.0))
                    do(A(B1[:, :], B1[:, :], ACT.Ln, bias=one), z_ln)
                    act.wait_ge(*ac_done.nth(l, h))
                    for i in range(NT):
                        n = NPR - 128 * i
                        if i == NT - 1:
                            do(A(B3[:, OFF[i]:OFF[i] + n], PS[:, 4 + i, 0:n], ACT.Exp), a_exp)
                        else:
                            do(A(B3[:, OFF[i]:OFF[i] + n], PS[:, 4 + i, 0:n], ACT.Exp))
                    if h % 2:
                        act.wait_ge(*pv_done.nth(l, h))
                        do(A(F[:, BQ + h // 2, 0:NPR], PS[:, 0, :], ACT.Copy), b_out)
                for i in range(NT):
                    w = 128 * (i + 1)
                    act.wait_ge(*ix_done.nth(l, i))
                    for h in range(4):
                        if h < 3:
                            do(A(S[:, h, 0:w], PS[:, 4 + h, 0:w], ACT.Relu))
                        else:
                            do(A(S[:, h, 0:w], PS[:, 4 + h, 0:w], ACT.Relu), ix_relu)
                    for h in range(4):
                        m = 4 * i + h
                        act.wait_ge(*at_max.nth(l, m))
                        do(A(S[:, h, 0:w], S[:, h, 0:w], ACT.Exp, bias=MX[:, h:h + 1], scale=0.125,
                             accum_out=MX[:, 4 + h:5 + h]), at_exp)
                    for h in range(4):
                        m = 4 * i + h
                        act.wait_ge(*at_tr.nth(l, m))
                        if m >= 2:
                            act.wait_ge(*at_pv.nth(l, m - 2))
                        do(A(B3[:, 512 * (h % 2):512 * (h % 2) + w], PS[:, 4 + h, 0:w], ACT.Copy), at_trc)
                act.wait_ge(*at_pv.nth(l, 15))
                for c in range(2):
                    do(A(F[:, AQ + c, 0:NPR], PS[:, c, :], ACT.Copy), a_out)
                def wide(ap):
                    return ap.rearrange("p (a c) -> p a c", a=2)
                act.wait_ge(*sx_done.nth(l, 0))
                do(A(wide(B3[0:32, 0:1024]), PS[0:32, 4:6, :], ACT.Relu))
                do(A(B3[0:32, 1024:1025], PS[0:32, 6, 0:1], ACT.Relu), sx_relu)
                do(A(wide(B1[0:32, 0:1024]), PS[0:32, 2:4, :], ACT.Copy), sb_zc)
                act.wait_ge(*sx_done.nth(l, 1))
                do(A(wide(B2[0:8, 0:1024]), PS[0:8, 4:6, :], ACT.Copy))
                do(A(B2[0:8, 1024:1025], PS[0:8, 7, 0:1], ACT.Copy), sx_score)
                act.wait_ge(*sb_zt.nth(l, 0))
                do(A(S[:, 1, 0:256], PS[:, 2, 0:256], ACT.Copy))
                do(A(S[:, 0, 0:256], S[:, 1, 0:256], ACT.Abs))
                do(A(S[:, 0, 0:256], S[:, 0, 0:256], ACT.Exp, scale=-1.0))
                do(A(S[:, 0, 0:256], S[:, 0, 0:256], ACT.Ln, bias=one), sb_ln)
                act.wait_ge(*sb_arg.nth(l, 0))
                do(A(S[:, 3, 0:256], S[:, 1, 0:256], ACT.Exp), sb_a)
                act.wait_ge(*sx_bc.nth(l, 0))
                act.wait_ge(*sa_max.nth(l, 0))
                do(A(B1[0:32, 0:1025], B1[0:32, 0:1025], ACT.Exp, bias=MX[0:32, 8:9], scale=0.125,
                     accum_out=MX[0:32, 9:10]), sa_exp)
                act.wait_ge(*sa_tr.nth(l, 0))
                do(A(S[:, 2, 0:256], PS[:, 4, 0:256], ACT.Copy), sa_trc)
                split(l, NPROJ)
                split(l, NPROJ + 1)
                for q in range(32):
                    act.wait_ge(*tile_done(l, FIRST["gate"] + 5 * (q // 4) + q % 4))
                    if q + 2 < 32:
                        split(l, NPROJ + q + 2)
                    if q >= 4:
                        act.wait_ge(*br_used.nth(l, q - 4))
                    do(A(halves(S[:, q % 4, :]), pair(2 * (q % 2)), ACT.Sigmoid), g_sig)

                def evac(l, j, done, out):
                    for d in range(KD):
                        act.wait_ge(*done(d))
                        do(A(halves(F[:, out + d, :]), pair(2 * (d % 2)), ACT.Copy))
                        if d >= 2:
                            act.wait_ge(*sq_added.nth(l, 8 * j + d - 2))
                        else:
                            act.wait_ge(*(br_used.nth(l, 31) if j == 1 else h_ready.nth(l, JF - 1)))
                        do(A(halves(S[:, d % 2, :]), pair(2 * (d % 2)), ACT.Square), sq_ready)
                    root(l, j)

                evac(l, 1, lambda d: tile_done(l, FIRST["out"] + d), 0)
                for k in range(KD):
                    act.wait_ge(*norm_out.nth(l, 8 + k))
                    if k >= 2:
                        act.wait_ge(*sq_added.nth(l, 16 + k - 2))
                    do(A(S[:, k % 2, :], X[:, k, :], ACT.Square), sq_ready)
                split(l, 61)
                split(l, 62)
                root(l, 2)
                leading(l, 1)
                for j in range(JF):
                    for g in range(2):
                        m = 2 * j + g
                        ch = g * JF + j
                        act.wait_ge(*tile_done(l, FIRST["up"] + m))
                        if m + 2 < 2 * JF:
                            split(l, 61 + m + 2)
                        if m >= 2:
                            act.wait_ge(*fcv.nth(l, m - 2))
                        else:
                            act.wait_ge(*norm_out.nth(l, 23))
                        do(A(halves(S[:, g, :]), pair(2 * (m % 4)), ACT.Copy))
                        do(A(FO[:, ch, :], S[:, g, NPR - 2:TOK], ACT.Copy))
                        if j:
                            act.wait_ge(*h_ready.nth(l, j - 1))
                        do(A(halves(S[:, 2 + g, :]), pair(2 * (m % 4)), ACT.Identity,
                             bias=V[:, l, V_FCB + ch:V_FCB + ch + 1],
                             scale=V[:, l, V_FCW + 3 * ch + 2:V_FCW + 3 * ch + 3]), up_evac)
                    act.wait_ge(*fcv.nth(l, 2 * j + 1))
                    do(A(S[:, 4, :], S[:, 3, :], ACT.Gelu_apprx_tanh), gl_done)
                store(fconv_o[l], FO[:, :, :])
                store(fconv_s_o[l], ST[:, S_FC:S_FC + 4 * JF * 8])
                evac(l, 3, lambda d: dn_done.nth(l, d), JF)

        @block.vector
        def _(dve):
            v_ = nc.vector

            def do(ins, s=dve_own):
                ins.then_inc(s.sem, 1)
                s.n += 1
                dve.wait_ge(s.sem, s.n)

            def tt(out, a, b, op, s=dve_own):
                do(v_.tensor_tensor(out, a, b, op), s)

            def stt(out, a, sc, b, o0, o1, s=dve_own):
                do(v_.scalar_tensor_tensor(out, a, sc, b, o0, o1), s)

            def ts(out, a, s1, s2, o0, o1, s=dve_own):
                do(v_.tensor_scalar(out, a, s1, s2, o0, o1), s)

            for t in (QI, QA, RT, QB):
                do(v_.memset(t[:], 0.0))
            dve.wait_ge(loaded.sem, 48)

            def add_squares(l, j):
                for k in range(KD):
                    dve.wait_ge(*sq_ready.nth(l, 8 * j + k))
                    if k == 0:
                        do(v_.tensor_copy(S[:, 2, :], S[:, 0, :]), sq_added)
                    else:
                        tt(S[:, 2, :], S[:, 2, :], S[:, k % 2, :], ALU.add, sq_added)
                dve.wait_ge(*root_ready.nth(l, j))
                do(v_.reciprocal(S[:, 3, :], S[:, 3, :]))

            def split(l, m):
                if m < 105:
                    dve.wait_ge(*w_hi.nth(l, m))
                    tt(WL[:, m % 2, :], slot(l, SPLIT[m]), WH[:, m % 2, :].bitcast(f32), ALU.subtract, w_lo)

            def pre_norm(l, j, col):
                add_squares(l, j)
                do(v_.tensor_copy(RB[:, :], S[:, 3, :]))

                def rest(k):
                    dve.wait_ge(*xh_ready.nth(l, 4 * j + k))
                    tt(XL[:, k, :], S[:, k % 2, :], XH[:, k, :].bitcast(f32), ALU.subtract, norm_out)
                for k in range(KD):
                    if k >= 2:
                        rest(k - 2)
                    stt(S[:, k % 2, :], X[:, k, :], V[:, l, col + k:col + k + 1], RB[:, :], ALU.mult, ALU.mult,
                        xt_ready)
                rest(6)
                rest(7)

            def post_norm(l, j, col, out):
                add_squares(l, j)
                for k in range(KD):
                    stt(S[:, 4, :], F[:, out + k, :], V[:, l, col + k:col + k + 1], S[:, 3, :], ALU.mult, ALU.mult)
                    tt(X[:, k, :], X[:, k, :], S[:, 4, :], ALU.add, norm_out)

            for l in range(L):
                def vc(col, n=1, p0=0, p1=128):
                    return V[p0:p1, l, col:col + n]

                pre_norm(l, 0, V_NPRE)
                for m in range(NPROJ):
                    split(l, m)
                for i, c in enumerate([AQ, AQ + 1, AK, IQ, IQ + 1]):
                    dve.wait_ge(*proj_out.nth(l, c))
                    tt(S[:, 0, :], F[:, c, :], kc(C_COS, TOK), ALU.mult)
                    dve.wait_ge(*perm_done.nth(l, i))
                    tt(halves(S[:, 1, :]), pair(4 + 2 * (i % 2)), halves(kc(C_SIN, TOK)), ALU.mult, perm_used)
                    tt(F[:, c, :], S[:, 0, :], S[:, 1, :], ALU.add, rope_done)
                dve.wait_ge(*perm_done.nth(l, 5))
                tt(halves(S[:, 0, :]), pair(6), halves(kc(C_COS, TOK)), ALU.mult, perm_used)
                dve.wait_ge(*perm_done.nth(l, 6))
                tt(halves(S[:, 1, :]), pair(4), halves(kc(C_SIN, TOK)), ALU.mult, perm_used)
                tt(F[:, IKD, :], S[:, 0, :], S[:, 1, :], ALU.add, rope_done)
                dve.wait_ge(st_loaded.sem, 48 * (l + 1))
                for c in range(6):
                    dve.wait_ge(*cv_init.nth(l, c))
                    y, x = S[:, c % 2, :], F[:, XX + c, :]
                    for k in range(3):
                        w = vc(V_DCW + 4 * c + k)
                        d = 3 - k
                        stt(y[:, d:NPR], x[:, 0:NPR - d], w, y[:, d:NPR], ALU.mult, ALU.add)
                        o = S_DC + 24 * c + 8 * k
                        stt(y[:, NPR:TOK], ST[:, o:o + 8], w, y[:, NPR:TOK], ALU.mult, ALU.add,
                            cv_done if k == 2 else dve_own)
                dve.wait_ge(*scaled.nth(l, 1))

                def place(t, h):
                    return t.rearrange("p b c -> p (b c)")[:, h:h + 36 * 7 + 1:36]
                for h in range(4):
                    r0 = 64 * (h % 2)
                    do(v_.tensor_copy(place(QI[:, :, :], h), F[r0:r0 + 64, IQ + h // 2, NPR:TOK]))
                    do(v_.tensor_copy(place(QB[r0:r0 + 64, h // 2, :, :], h), F[r0:r0 + 64, BQ + h // 2, NPR:TOK]))
                    r0 = 64 * (h // 2)
                    do(v_.tensor_copy(place(QA[r0:r0 + 64, :, :], h), F[r0:r0 + 64, AQ + h % 2, NPR:TOK]),
                       q_pad if h == 3 else dve_own)
                dve.wait_ge(*tm_ready.nth(l, 0))
                t0 = SMT[:, :, 48:64]

                def bc3(ap, n, axis_len):
                    return ap.unsqueeze(1).to_broadcast([128, n, axis_len])
                tt(SMT[:, :, 0:8], t0[:, :, 8:16], bc3(vc(V_BFD, 8), NT, 8), ALU.add)
                tt(SMT[:, :, 0:8], SMT[:, :, 0:8], bc3(kc(C_SGN, 8), NT, 8), ALU.mult, sm_v)
                tt(SMT[:, :, 32:36], t0[:, :, 4:8], bc3(vc(V_BI, 4), NT, 4), ALU.add)
                ts(SMT[:, :, 36:40], t0[:, :, 0:4], 1.0 / 16, None, ALU.mult, ALU.bypass)
                dve.wait_ge(*sm_ln.nth(l, 1))
                stt(SMT[:, :, 24:32], SMT[:, :, 0:8], 0.0, SMT[:, :, 8:16], ALU.max, ALU.add)
                do(v_.memset(NEGA[:, 0:4], -1.0))
                ts(NEGA[:, 4:8], NEGA[:, 4:8], -1.0, None, ALU.mult, ALU.bypass)
                tt(SMT[:, :, 16:24], SMT[:, :, 24:32], bc3(NEGA[:, :], NT, 8), ALU.mult, sm_cin)
                dve.wait_ge(*sm_cum.nth(l, 0))
                cum = PS[:, 4, 0:32].rearrange("p (t c) -> p t c", t=NT)
                tt(RT[:, :, 0:4], SMT[:, :, 32:36], cum[:, :, 0:4], ALU.subtract)
                do(v_.tensor_copy(RT[:, :, 32:36], cum[:, :, 4:8]))
                do(v_.tensor_copy(RT[:, :, 64:68], cum[:, :, 0:4]), sm_rt)
                ts(SMT[:, :, 40:44], RT[:, :, 0:4], -1.0, None, ALU.mult, ALU.bypass, sm_ng)
                dve.wait_ge(*sm_row.nth(l, 0))
                do(v_.tensor_tensor_scan(SROW[0:4, :], SROW[0:4, :], SROW[0:4, :], 0.0, ALU.max, ALU.max))
                tt(MR[:, :], SROW[0:4, :], PS[64:68, 5, :], ALU.add, sm_g)
                dve.wait_ge(*tm_ready.nth(l, 9))
                for c in range(2):
                    x4 = TM[:, T_XX + c, :, :].rearrange("p t (h d) -> p t h d", h=2)
                    tt(x4, x4, SMT[:, :, 28 + 2 * c:30 + 2 * c].unsqueeze(3).to_broadcast([128, NT, 2, HD]), ALU.mult)
                def fs(c0):
                    return F[:, c0:c0 + 2, NPR:TOK]

                def ss(i):
                    return SS[:, i, :].rearrange("p (c b) -> p c b", c=2)

                def bb(col):
                    return vc(col, 2).unsqueeze(2).to_broadcast([128, 2, NSM])
                dve.wait_ge(*xbc_ready.nth(l, 5))
                tt(ss(0), fs(CQ), fs(CK), ALU.mult)
                tt(ss(1), fs(CQ), ST[:, S_N:S_N + 16].rearrange("p (c b) -> p c b", c=2), ALU.mult)
                tt(ss(2), fs(XB), fs(XC), ALU.mult, r_prod)
                dve.wait_ge(*r_sel.nth(l, 0))
                sel = PS[:, 6, 0:48].rearrange("p (k c b) -> p k c b", k=3, c=2)
                tt(ss(15), sel[:, 0], bb(V_SBI), ALU.add)
                tt(ss(16), sel[:, 1], bb(V_SBF), ALU.add)
                ts(ss(3), ss(16), -1.0, None, ALU.mult, ALU.bypass)
                tt(ss(4), sel[:, 2], bb(V_SBD), ALU.add, r_v)
                dve.wait_ge(*r_ln.nth(l, 0))
                stt(SS[:, 5:7, :], SS[:, 3:5, :], 0.0, SS[:, 5:7, :], ALU.max, ALU.add)
                tt(ss(16), ST[:, S_M:S_M + 16].rearrange("p (c b) -> p c b", c=2), ss(5), ALU.subtract)
                tt(ss(21), ss(16), ss(15), ALU.max)
                tt(ss(7), ss(16), ss(21), ALU.subtract)
                tt(ss(8), ss(15), ss(21), ALU.subtract)
                ts(ss(9), ss(21), -1.0, None, ALU.mult, ALU.bypass)
                stt(ss(10), ss(6), -1.0, SS[:, 17, 0:2].unsqueeze(2).to_broadcast([128, 2, NSM]),
                    ALU.mult, ALU.mult, r_arg)
                dve.wait_ge(*r_exp.nth(l, 0))
                dve.wait_ge(*r_dot.nth(l, 0))
                dots = PS[:, 7, 0:48].rearrange("p (k c b) -> p k c b", k=3, c=2)
                tt(ss(18), dots[:, 0], ss(12), ALU.mult)
                tt(ss(19), dots[:, 1], ss(11), ALU.mult)
                tt(ss(19), ss(19), ss(18), ALU.add)
                tt(ss(22), ss(11), ST[:, S_N:S_N + 16].rearrange("p (c b) -> p c b", c=2), ALU.mult)
                tt(ss(20), ss(12), fs(CK), ALU.mult)
                tt(ss(22), ss(22), ss(20), ALU.add)
                tt(ss(20), ss(12), fs(CV), ALU.mult)
                tt(ss(23), ss(6), fs(XX), ALU.mult)
                tt(ss(0), dots[:, 2], ss(23), ALU.mult)
                for s in range(8):
                    dve.wait_ge(*r_bc.nth(l, s))
                    bank = 2 * (s % 2)
                    c = s % 2
                    wide = HD if s < 4 else 128
                    if s < 4:
                        p = PS[:, bank, :].rearrange("p (b d) -> p b d", b=NSM)
                        stt_, t = CS[:, c], B3[:, 0:512].rearrange("p (b d) -> p b d", b=NSM)
                    else:
                        p = PS[:, bank:bank + 2, :].rearrange("p a (b d) -> p (a b) d", d=128)
                        stt_, t = HS[:, c], B3[:, 0:1024].rearrange("p (b d) -> p b d", b=NSM)

                    def over(i):
                        return SS[:, i, 8 * c:8 * c + 8].unsqueeze(2).to_broadcast([128, NSM, wide])
                    if s in (0, 1, 4, 5):
                        tt(t, stt_, p, ALU.mult, r_bcu)
                        do(v_.tensor_reduce(SS[:, 1 if s < 4 else 2, 8 * c:8 * c + 8], t, AX, ALU.add))
                    else:
                        tt(t, p, over(20 if s < 4 else 23), ALU.mult, r_bcu)
                        tt(stt_, stt_, over(11 if s < 4 else 14), ALU.mult)
                        tt(stt_, stt_, t, ALU.add)
                tt(ss(1), ss(1), ss(11), ALU.mult)
                tt(ss(3), ss(18), fs(CV), ALU.mult)
                tt(ss(1), ss(1), ss(3), ALU.add)
                ts(ss(4), ss(19), -1.0, None, ALU.mult, ALU.bypass)
                tt(ss(19), ss(19), ss(4), ALU.max)
                tt(ss(19), ss(19), ss(13), ALU.max)
                do(v_.reciprocal(ss(19), ss(19)))
                tt(ss(1), ss(1), ss(19), ALU.mult)
                tt(ss(2), ss(2), ss(14), ALU.mult)
                tt(ss(2), ss(2), ss(0), ALU.add, r_out)
                for v in range(8):
                    h, c, r0 = v % 4, (v % 4) // 2, 64 * (v % 2)
                    E = (B1, B2)[v % 2]
                    dve.wait_ge(*vu_ready.nth(l, v))
                    for i in range(NT):
                        n = NPR - 128 * i
                        m = 4 * v + i
                        dve.wait_ge(*st_block.nth(l, m))
                        tt(E[:, OFF[i]:OFF[i] + n], E[:, OFF[i]:OFF[i] + n], PS[:, 5 + m % 2, 0:n], ALU.mult,
                           w_ready)
                    if v in (1, 3):
                        dve.wait_ge(*c_em.nth(l, c))
                        dve.wait_ge(*c_abs.nth(l, c))
                        tt(S[:, 0, 0:NPR], S[:, 0, 0:NPR], PS[:, 3, :], ALU.max)
                        do(v_.reciprocal(S[:, 0, 0:NPR], S[:, 0, 0:NPR]))
                        do(v_.tensor_copy(S[:, 1, NPR:TOK], SS[:, 1, 8 * c:8 * c + 8]))
                        tt(S[:, 1, 0:NPR], PS[:, 0, :], S[:, 0, 0:NPR], ALU.mult, c_h)
                        dve.wait_ge(*c_root.nth(l, c))
                        do(v_.reciprocal(S[:, 3, :], S[:, 3, :]))
                        tt(S[:, 1, :], S[:, 1, :], S[:, 3, :], ALU.mult)
                        dve.wait_ge(*c_sg.nth(l, c))
                        stt(F[:, CQ + c, :], S[:, 1, :], vc(V_CN + c), F[:, CO + c, :], ALU.mult, ALU.mult, c_out)
                dve.wait_ge(*num_done.nth(l, 7))
                for c in range(2):
                    do(v_.tensor_copy(S[:, 4, NPR:TOK], SS[:, 2, 8 * c:8 * c + 8]))
                    do(v_.tensor_copy(S[:, 4, 0:NPR], PS[:, c, :]))
                    stt(S[:, c, :], F[:, XX + c, :], vc(V_D + c), S[:, 4, :], ALU.mult, ALU.add)
                    dve.wait_ge(*d_sl.nth(l, c))
                    tt(S[:, c, :], S[:, c, :], F[:, DZ + c, :], ALU.mult, d_y)
                dve.wait_ge(*d_root.nth(l, 0))
                do(v_.reciprocal(S[:, 4, :], S[:, 4, :]))
                for c in range(2):
                    stt(F[:, DZ + c, :], S[:, c, :], vc(V_DN + c), S[:, 4, :], ALU.mult, ALU.mult, d_out)
                for h in range(4):
                    dve.wait_ge(*z_ln.nth(l, h))
                    for i in range(NT):
                        n = NPR - 128 * i
                        stt(B2[:, OFF[i]:OFF[i] + n], PS[:, 4 + i, 0:n], 0.0, B1[:, OFF[i]:OFF[i] + n],
                            ALU.max, ALU.add, sp_done if i == NT - 1 else dve_own)
                dve.wait_ge(*b_out.nth(l, 1))
                for i in range(NT):
                    w = 128 * (i + 1)
                    dve.wait_ge(*ix_relu.nth(l, i))
                    ts(B1[:, 0:w], S[:, 0, 0:w], SMT[:, i, 36:37], None, ALU.mult, ALU.bypass)
                    for h in range(1, 4):
                        stt(B1[:, 0:w], S[:, h, 0:w], SMT[:, i, 36 + h:37 + h], B1[:, 0:w], ALU.mult, ALU.add,
                            ix_sum if h == 3 else dve_own)
                    dve.wait_ge(*ix_mask.nth(l, i))
                    if w <= TOPK_P:
                        ts(B2[:, 0:w], B1[:, 0:w], NEG / 2, NEG, ALU.is_le, ALU.mult, bias_ready)
                    else:
                        for _ in range(TOPK_P // 8):
                            do(v_.max(M8[:, :], B1[:, 0:w]))
                            do(v_.match_replace(B1[:, 0:w], M8[:, :], B1[:, 0:w], TAKEN))
                        ts(B2[:, 0:w], B1[:, 0:w], TAKEN / 2, NEG, ALU.is_gt, ALU.mult, bias_ready)
                    for h in range(4):
                        dve.wait_ge(*at_qk.nth(l, 4 * i + h))
                        tt(S[:, h, 0:w], PS[:, 4 + h, 0:w], B2[:, 0:w], ALU.add)
                        do(v_.reduce_max(MX[:, h:h + 1], S[:, h, 0:w], AX))
                        ts(MX[:, h:h + 1], MX[:, h:h + 1], -0.125, None, ALU.mult, ALU.bypass, at_max)
                    for h in range(4):
                        dve.wait_ge(*at_exp.nth(l, 4 * i + h))
                        do(v_.reciprocal(MX[:, 4 + h:5 + h], MX[:, 4 + h:5 + h]))
                        ts(S[:, h, 0:w], S[:, h, 0:w], MX[:, 4 + h:5 + h], None, ALU.mult, ALU.bypass, at_norm)
                dve.wait_ge(*sx_done.nth(l, 0))
                stt(IWW[:, :], PS[0:32, 7, 0:8], 1.0 / 16, K[0:32, C_EM:C_EM + 8], ALU.mult, ALU.mult, sx_iw)
                dve.wait_ge(*sx_score.nth(l, 0))
                for k in range(TOPK_S // 8):
                    if k == 4:
                        dve.wait_ge(*sb_ln.nth(l, 0))
                        stt(S[:, 2, 0:256], S[:, 1, 0:256], 0.0, S[:, 0, 0:256], ALU.max, ALU.add, sb_sp)
                    if k == 8:
                        dve.wait_ge(*sb_ac.nth(l, 0))
                        tt(S[:, 1, 0:256], S[:, 1, 0:256], PS[:, 3, 0:256], ALU.add, sb_arg)
                    do(v_.max(M8[0:8, :], B2[0:8, 0:PAST + 1]))
                    do(v_.match_replace(B2[0:8, 0:PAST + 1], M8[0:8, :], B2[0:8, 0:PAST + 1], TAKEN))
                ts(B2[0:8, 0:PAST + 1], B2[0:8, 0:PAST + 1], TAKEN / 2, None, ALU.is_le, ALU.bypass, sx_sel)
                def wide(ap):
                    return ap.rearrange("p (a c) -> p a c", a=2)
                dve.wait_ge(*sx_bc.nth(l, 0))
                ts(wide(B3[0:32, 0:1024]), PS[0:32, 4:6, :], -NEG, NEG, ALU.mult, ALU.add)
                ts(B3[0:32, 1024:1025], PS[0:32, 7, 0:1], -NEG, NEG, ALU.mult, ALU.add)
                tt(wide(B1[0:32, 0:1024]), PS[0:32, 0:2, :], wide(B3[0:32, 0:1024]), ALU.add)
                tt(B1[0:32, 1024:1025], PS[0:32, 6, 1:2], B3[0:32, 1024:1025], ALU.add)
                do(v_.reduce_max(MX[0:32, 8:9], B1[0:32, 0:1025], AX))
                ts(MX[0:32, 8:9], MX[0:32, 8:9], -0.125, None, ALU.mult, ALU.bypass, sa_max)
                dve.wait_ge(*sa_exp.nth(l, 0))
                do(v_.reciprocal(MX[0:32, 9:10], MX[0:32, 9:10]))
                ts(B1[0:32, 0:1025], B1[0:32, 0:1025], MX[0:32, 9:10], None, ALU.mult, ALU.bypass)
                ts(DG[:, :], K[0:32, C_ID:C_ID + 32], B1[0:32, 1024:1025], None, ALU.mult, ALU.bypass, sa_p)
                dve.wait_ge(*sa_tr.nth(l, 0))
                tt(OS[:, :].rearrange("p (b h) -> p b h", h=4), PS[:, 7, 0:32].rearrange("p (b h) -> p b h", h=4),
                   F[:, AV, NPR:TOK].unsqueeze(2).to_broadcast([128, NSM, 4]), ALU.mult)
                dve.wait_ge(*tile_done(l, FIRST["V"] + NU - 1))
                tt(OS[:, :], OS[:, :], PS[:, 6, 0:32], ALU.add)
                for h in range(4):
                    r0 = 64 * (h // 2)
                    do(v_.tensor_copy(F[r0:r0 + 64, AQ + h % 2, NPR:TOK], OS[r0:r0 + 64, h:32:4]))
                for h in range(4):
                    r0, c = 64 * (h % 2), h // 2
                    do(v_.tensor_copy(F[r0:r0 + 64, BQ + c, NPR:TOK], PS[r0:r0 + 64, 2 + c, h % 2:16:2]),
                       sa_out if h == 3 else dve_own)
                for k in range(KD):
                    stt(S[:, k % 2, :], X[:, k, :], V[:, l, V_NPRE + k:V_NPRE + k + 1], RB[:, :], ALU.mult, ALU.mult)
                    tt(XL[:, k, :], S[:, k % 2, :], XH[:, k, :].bitcast(f32), ALU.subtract, xl_again)
                dve.wait_ge(stored.sem, N_STORES_MID[l])
                split(l, NPROJ)
                split(l, NPROJ + 1)
                for d in range(KD):
                    for m in range(4 * d + 2, min(4 * d + 6, 32)):
                        split(l, NPROJ + m)
                    for br in range(4):
                        q = 4 * d + br
                        dve.wait_ge(*g_sig.nth(l, q))
                        dve.wait_ge(*(tile_done(l, FIRST["gate"] + 5 * d + 4) if br == 3
                                      else br_done.nth(l, 3 * d + br)))
                        p = pair(4 + 2 * (q % 2))
                        if br == 0:
                            tt(halves(F[:, MERGED + d, :]), halves(S[:, q % 4, :]), p, ALU.mult, br_used)
                        else:
                            tt(halves(S[:, 4, :]), halves(S[:, q % 4, :]), p, ALU.mult)
                            tt(F[:, MERGED + d, :], F[:, MERGED + d, :], S[:, 4, :], ALU.add, br_used)
                post_norm(l, 1, V_NPOST, 0)
                pre_norm(l, 2, V_FPRE)
                split(l, 61)
                split(l, 62)
                for j in range(JF):
                    for g in range(2):
                        m, ch = 2 * j + g, g * JF + j
                        if m + 2 < 2 * JF:
                            split(l, 61 + m + 2)
                        dve.wait_ge(*up_evac.nth(l, m))
                        u, y = S[:, g, :], S[:, 2 + g, :]
                        for k in range(2):
                            w = vc(V_FCW + 3 * ch + k)
                            d = 2 - k
                            stt(y[:, d:NPR], u[:, 0:NPR - d], w, y[:, d:NPR], ALU.mult, ALU.add)
                            o = S_FC + 16 * ch + 8 * k
                            stt(y[:, NPR:TOK], ST[:, o:o + 8], w, y[:, NPR:TOK], ALU.mult, ALU.add,
                                fcv if k == 1 else dve_own)
                    dve.wait_ge(*gl_done.nth(l, j))
                    tt(F[:, j, :], S[:, 2, :], S[:, 4, :], ALU.mult, h_ready)
                post_norm(l, 3, V_FPOST, JF)

        @block.gpsimd
        def _(pool):
            g_ = nc.gpsimd

            def do(ins, s=pool_own):
                ins.then_inc(s.sem, 1)
                s.n += 1
                pool.wait_ge(s.sem, s.n)

            def diagonal(buf, i, base):
                return g_.affine_select(out=buf[:, OFF[i]:OFF[i] + 128], in_=buf[:, OFF[i]:OFF[i] + 128],
                                        pattern=[[1, 128]], compare_op=ALU.is_ge, fill=0.0, base=base,
                                        channel_multiplier=-1)
            pool.wait_ge(loaded.sem, 48)
            for l in range(L):
                pool.wait_ge(*proj_out.nth(l, CK + 1))
                do(g_.tensor_scalar(F[:, BQ:BQ + 2, :], F[:, BQ:BQ + 2, :], 0.125, None, ALU.mult), scaled)
                do(g_.tensor_scalar(F[:, CK:CK + 2, :], F[:, CK:CK + 2, :], 0.125, None, ALU.mult), scaled)
                pool.wait_ge(*r_trc.nth(l, 0))
                for s in range(8):
                    if s >= 2:
                        pool.wait_ge(*r_bc.nth(l, s - 2))
                    md = (B1, B2)[s % 2]
                    id8 = K[0:8, C_ID:C_ID + 8]
                    if s < 4:
                        out = md[0:8, 0:1024].rearrange("p (h b d) -> p h b d", h=2, b=NSM)
                        for hh in range(2):
                            do(g_.tensor_tensor(out[:, hh], STM[:, s // 4, s % 4, 64 * hh:64 * hh + 64].unsqueeze(1)
                                                .to_broadcast([8, NSM, HD]),
                                                id8.unsqueeze(2).to_broadcast([8, NSM, HD]), ALU.mult),
                               r_md if hh else pool_own)
                    else:
                        out = md[0:8, 0:1024].rearrange("p (b d) -> p b d", b=NSM)
                        do(g_.tensor_tensor(out, STM[:, s // 4, s % 4, :].unsqueeze(1).to_broadcast([8, NSM, 128]),
                                            id8.unsqueeze(2).to_broadcast([8, NSM, 128]), ALU.mult), r_md)
                for v in range(8):
                    h, c, r0, E = v % 4, (v % 4) // 2, 64 * (v % 2), (B1, B2)[v % 2]
                    pool.wait_ge(*ex_done.nth(l, v))
                    for i in range(NT):
                        do(diagonal(E, i, 0))
                    if v >= 2:
                        pool.wait_ge(*num_done.nth(l, v - 2))
                    src = TM[:, T_CV + c, :, r0:r0 + 64] if v < 4 else TM[:, T_XX + c, :, r0:r0 + 64]
                    for i in range(NT):
                        last = OFF[i] + NPR - 128 * i - 1
                        do(g_.tensor_copy(U4[:, v % 2, i:i + 1], E[:, last:last + 1]))
                    for i in range(NT):
                        do(g_.tensor_scalar(VU[:, v % 2, i, :], src[:, i, :], U4[:, v % 2, i:i + 1], None, ALU.mult),
                           vu_ready if i == NT - 1 else pool_own)
                for h in range(4):
                    pool.wait_ge(*sp_done.nth(l, h))
                    for i in range(NT):
                        do(diagonal(B2, i, -1), sp_mask if i == NT - 1 else pool_own)
                    pool.wait_ge(*a_exp.nth(l, h))
                    for i in range(NT):
                        do(diagonal(B3, i, -1), a_mask if i == NT - 1 else pool_own)
                for i in range(NT):
                    pool.wait_ge(*ix_sum.nth(l, i))
                    blk = B1[:, 128 * i:128 * i + 128]
                    do(g_.affine_select(out=blk, in_=blk, pattern=[[-1, 128]], compare_op=ALU.is_ge, fill=NEG,
                                        base=0, channel_multiplier=1), ix_mask)


N_MID, N_END, N_ALL = 15, 17, 17
N_STORES_MID = [16 * (N_ALL * l + N_MID) for l in range(L)]
N_STORES_UPTO = [16 * N_ALL * (l + 1) for l in range(L)] + [16 * (N_ALL * L + 1)]


def _f(a, *order):
    return a


def kernel(**inputs):
    import numpy as np
    import concourse.bacc as bacc
    from concourse.bass_utils import run_bass_kernel_spmd

    g = {k: np.asarray(v) for k, v in inputs.items()}
    x = np.concatenate([g["x_prompt"][0], g["x_sample"][:, 0]], 0)
    arr = {}
    arr["x"] = x.T.reshape(KD, 128, TOK).transpose(1, 0, 2)
    arr["pages"] = g["page_table"].reshape(1, -1)
    a = {}
    offs = np.cumsum([0, 256, 128, 128, 256, 64, 4, 256, 256, 256, 256, 256, 256, 4, 4, 256, 256, 768, 4, 4096])
    (o_aq, o_ak, o_av, o_iq, o_ik, o_iw, o_bq, o_bk, o_bv, o_cq, o_ck, o_cv, o_ci, o_cf, o_co, o_dz, o_x, o_dt,
     o_g) = offs[:19]
    w = g["w_in"]
    r = np.arange
    zero = np.zeros((L, DM, 48), w.dtype)
    aq = np.concatenate([o_aq + 64 * h + r(64) for h in (0, 2, 1, 3)])
    cols = [w[:, :, aq], w[:, :, o_ak:o_ak + 128], w[:, :, o_av:o_av + 128], w[:, :, o_iq:o_iq + 256],
            w[:, :, o_ik:o_ik + 64], w[:, :, o_iw:o_iw + 4], w[:, :, o_ci:o_ci + 4], w[:, :, o_cf:o_cf + 4],
            w[:, :, o_dt:o_dt + 4], zero, w[:, :, o_bq:o_bq + 768], w[:, :, o_cq:o_cq + 768],
            w[:, :, o_co:o_co + 256], w[:, :, o_dz:o_dz + 256], w[:, :, o_x:o_x + 768]]
    wp = np.concatenate(cols, 2)

    def tiles(m, kk, nn):
        return m.reshape(L, kk, 128, nn, 128).transpose(0, 3, 2, 1, 4).reshape(L, nn, 128, kk * 128)
    arr["w_proj"] = tiles(wp, KD, NPROJ)
    wg = tiles(w[:, :, o_g:], KD, 32).reshape(L, 4, 8, 128, 1024).transpose(0, 2, 1, 3, 4)
    arr["w_gate"] = wg.reshape(L, 32, 128, 1024)
    ra = np.concatenate([64 * h + r(64) for h in (0, 2, 1, 3)])
    brs = [tiles(m, 2, KD) for m in (g["w_br_a"][:, ra], g["w_br_b"], g["w_br_c"], g["w_br_d"])]
    arr["w_br"] = np.concatenate(brs, 3)
    arr["w_out"] = tiles(g["w_out"], KD, KD)
    up = tiles(g["ffn_up"], KD, 2 * JF).reshape(L, 2, JF, 128, 1024).transpose(0, 2, 1, 3, 4)
    arr["w_up"] = up.reshape(L, 2 * JF, 128, 1024)
    dn = tiles(g["ffn_down"], JF, KD).reshape(L, KD, 128, JF, 128).transpose(0, 1, 3, 2, 4)
    arr["w_down"] = dn.reshape(L, JF, 8, 128, 128).transpose(0, 1, 3, 2, 4).reshape(L, JF, 128, SLOT)

    def fm(v, n):
        return v.reshape(L, n, 128).transpose(0, 2, 1)

    def bcast(v):
        return np.broadcast_to(v[:, None, :], (L, 128, v.shape[1]))

    def heads(v):
        return np.repeat(v.reshape(L, 2, 2), 64, 2).transpose(0, 2, 1)
    packs = [fm(g["norm_mix_pre"], 8), fm(g["norm_mix_post"], 8), fm(g["norm_ffn_pre"], 8),
             fm(g["norm_ffn_post"], 8), fm(g["c_norm"], 2), fm(g["d_norm"], 2),
             g["d_conv_w"].reshape(L, 4, 6, 128).transpose(0, 3, 2, 1).reshape(L, 128, 24), fm(g["d_conv_b"], 6),
             g["ffn_conv_w"].reshape(L, 3, 44, 128).transpose(0, 3, 2, 1).reshape(L, 128, 132),
             fm(g["ffn_conv_b"], 44), heads(g["d_D"]), bcast(g["c_b_i"]), bcast(g["c_b_f"]),
             bcast(g["d_dt_bias"]), bcast(g["d_A_log"]), heads(g["c_b_i"]), heads(g["c_b_f"]),
             heads(g["d_dt_bias"]), heads(g["d_A_log"])]
    vec = np.concatenate(packs, 2)
    assert vec.shape[2] == NV
    arr["vecs"] = vec.transpose(1, 0, 2)
    n_ = g["state_c_n"].reshape(L, 8, 2, 128).transpose(0, 3, 2, 1).reshape(L, 128, 16)
    m_ = np.repeat(g["state_c_m"].reshape(L, 8, 2, 2), 64, 3).transpose(0, 3, 2, 1).reshape(L, 128, 16)
    dc = g["state_d_conv"].reshape(L, 8, 3, 6, 128).transpose(0, 4, 3, 2, 1).reshape(L, 128, 144)
    fc = g["state_ffn_conv"].reshape(L, 8, 2, 44, 128).transpose(0, 4, 3, 2, 1).reshape(L, 128, 704)
    arr["states"] = np.concatenate([n_, m_, dc, fc], 2)
    arr["c_state"] = g["state_c_C"].reshape(L, 8, 2, 128, 64).transpose(0, 3, 2, 1, 4)
    arr["d_state"] = g["state_d_ssm"].reshape(L, 8, 2, 128, 128).transpose(0, 3, 2, 1, 4)
    ki = g["cache_a_kidx"].transpose(0, 1, 3, 2)
    ka = g["cache_a_k"].reshape(L, POOL, 128, 128).transpose(0, 1, 3, 2)
    kb = g["cache_b_k"].reshape(L, POOL, 128, 2, 128).transpose(3, 0, 1, 4, 2)
    arr["k_c"] = np.concatenate([ka, kb[0], kb[1], np.concatenate([ki, np.zeros_like(ki)], 2)], 3)
    arr["v_c"] = np.concatenate([g["cache_a_v"].reshape(L, POOL, 128, 128),
                                 g["cache_b_v"].reshape(L, POOL, 128, 256)], 3)

    k_ = np.zeros((128, NC_), np.float32)
    i = r(128)
    k_[:, C_ID:C_ID + 128] = np.eye(128)
    k_[:, C_ONE:C_ONE + 128] = 1
    k_[:, C_TRI:C_TRI + 128] = i[:, None] <= i[None]
    k_[:, C_NTRI:C_NTRI + 128] = -1.0 * (i[:, None] >= i[None])
    k_[:, C_NONE:C_NONE + 128] = -1
    swap = (i // 64) * 64 + (i % 64 + 32) % 64
    k_[swap, C_PERM + i] = 1
    k_[i % 64, C_DUP1 + i] = 1
    k_[(i % 64 + 32) % 64, C_DUP2 + i] = 1
    k_[:, C_BLK:C_BLK + 128] = (i[:, None] // 64) == (i[None] // 64)
    for h in range(4):
        k_[[h, 32 + h], C_SEL + 128 * h:C_SEL + 128 * h + 128] = 1
        k_[h, C_SELP + 128 * (h // 2) + 64 * (h % 2):C_SELP + 128 * (h // 2) + 64 * (h % 2) + 64] = 1
        for what in range(3):
            col = C_SELS + 128 * (2 * what + h // 2) + 64 * (h % 2)
            k_[64 + 4 * (what + 1) + h, col:col + 64] = 1
        k_[64 + h, C_AIW + h:C_AIW + 32:4] = 1
    for b in range(8):
        k_[4 * b:4 * b + 4, C_EM + b] = 1
        k_[b, C_EB + 4 * b:C_EB + 4 * b + 4] = 1
    k_[:, C_SGN:C_SGN + 4] = -1
    k_[:, C_SGN + 4:C_SGN + 8] = 1
    k_[:, C_EPS] = EPS
    inv = (10000.0 ** (-r(32) / 32)).astype(np.float32)
    pos = np.concatenate([r(NPR), np.full(NSM, PAST)]).astype(np.float32)
    ang = (inv[i % 32][:, None] * pos[None]).astype(np.float32)
    k_[:, C_COS:C_COS + TOK] = np.cos(ang)
    k_[:, C_SIN:C_SIN + TOK] = np.sin(ang) * np.where(i % 64 < 32, -1.0, 1.0)[:, None]
    arr["consts"] = k_

    nc = bacc.Bacc("TRN2", target_bir_lowering=False, num_devices=1)
    dt_of = mybir.dt.from_np

    def dram(name):
        arr[name] = np.ascontiguousarray(arr[name])
        return nc.dram_tensor(name, arr[name].shape, dt_of(arr[name].dtype), kind="ExternalInput").ap()
    shapes = {"y_o": (128, KD, TOK), "ka_o": (L, 128, TOK), "va_o": (L, 128, TOK), "ki_o": (L, 64, TOK),
              "kb_o": (L, 128, 2, TOK), "vb_o": (L, 128, 2, TOK), "pc_o": (L, 128, 128), "pn_o": (L, 128, 2),
              "pm_o": (L, 4, 1), "dconv_o": (L, 128, 6, 11), "dconv_s_o": (L, 128, 144), "pssm_o": (L, 128, 256),
              "fconv_o": (L, 128, 44, 10), "fconv_s_o": (L, 128, 704), "sc_o": (L, 128, 2, 8, 64),
              "sn_o": (L, 128, 16), "sm_o": (L, 128, 16), "sssm_o": (L, 128, 2, 8, 128)}
    outs = {n: nc.dram_tensor(n, s, mybir.dt.float32, kind="ExternalOutput").ap() for n, s in shapes.items()}
    trunk_kernel(nc, *[dram(n) for n in ("x", "pages", "consts", "vecs", "states", "c_state", "d_state",
                                         "k_c", "v_c", "w_proj", "w_gate", "w_br", "w_out", "w_up", "w_down")],
                 *outs.values())
    res = run_bass_kernel_spmd(nc, [arr], core_ids=[0]).results[0]
    o = {n: np.asarray(res[n]) for n in shapes}

    y = o["y_o"].transpose(2, 1, 0).reshape(TOK, DM)

    def rows(t, c):
        return t.reshape(L, -1, c, TOK).transpose(0, 3, 2, 1).reshape(L, TOK, -1)
    both = {}
    for name, t, c, tail in (("a_k", o["ka_o"], 1, (2, 64)), ("a_v", o["va_o"], 1, (2, 64)),
                             ("kidx", o["ki_o"], 1, (64,)), ("b_k", o["kb_o"], 2, (4, 64)),
                             ("b_v", o["vb_o"], 2, (4, 64))):
        t = rows(t, c)
        both["p_" + name] = t[:, None, :NPR].reshape((L, 1, NPR) + tail)
        both["s_" + name] = t[:, NPR:, None].reshape((L, NSM, 1) + tail)
    p_c = o["pc_o"].reshape(L, 2, 64, 2, 64).transpose(0, 3, 1, 2, 4).reshape(L, 1, 4, 64, 64)
    p_n = o["pn_o"].reshape(L, 2, 64, 2).transpose(0, 3, 1, 2).reshape(L, 1, 4, 64)
    p_m = o["pm_o"].reshape(L, 1, 4)
    dco = o["dconv_o"]
    p_dc = dco[..., :3].transpose(0, 3, 2, 1).reshape(L, 1, 3, 768)
    s_old = o["dconv_s_o"].reshape(L, 128, 6, 3, 8)[:, :, :, 1:]
    s_dc = np.concatenate([s_old, dco[:, :, :, None, 3:]], 3).transpose(0, 4, 3, 2, 1).reshape(L, 8, 3, 768)
    p_h = o["pssm_o"].reshape(L, 2, 64, 2, 128).transpose(0, 3, 1, 2, 4).reshape(L, 1, 4, 64, 128)
    fco = o["fconv_o"]
    p_fc = fco[..., :2].transpose(0, 3, 2, 1).reshape(L, 1, 2, 2 * DFF)
    f_old = o["fconv_s_o"].reshape(L, 128, 44, 2, 8)[:, :, :, 1:]
    s_fc = np.concatenate([f_old, fco[:, :, :, None, 2:]], 3).transpose(0, 4, 3, 2, 1).reshape(L, 8, 2, 2 * DFF)
    s_c = o["sc_o"].reshape(L, 2, 64, 2, 8, 64).transpose(0, 4, 3, 1, 2, 5).reshape(L, 8, 4, 64, 64)
    s_n = o["sn_o"].reshape(L, 2, 64, 2, 8).transpose(0, 4, 3, 1, 2).reshape(L, 8, 4, 64)
    s_m = o["sm_o"].reshape(L, 2, 64, 2, 8)[:, :, 0].transpose(0, 3, 2, 1).reshape(L, 8, 4)
    s_h = o["sssm_o"].reshape(L, 2, 64, 2, 8, 128).transpose(0, 4, 3, 1, 2, 5).reshape(L, 8, 4, 64, 128)
    out = (y[None, :NPR], y[NPR:, None], both["p_a_k"], both["p_a_v"], both["p_kidx"], both["p_b_k"],
           both["p_b_v"], p_c, p_n, p_m, p_dc, p_h, p_fc, both["s_a_k"], both["s_a_v"], both["s_kidx"],
           both["s_b_k"], both["s_b_v"], s_c, s_n, s_m, s_dc, s_h, s_fc)
    return tuple(np.ascontiguousarray(t) for t in out)
```

```python
import concourse.bass as bass
from concourse import mybir
from contextlib import ExitStack

L = 2
NPR = 512
NSM = 8
TOK = NPR + NSM
HALF = TOK // 2
DM = 1024
KD = DM // 128
DFF = 2816
JF = DFF // 128
NT = NPR // 128
PAGES = 8
PAST = 1024
POOL = 80
HD = 64
TOPK_P = 128
TOPK_S = 256
RING = 4
SLOT = 8 * 128
NEG = -1e30
TAKEN = -3e38
EPS = 1e-6

AQ, AK, AV, IQ, SM, BQ, BK, BV, CQ, CK, CV, CO, DZ, XX, XB, XC = (
    0, 2, 3, 4, 6, 7, 9, 11, 13, 15, 17, 19, 21, 23, 25, 27)
NPROJ = 29
IKD = 29
NF = 31
MERGED = 23
T_SM, T_AV, T_BV, T_CK, T_CV, T_XX, T_XB = -1, 0, 1, 3, 5, 7, 9
TO_TM = [(SM, T_SM), (AV, T_AV), (BV, T_BV), (BV + 1, T_BV + 1), (CK, T_CK), (CK + 1, T_CK + 1),
         (CV, T_CV), (CV + 1, T_CV + 1), (XX, T_XX), (XX + 1, T_XX + 1), (XB, T_XB), (XB + 1, T_XB + 1)]
V_NPRE, V_NPOST, V_FPRE, V_FPOST, V_CN, V_DN, V_DCW, V_DCB = 0, 8, 16, 24, 32, 34, 36, 60
V_FCW, V_FCB, V_D, V_BI, V_BFD, V_AL, V_SBI, V_SBF, V_SBD, V_SAL = 66, 198, 242, 244, 248, 256, 260, 262, 264, 266
NV = 268
S_N, S_M, S_DC, S_FC = 0, 16, 32, 176
NST = 880
C_ID, C_ONE, C_TRI, C_NTRI, C_NONE, C_PERM, C_DUP1, C_DUP2, C_BLK = (128 * i for i in range(9))
C_SEL = 1152
C_SELP = C_SEL + 512
C_SELS = C_SEL
C_AIW = C_SELP + 256
C_EM = C_AIW + 32
C_EB = C_EM + 8
C_SGN = C_EB + 32
C_EPS = C_SGN + 8
C_COS = C_EPS + 1
C_SIN = C_COS + TOK
NC_ = C_SIN + TOK
OFF = [0, 512, 896, 1152]
TRI_W = 1280
K_REC, V_REC = 512, 384
UPS = PAGES // 2
NU = NSM * UPS
NSPLIT = NPROJ + 32 + 8 + 44 + 22
S_OUT, S_UP, S_DOWN = NPROJ + 32, NPROJ + 40, NPROJ + 84
HI_OF = [15, 16, 17, 18, 19, 20, 9, 10]
K_ORDER = [16, 17, 18, 19, 20] + list(range(16)) + [21]
DOWN_END = [(JF * d + JF - 1) // 8 for d in range(KD)]
CUT = 12
BY_POOL = NPROJ - CUT - 2


class Signal:

    def __init__(self, sem, per):
        self.sem, self.per, self.n = sem, per, 0

    def nth(self, l, k):
        return self.sem, l * self.per + k + 1

    def all(self, l):
        return self.sem, (l + 1) * self.per


def trunk_kernel(nc, x_in, pages, consts, vecs, states, c_state, d_state, k_c, v_c,
                 w_proj, w_gate, w_br, w_out, w_up, w_down,
                 y_out, ka_o, va_o, ki_o, kb_o, vb_o, pc_o, pn_o, pm_o, dconv_o, dconv_s_o, pssm_o,
                 fconv_o, fconv_s_o, sc_o, sn_o, sm_o, sssm_o):
    f32 = mybir.dt.float32
    f32r = mybir.dt.float32r
    ALU = mybir.AluOpType
    ACT = mybir.ActivationFunctionType
    AX = mybir.AxisListType.X
    ctx = ExitStack()
    with ctx:
        def sb(name, shape, dt=f32):
            return ctx.enter_context(nc.sbuf_tensor(name, shape, dt))

        signals = []

        def sig(name, per):
            s = Signal(ctx.enter_context(nc.semaphore(name)), per)
            signals.append((name, s))
            return s

        X = sb("X", [128, KD, TOK])
        XH = sb("XH", [128, KD, TOK], f32r)
        RB = sb("RB", [128, TOK])
        with nc.sbuf_tensor("FR", [128, NF, TOK], f32r) as FR:
            pass
        F = sb("F", [128, NF, TOK])
        with nc.sbuf_tensor("TM", [128, 11, NT, 128], f32) as TM:
            pass
        WH = sb("WH", [128, 2, SLOT], f32r)
        WL = sb("WL", [128, 2, SLOT], f32r)
        T = sb("T", [128, 11 * NT * 128 - 4 * SLOT])
        R = sb("R", [128, RING, SLOT])
        S = sb("S", [128, 5, TOK])
        with nc.sbuf_tensor("B1", [128, TRI_W], f32) as B1, nc.sbuf_tensor("B2", [128, TRI_W], f32) as B2, \
                nc.sbuf_tensor("B3", [128, TRI_W], f32) as B3:
            pass
        XL = sb("XL", [128, KD, TOK], f32r)
        K = sb("K", [128, NC_])
        V = sb("V", [128, L, NV])
        ST = sb("ST", [128, NST])
        CS = sb("CS", [128, 2, NSM, HD])
        HS = sb("HS", [128, 2, NSM, 128])
        PT = sb("PT", [1, NSM * PAGES], mybir.dt.int32)
        DO = sb("DO", [128, 6, 11])
        FO = sb("FO", [128, 2 * JF, 10])
        RT = sb("RT", [128, NT, 96])
        SMT = sb("SMT", [128, NT, 64])
        NEGA = sb("NEGA", [128, 8])
        SROW = sb("SROW", [128, 512])
        MR = sb("MR", [4, 512])
        ML = sb("ML", [4, 1])
        U4 = sb("U4", [128, 2, NT])
        VU = S[:, 4, 0:512].rearrange("p (v t d) -> p v t d", v=2, t=NT)
        PST = sb("PST", [128, 386])
        M8 = sb("M8", [128, 8])
        MX = sb("MX", [128, 16])
        QI = sb("QI", [64, NSM, 32])
        QA = sb("QA", [128, NSM, 32])
        QB = sb("QB", [128, 2, NSM, 32])
        IWW = sb("IWW", [32, 8])
        DG = sb("DG", [64, 32])
        PA = QB[:, :, :, :].rearrange("p c b h -> p (c b h)")
        SF = S[:, 0:2, :].rearrange("p a t -> p (a t)")
        STM = S[0:8, 2:4, 0:512].rearrange("p a (c d) -> p a c d", d=128)
        SS = sb("SS", [128, 24, 16])
        OS = sb("OS", [128, 32])
        PS = ctx.enter_context(nc.psum_tensor("PS", [128, 8, 512], f32))

        def kc(col, n=128, p0=0, p1=128):
            return K[p0:p1, col:col + n]

        def pair(b):
            return PS[:, b:b + 2, 0:HALF]

        def halves(ap):
            return ap.rearrange("p (a t) -> p a t", a=2)

        def bblock(i, first=0):
            bank, col = ((4, 0), (5, 0), (6, 0), (6, 256))[i]
            return PS[:, bank, col + first:col + NPR - 128 * i]

        PTR = (B3[:, 512:1024], S[:, 4, 0:512])
        ident = kc(C_ID)
        eps = K[:, C_EPS:C_EPS + 1]
        one = K[:, C_ONE:C_ONE + 1]

        loaded = sig("inputs_loaded", 0)
        pt_loaded = sig("page_table_loaded", 0)
        st_loaded = sig("states_loaded", 3 * 16)
        slot_full = [sig(f"slot{i}_full", 0) for i in range(RING)]
        tile_used = sig("tile_used", NPROJ + 2 * NU + 40 + 8 + 44 + 22)
        xt_ready = sig("normalised_ready", 16)
        xh_ready = sig("leading_part_ready", 16)
        xl_first = sig("first_chunks_rest_part_ready_again", 4)
        xl_again = sig("rest_part_ready_again", 4)
        w_hi = sig("weight_leading_part_ready", NSPLIT)
        w_lo = sig("weight_rest_part_ready", NSPLIT - BY_POOL)
        w_lo_p = sig("weight_rest_part_ready_by_pool", BY_POOL)
        mg_hi = sig("merged_leading_part_ready", KD)
        mg_lo = sig("merged_rest_part_ready", KD)
        hd_hi = sig("hidden_leading_part_ready", 2 * KD)
        hd_lo = sig("hidden_rest_part_ready", 2 * KD)
        sq_ready = sig("squares_ready", 32)
        sq_added = sig("squares_added", 16)
        sq_summed = sig("squares_summed_by_pe", 16)
        sum_ready = sig("sum_of_squares_ready", 2)
        root_ready = sig("root_ready", 4)
        norm_out = sig("norm_applied", 32)
        proj_out = sig("projection_copied", NPROJ)
        scaled = sig("queries_keys_scaled", 2)
        perm_done = sig("rotated_halves_ready", 7)
        perm_used = sig("rotated_halves_used", 7)
        rope_done = sig("rope_done", 6)
        cv_init = sig("conv_started", 6)
        cv_done = sig("conv_summed", 6)
        cv_saved = sig("conv_tail_saved", 6)
        xbc_ready = sig("conv_activated", 6)
        tm_done = sig("transposed", 12)
        tm_ready = sig("token_major_ready", 12)
        sm_v = sig("gate_inputs_ready", 1)
        sm_ln = sig("gate_logs_ready", 2)
        sm_cin = sig("log_decays_ready", 1)
        sm_cum = sig("log_decays_summed", 1)
        sm_rt = sig("row_terms_ready", 1)
        sm_ng = sig("negated_column_terms_ready", 1)
        sm_tr = sig("row_terms_transposed", 1)
        sm_row = sig("rows_copied", 1)
        sm_g = sig("running_max_ready", 1)
        sm_em = sig("exp_m_ready", 1)
        bc_done = sig("row_broadcast", 8)
        ex_arg = sig("decay_exponent_ready", 8)
        ex_done = sig("decay_exp_done", 8)
        st_block = sig("key_query_block_done", 32)
        w_ready = sig("weighted_block_ready", 32)
        vu_ready = sig("state_weights_ready", 8)
        num_done = sig("numerator_done", 8)
        c_em = sig("c_floor_broadcast", 2)
        c_abs = sig("c_denominator_abs", 2)
        c_h = sig("c_h_ready", 2)
        c_sq = sig("c_squares_ready", 2)
        c_sum = sig("c_sum_ready", 2)
        c_root = sig("c_root_ready", 2)
        c_sg = sig("c_output_gate_ready", 2)
        c_out = sig("c_output_ready", 2)
        d_sl = sig("d_silu_ready", 2)
        d_y = sig("d_y_ready", 2)
        d_sq = sig("d_squares_ready", 2)
        d_sum = sig("d_sum_ready", 1)
        d_root = sig("d_root_ready", 1)
        d_out = sig("d_output_ready", 2)
        pst_done = sig("prompt_state_copied", 1)
        z_done = sig("b_logits_ready", 4)
        z_ln = sig("b_log_term_ready", 4)
        sp_done = sig("b_softplus_ready", 4)
        sp_mask = sig("b_softplus_masked", 4)
        ac_done = sig("b_log_weights_ready", 4)
        a_exp = sig("b_weights_exp", 4)
        a_mask = sig("b_weights_masked", 4)
        pv_done = sig("b_values_summed", 4)
        b_out = sig("b_output_copied", 2)
        ix_done = sig("index_products_ready", 4 * NT)
        ix_relu = sig("index_relu_ready", 4 * NT)
        ix_sum = sig("index_scores_ready", NT)
        ix_mask = sig("index_scores_masked", NT)
        bias_ready = sig("selection_bias_ready", NT)
        at_qk = sig("a_logits_ready", 16)
        at_max = sig("a_max_ready", 16)
        at_exp = sig("a_exp_ready", 16)
        at_norm = sig("a_probs_ready", 16)
        at_tr = sig("a_probs_transposed", 16)
        at_trc = sig("a_probs_copied", 16)
        at_pv = sig("a_values_summed", 16)
        a_out = sig("a_output_copied", NT)
        q_pad = sig("sample_queries_placed", 1)
        sx_done = sig("sample_index_products", 2)
        sx_iw = sig("sample_index_weights", 1)
        sx_score = sig("sample_scores_ready", 1)
        sx_sel = sig("sample_selection_ready", 1)
        sx_bc = sig("sample_selection_broadcast", 1)
        sb_zc = sig("sample_b_logits_copied", 1)
        sb_zt = sig("sample_b_logits_transposed", 1)
        sb_ln = sig("sample_b_log_term", 1)
        sb_sp = sig("sample_b_softplus", 1)
        sb_ac = sig("sample_b_log_weights", 1)
        sb_arg = sig("sample_b_exponent", 1)
        sb_a = sig("sample_b_weights", 1)
        sa_max = sig("sample_a_max", 1)
        sa_exp = sig("sample_a_exp", 1)
        sa_p = sig("sample_a_probs", 1)
        sa_tr = sig("sample_a_probs_transposed", 1)
        sa_trc = sig("sample_a_probs_copied", 1)
        sa_own = sig("sample_a_own_value", 1)
        sa_out = sig("sample_a_output", 1)
        r_sel = sig("sample_gates_broadcast", 1)
        r_v = sig("sample_gate_inputs", 1)
        r_ln = sig("sample_gate_logs", 1)
        r_arg = sig("sample_exponents", 1)
        r_exp = sig("sample_exps", 1)
        r_dot = sig("sample_dots_ready", 1)
        r_tr = sig("sample_rows_transposed", 1)
        r_trc = sig("sample_rows_copied", 1)
        r_md = sig("sample_diagonals_ready", 8)
        r_bc = sig("sample_rows_broadcast", 8)
        r_bcu = sig("sample_rows_used", 8)
        r_out = sig("sample_states_updated", 1)
        r_prod = sig("sample_products_ready", 1)
        g_sig = sig("gate_sigmoid", 32)
        br_done = sig("branch_done", 24)
        br_used = sig("branch_merged", 32)
        up_evac = sig("up_copied", 2 * JF)
        fcv = sig("ffn_conv_done", 2 * JF)
        gl_done = sig("gelu_done", JF)
        h_ready = sig("hidden_ready", JF)
        dn_done = sig("down_chunk_done", 8)
        stored = sig("outputs_stored", 0)
        act_own = sig("act_own", 0)
        dve_own = sig("dve_own", 0)
        pool_own = sig("pool_own", 0)
        tiles_per = tile_used.per
        FIRST = {"K": CUT, "V": NPROJ + NU, "gate": NPROJ + 2 * NU, "out": NPROJ + 2 * NU + 40,
                 "up": NPROJ + 2 * NU + 48, "down": NPROJ + 2 * NU + 92}
        full_at, at = [], [0] * RING
        for l in range(L):
            for n in range(tiles_per):
                cache = CUT <= n < CUT + NU or FIRST["V"] <= n < FIRST["gate"]
                at[(l * tiles_per + n) % RING] += 32 if cache else 16
                full_at.append(at[(l * tiles_per + n) % RING])

        def slot(l, n):
            return R[:, (l * tiles_per + n) % RING, :]

        def proj(c):
            return c if c < CUT else c + NU

        def tile_done(l, n):
            return tile_used.nth(l, n)

        SPLIT = ([proj(c) for c in range(NPROJ)] + [FIRST["gate"] + 5 * (q // 4) + q % 4 for q in range(32)]
                 + [FIRST["out"] + d for d in range(KD)] + [FIRST["up"] + j for j in range(2 * JF)]
                 + [FIRST["down"] + t for t in range(JF)])
        split_no = {n: m for m, n in enumerate(SPLIT)}

        def half(l, m):
            return (l * NSPLIT + m) % 2

        def lo_ready(l, m):
            if CUT + 2 <= m < NPROJ:
                return w_lo_p.nth(l, m - CUT - 2)
            return w_lo.nth(l, m if m < NPROJ else m - BY_POOL)

        def full(l, n):
            m = l * tiles_per + n
            return slot_full[m % RING].sem, full_at[m]

        def by_act(u):
            return u >= RING and u % 2 == 1

        def cached(eng, l, n, u, rec, src):
            eng.wait_ge(tile_used.sem, l * tiles_per + n - RING + 1)
            for j in range(2):
                pg = eng.value_load(PT[0:1, 2 * u + j:2 * u + j + 1], min_val=0, max_val=POOL - 1)
                eng.dma_start(slot(l, n)[:, rec * j:rec * (j + 1)],
                              src[l, bass.ds(pg, 1)].rearrange("o p c -> (o p) c")).then_inc(full(l, n)[0], 16)

        block = ctx.enter_context(nc.Block())

        @block.sync
        def _(sp):
            sp.dma_start(PT[:, :], pages).then_inc(pt_loaded.sem, 16)
            for dst, src in ((X[:, :, :], x_in), (K[:, :], consts), (V[:, :, :], vecs)):
                sp.dma_start(dst, src).then_inc(loaded.sem, 16)
            sp.wait_ge(pt_loaded.sem, 16)

            def room(l, n):
                m = l * tiles_per + n
                if m >= RING:
                    sp.wait_ge(tile_used.sem, m - RING + 1)

            def tile(l, n, src, width):
                room(l, n)
                sp.dma_start(slot(l, n)[:, 0:width], src).then_inc(full(l, n)[0], 16)

            for l in range(L):
                for c in range(CUT):
                    tile(l, proj(c), w_proj[l, c], 1024)
                    if c == RING - 1:
                        if l:
                            sp.wait_ge(stored.sem, N_STORES_UPTO[l - 1])
                        sp.dma_start(ST[:, :], states[l]).then_inc(st_loaded.sem, 16)
                        sp.dma_start(CS[:, :, :, :], c_state[l]).then_inc(st_loaded.sem, 16)
                        sp.dma_start(HS[:, :, :, :], d_state[l]).then_inc(st_loaded.sem, 16)
                for u in range(NU):
                    if not by_act(u):
                        cached(sp, l, FIRST["K"] + u, u, K_REC, k_c)
                for c in range(CUT, NPROJ):
                    tile(l, proj(c), w_proj[l, c], 1024)
                for u in range(NU):
                    cached(sp, l, FIRST["V"] + u, u, V_REC, v_c)
                for d in range(KD):
                    for br in range(4):
                        tile(l, FIRST["gate"] + 5 * d + br, w_gate[l, 4 * d + br], 1024)
                    tile(l, FIRST["gate"] + 5 * d + 4, w_br[l, d], 1024)
                for d in range(KD):
                    tile(l, FIRST["out"] + d, w_out[l, d], 1024)
                for j in range(2 * JF):
                    tile(l, FIRST["up"] + j, w_up[l, j], 1024)
                for j in range(JF):
                    tile(l, FIRST["down"] + j, w_down[l, j], SLOT)
            sp.wait_ge(norm_out.sem, L * norm_out.per)
            sp.dma_start(y_out, X[:, :, :]).then_inc(stored.sem, 16)
            sp.wait_ge(stored.sem, N_STORES_UPTO[L])

        @block.tensor
        def _(pe):
            pe.wait_ge(loaded.sem, 48)
            mm = nc.tensor.matmul

            def block_split(w, k, hi, lo, bank, first, last):
                for p, x in ((WH, hi), (WH, lo), (WL, hi)):
                    for a in range(2):
                        i = mm(PS[:, bank + a, 0:HALF], p[:, w, k * 128:(k + 1) * 128],
                               x[:, a * HALF:(a + 1) * HALF], start=first and p is WH and x is hi,
                               stop=last and p is WL)
                return i

            def dense_split(l, n, bank, chunk, before=lambda k: None):
                m = split_no[n]
                pe.wait_ge(*w_hi.nth(l, m))
                pe.wait_ge(*lo_ready(l, m))
                for k in range(KD):
                    before(k)
                    hi, lo = chunk(k)
                    i = block_split(half(l, m), k, hi, lo, bank, k == 0, k == KD - 1)
                i.then_inc(tile_used.sem, 1)

            def x_parts(k):
                return XH[:, k, :], XL[:, k, :]

            def normed(l, j):
                return lambda k: pe.wait_ge(*norm_out.nth(l, 8 * j + k))

            def norm_sum(l, j):
                pe.wait_ge(*sq_added.nth(l, 8 * (j // 2) + 7))
                for a in range(2):
                    i = mm(PS[:, 4 + a, 0:HALF], kc(C_ONE), S[:, 2, a * HALF:(a + 1) * HALF], start=True, stop=True)
                i.then_inc(sum_ready.sem, 1)

            def norm_sum_chunks(l, j):
                for k in range(KD):
                    pe.wait_ge(*sq_ready.nth(l, 8 * j + k))
                    for a in range(2):
                        i = mm(PS[:, 4 + a, 0:HALF], kc(C_ONE), S[:, k % 2, a * HALF:(a + 1) * HALF],
                               start=k == 0, stop=k == KD - 1)
                    i.then_inc(sq_summed.sem, 1)

            def finish(i, s):
                i.then_inc(s.sem, 1)

            def values(l, t, h):
                q0 = 64 * (h // 2)
                if t and h == 0:
                    pe.wait_ge(*a_out.nth(l, t - 1))
                pe.wait_ge(*at_trc.nth(l, 4 * t + h))
                for j in range(t + 1):
                    ins = mm(PS[q0:q0 + 64, 2, 128 * (h % 2):128 * (h % 2) + 128], TM[:, T_AV, j, q0:q0 + 64],
                             PTR[h % 2][:, 128 * j:128 * j + 128], start=j == 0, stop=j == t)
                finish(ins, at_pv)

            def cached_values(l, b):
                for u in range(UPS * b, UPS * b + UPS):
                    t = u - UPS * b
                    n = FIRST["V"] + u
                    pe.wait_ge(*full(l, n))
                    for jj in range(2):
                        j, v0 = 2 * t + jj, V_REC * jj
                        mm(PS[:, 3, 4 * b:4 * b + 4], slot(l, n)[:, v0:v0 + 128],
                           PA[:, 32 * j + 4 * b:32 * j + 4 * b + 4], start=j == 0, stop=j == 7,
                           skip_group_check=True)
                        for c in range(2):
                            o = 32 + 16 * c + 2 * b
                            ins = mm(PS[:, 3, o:o + 2], slot(l, n)[:, v0 + 128 + 128 * c:v0 + 256 + 128 * c],
                                     PA[:, 256 + 32 * j + 4 * b + 2 * c:256 + 32 * j + 4 * b + 2 * c + 2],
                                     start=False, stop=j == 7, skip_group_check=True)
                    ins.then_inc(tile_used.sem, 1)

            for l in range(L):
                norm_sum_chunks(l, 0)
                def project(c):
                    if c >= 2:
                        pe.wait_ge(*proj_out.nth(l, c - 2))
                    dense_split(l, proj(c), 2 * (c % 2), x_parts, *[normed(l, 0)] * (c == 0))

                def partner(i):
                    c = [AQ, AQ + 1, AK, IQ, IQ + 1, SM, SM][i]
                    pe.wait_ge(*proj_out.nth(l, c))
                    if i >= 2:
                        pe.wait_ge(*perm_used.nth(l, i - 2))
                    if i < 2:
                        pe.wait_ge(*root_ready.nth(l, 0))
                    for a in range(2):
                        if i < 5:
                            ins = mm(PS[:, 4 + 2 * (i % 2) + a, 0:HALF], kc(C_PERM),
                                     F[:, c, a * HALF:(a + 1) * HALF], start=True, stop=True)
                        else:
                            ins = mm(PS[:, 4 + 2 * (i % 2) + a, 0:HALF], kc((C_DUP1, C_DUP2)[i - 5], 128, 0, 64),
                                     F[0:64, c, a * HALF:(a + 1) * HALF], start=True, stop=True)
                    finish(ins, perm_done)
                for c in range(CUT):
                    project(c)
                    if c >= CUT - 4:
                        for i in range(2 * (c - CUT + 4), min(7, 2 * (c - CUT + 4) + 2)):
                            partner(i)
                pe.wait_ge(*q_pad.nth(l, 0))
                for u in range(NU):
                    b, t = divmod(u, UPS)
                    n = FIRST["K"] + u
                    pe.wait_ge(*full(l, n))
                    rec = slot(l, n).rearrange("p (j k c) -> p k j c", j=2, k=4)
                    bank, col = 4 + t // 2, 256 * (t % 2)
                    st = b == 0 and t % 2 == 0
                    end = b == NSM - 1
                    mm(PS[0:32, bank, col:col + 256], QI[:, b, :], rec[0:64, 3], start=st, stop=end,
                       skip_group_check=True)
                    mm(PS[32:64, bank, col:col + 256], QA[:, b, :], rec[:, 0], start=st, stop=end,
                       skip_group_check=True)
                    if t == 0:
                        mm(PS[0:32, 6, 0:1], QI[:, b, :], F[0:64, IKD, NPR + b:NPR + b + 1], start=b == 0,
                           stop=end, skip_group_check=True)
                        mm(PS[32:64, 6, 0:1], QA[:, b, :], F[:, AK, NPR + b:NPR + b + 1], start=b == 0,
                           stop=end, skip_group_check=True)
                    for c in range(2):
                        ins = mm(PS[64:96, bank, col:col + 256], QB[:, c, b, :], rec[:, 1 + c],
                                 start=st and c == 0, stop=end and c == 1, skip_group_check=True)
                    ins.then_inc(tile_used.sem, 1)
                finish(mm(PS[0:32, 7, 0:8], K[64:68, C_AIW:C_AIW + 32], F[64:68, SM, NPR:TOK],
                          start=True, stop=True), sx_done)
                for c in range(CUT, NPROJ):
                    project(c)
                    if c == CUT:
                        pe.wait_ge(*sb_zc.nth(l, 0))
                        pe.wait_ge(*sx_iw.nth(l, 0))
                        mm(PS[0:8, 4, :], IWW[:, :], SF[0:32, 0:512], start=True, stop=True)
                        mm(PS[0:8, 5, :], IWW[:, :], SF[0:32, 512:1024], start=True, stop=True)
                        finish(mm(PS[0:8, 7, 0:1], IWW[:, :], SF[0:32, 1024:1025], start=True, stop=True), sx_done)
                    elif c == CUT + 1:
                        for j in range(PAGES):
                            ins = nc.tensor.transpose(PS[:, 6, 32 * j:32 * j + 32], SF[64:96, 128 * j:128 * j + 128],
                                                      K[64:96, C_ID + 64:C_ID + 96])
                        finish(ins, sb_zt)
                    elif c == CUT + 4:
                        pe.wait_ge(*sb_sp.nth(l, 0))
                        mm(PS[:, 7, 0:256], kc(C_NTRI), S[:, 2, 0:256], start=True, stop=False)
                        for k in range(1, PAGES):
                            ins = mm(PS[:, 7, 0:256 - 32 * k], kc(C_NONE), S[:, 2, 32 * k:256], start=False,
                                     stop=k == 7)
                        finish(ins, sb_ac)
                    elif c == NPROJ - 3:
                        pe.wait_ge(*sx_sel.nth(l, 0))
                        for bank, lo, hi in ((4, 0, 512), (5, 512, 1024), (7, 1024, 1025)):
                            ins = mm(PS[32:64, bank, 0:hi - lo], K[0:8, C_EB:C_EB + 32], T[0:8, lo:hi],
                                     start=True, stop=True)
                        finish(ins, sx_bc)
                pe.wait_ge(*sa_p.nth(l, 0))
                for j in range(PAGES):
                    nc.tensor.transpose(PS[:, 4, 32 * j:32 * j + 32], SF[32:64, 128 * j:128 * j + 128],
                                        K[32:64, C_ID + 32:C_ID + 64])
                finish(mm(PS[:, 7, 0:32], K[32:64, C_ONE:C_ONE + 128], DG[32:64, :], start=True, stop=True), sa_tr)
                pe.wait_ge(*sa_trc.nth(l, 0))
                pe.wait_ge(*sa_own.nth(l, 0))
                pe.wait_ge(*rope_done.nth(l, 5))
                for i, (src, dst) in enumerate(TO_TM):
                    if i >= 4:
                        pe.wait_ge(*tm_ready.nth(l, i - 4))
                    pe.wait_ge(*(xbc_ready.nth(l, src - XX) if src >= XX else proj_out.nth(l, src)))
                    if src == CK:
                        pe.wait_ge(*scaled.nth(l, 1))
                    for t in range(NT):
                        ins = nc.tensor.transpose(PS[:, 4 + i % 4, t * 128:(t + 1) * 128],
                                                  F[:, src, t * 128:(t + 1) * 128], ident)
                    finish(ins, tm_done)
                pe.wait_ge(*sm_cin.nth(l, 0))
                pe.wait_ge(*tm_ready.nth(l, 11))
                CIN = SMT[:, :, 16:24]
                mm(PS[:, 4, 0:32], kc(C_TRI), CIN, start=True, stop=False)
                for k in range(1, NT):
                    ins = mm(PS[:, 4, 8 * k:32], kc(C_ONE), SMT[:, 0:NT - k, 16:24], start=False, stop=k == NT - 1)
                finish(ins, sm_cum)
                pe.wait_ge(*sm_rt.nth(l, 0))
                for t in range(NT):
                    ins = nc.tensor.transpose(PS[0:96, 5, t * 128:(t + 1) * 128], RT[:, t, :], ident)
                finish(ins, sm_tr)
                pe.wait_ge(*xbc_ready.nth(l, 5))
                pe.wait_ge(*q_pad.nth(l, 0))
                for i in range(6):
                    ins = mm(PS[:, 6, 8 * i:8 * i + 8], K[64:80, C_SELS + 128 * i:C_SELS + 128 * i + 128],
                             F[64:80, SM, NPR:TOK], start=True, stop=True)
                finish(ins, r_sel)
                pe.wait_ge(*r_prod.nth(l, 0))
                mm(PS[:, 7, 0:32], kc(C_BLK), SS[:, 0:2, :], start=True, stop=True)
                finish(mm(PS[:, 7, 32:48], kc(C_ONE), SS[:, 2, :], start=True, stop=True), r_dot)
                for i, c in enumerate([CQ, CQ + 1, CK, CK + 1, XC, XC + 1, XB, XB + 1]):
                    ins = nc.tensor.transpose(PS[0:8, i // 4, (i % 4) * 128:(i % 4) * 128 + 128],
                                              F[:, c, NPR:TOK], ident)
                finish(ins, r_tr)
                for s in range(8):
                    pe.wait_ge(*r_md.nth(l, s))
                    if s >= 2:
                        pe.wait_ge(*r_bcu.nth(l, s - 2))
                    elif s == 0:
                        pe.wait_ge(*r_trc.nth(l, 0))
                    md = (B1, B2)[s % 2]
                    bank = 2 * (s % 2)
                    if s < 4:
                        for hh in range(2):
                            ins = mm(PS[64 * hh:64 * hh + 64, bank, :], K[0:8, C_ONE:C_ONE + 64],
                                     md[0:8, 512 * hh:512 * hh + 512], start=True, stop=True)
                    else:
                        for a in range(2):
                            ins = mm(PS[:, bank + a, :], K[0:8, C_ONE:C_ONE + 128],
                                     md[0:8, 512 * a:512 * a + 512], start=True, stop=True)
                    finish(ins, r_bc)
                pe.wait_ge(*sm_em.nth(l, 0))
                pe.wait_ge(*r_bcu.nth(l, 7))
                def broadcast(v):
                    if v:
                        pe.wait_ge(*ex_arg.nth(l, v - 1))
                    p0 = 0 if v < 4 else 32
                    col = C_SEL + 128 * (v % 4)
                    finish(mm(PS[:, 4, :], K[p0:p0 + 4, col:col + 128], SROW[p0:p0 + 4, :],
                              start=True, stop=True), bc_done)
                broadcast(0)
                for v in range(8):
                    h, c, r0 = v % 4, (v % 4) // 2, 64 * (v % 2)
                    E = (B1, B2)[v % 2]
                    for i in range(NT):
                        if i == 2 and v < 7:
                            broadcast(v + 1)
                        n = NPR - 128 * i
                        m = 4 * v + i
                        if m >= 2:
                            pe.wait_ge(*w_ready.nth(l, m - 2))
                        if v < 4:
                            ins = mm(PS[:, 5 + m % 2, 0:n], F[r0:r0 + 64, CK + c, 128 * i:128 * i + 128],
                                     F[r0:r0 + 64, CQ + c, 128 * i:NPR], start=True, stop=True)
                        else:
                            ins = mm(PS[:, 5 + m % 2, 0:n], F[:, XB + c, 128 * i:128 * i + 128],
                                     F[:, XC + c, 128 * i:NPR], start=True, stop=True)
                        finish(ins, st_block)
                    if v in (2, 4):
                        pe.wait_ge(*c_sq.nth(l, v // 2 - 1))
                        for a in range(2):
                            ins = mm(PS[:, 1 + 2 * a, 0:HALF], kc(C_BLK), S[:, 2, a * HALF:(a + 1) * HALF],
                                     start=True, stop=True)
                        finish(ins, c_sum)
                    pe.wait_ge(*vu_ready.nth(l, v))
                    for i in range(NT):
                        if v < 4:
                            mm(PS[r0:r0 + 64, 7, 64 * c:64 * c + 64], VU[:, v % 2, i, :], TM[:, T_CK + c, i, r0:r0 + 64],
                               start=i == 0, stop=i == NT - 1)
                        else:
                            mm(PS[r0:r0 + 64, 7, 130 + 128 * c:258 + 128 * c], VU[:, v % 2, i, :], TM[:, T_XB + c, i, :],
                               start=i == 0, stop=i == NT - 1)
                    if v < 4:
                        for i in range(NT):
                            mm(PS[r0:r0 + 64, 7, 128 + c:129 + c], TM[:, T_CK + c, i, r0:r0 + 64], U4[:, v % 2, i:i + 1],
                               start=i == 0, stop=i == NT - 1)
                    nb = 0 if v < 4 else c
                    if v == 2 or v == 4:
                        pe.wait_ge(*c_h.nth(l, (v - 2) // 2))
                    if v == 6:
                        pe.wait_ge(*c_root.nth(l, 1))
                    for i in range(NT):
                        n = NPR - 128 * i
                        pe.wait_ge(*w_ready.nth(l, 4 * v + i))
                        wv = (TM[:, T_CV + c, i, r0:r0 + 64] if v < 4 else TM[:, T_XX + c, i, r0:r0 + 64])
                        ins = mm(PS[r0:r0 + 64, nb, 128 * i:NPR], wv, E[:, OFF[i]:OFF[i] + n],
                                 start=i == 0, stop=i == NT - 1)
                    if v < 4:
                        for i in range(NT):
                            n = NPR - 128 * i
                            ins = mm(PS[r0:r0 + 64, 2, 128 * i:NPR], K[:, C_ONE:C_ONE + 64],
                                     E[:, OFF[i]:OFF[i] + n], start=i == 0, stop=i == NT - 1)
                    finish(ins, num_done)
                    if v in (1, 3):
                        if v == 3:
                            pe.wait_ge(*c_root.nth(l, 0))
                        finish(mm(PS[:, 3, :], K[0:4, C_SELP + 128 * c:C_SELP + 128 * c + 128], MR[:, :],
                                  start=True, stop=True), c_em)
                pe.wait_ge(*d_sq.nth(l, 1))
                for a in range(2):
                    for c in range(2):
                        ins = mm(PS[:, 2 + a, 0:HALF], kc(C_ONE), S[:, 2 + c, a * HALF:(a + 1) * HALF],
                                 start=c == 0, stop=c == 1)
                finish(ins, d_sum)
                pe.wait_ge(*sb_a.nth(l, 0))
                pe.wait_ge(*d_root.nth(l, 0))
                pe.wait_ge(*pst_done.nth(l, 0))
                pe.wait_ge(*scaled.nth(l, 1))
                for t in range(NT):
                    c, r0 = t // 2, 64 * (t % 2)
                    w = 128 * (t + 1)
                    for h in range(4):
                        p0 = 64 * (h % 2)
                        if h >= 2:
                            pe.wait_ge(*ix_relu.nth(l, 4 * t + h - 2))
                        elif t:
                            pe.wait_ge(*at_trc.nth(l, 4 * t - 2 + h))
                        finish(mm(PS[:, h % 2, 0:w], F[p0:p0 + 64, IQ + h // 2, 128 * t:128 * t + 128],
                                  F[p0:p0 + 64, IKD, 0:w], start=True, stop=True), ix_done)
                    if t:
                        pe.wait_ge(*a_exp.nth(l, t - 1))

                    def logits(i, start):
                        return mm(bblock(i), F[r0:r0 + 64, BK + c, 128 * i:128 * i + 128],
                                  F[r0:r0 + 64, BQ + c, 128 * i:NPR], start=start, stop=True)
                    for i in range(NT):
                        ins = logits(i, True)
                    finish(ins, z_done)

                    def attend(h):
                        q0 = 64 * (h // 2)
                        finish(mm(PS[:, h % 2, 0:w], F[q0:q0 + 64, AQ + h % 2, 128 * t:128 * t + 128],
                                  F[q0:q0 + 64, AK, 0:w], start=True, stop=True), at_qk)
                    for h in range(2):
                        pe.wait_ge(*ix_relu.nth(l, 4 * t + 2 + h))
                        attend(h)
                    cached_values(l, 2 * t)
                    pe.wait_ge(*sp_mask.nth(l, t))
                    for i in range(NT):
                        mm(bblock(i), kc(C_NTRI), B1[:, OFF[i]:OFF[i] + NPR - 128 * i], start=True, stop=False)
                        for j in range(i + 1, NT):
                            mm(bblock(i, 128 * (j - i)), kc(C_NONE),
                               B1[:, OFF[j]:OFF[j] + NPR - 128 * j], start=False, stop=False)
                        ins = logits(i, False)
                    finish(ins, ac_done)
                    cached_values(l, 2 * t + 1)
                    pe.wait_ge(*a_mask.nth(l, t))
                    if t == 2:
                        pe.wait_ge(*b_out.nth(l, 0))
                    for i in range(NT):
                        ins = mm(PS[r0:r0 + 64, 7, 128 * i:NPR], TM[:, T_BV + c, i, r0:r0 + 64],
                                 B2[:, OFF[i]:OFF[i] + NPR - 128 * i], start=i == 0, stop=i == NT - 1)
                    finish(ins, pv_done)
                    for h in range(2, 4):
                        pe.wait_ge(*at_max.nth(l, 4 * t + h - 2))
                        attend(h)
                    for h in range(4):
                        q0 = 64 * (h // 2)
                        pe.wait_ge(*at_norm.nth(l, 4 * t + h))
                        if h < 2:
                            pe.wait_ge(*at_max.nth(l, 4 * t + h + 2))
                        else:
                            pe.wait_ge(*at_trc.nth(l, 4 * t + h - 2))
                        for j in range(t + 1):
                            ins = nc.tensor.transpose(PS[:, h % 2, 128 * j:128 * j + 128],
                                                      S[:, h, 128 * j:128 * j + 128], ident)
                        finish(ins, at_tr)
                        if h:
                            values(l, t, h - 1)
                    values(l, t, 3)
                pe.wait_ge(*sa_out.nth(l, 0))
                for s in (c_out, d_out, b_out):
                    pe.wait_ge(*s.nth(l, 1))
                pe.wait_ge(*a_out.nth(l, NT - 1))

                def again(k):
                    pe.wait_ge(*(xl_first.nth(l, k) if k < 4 else xl_again.nth(l, k - 4)))
                for d in range(KD):
                    nb = FIRST["gate"] + 5 * d + 4
                    for br, o in enumerate((AQ, BQ, CQ, DZ)):
                        q = 4 * d + br
                        if q >= 2:
                            pe.wait_ge(*g_sig.nth(l, q - 2))
                        dense_split(l, nb - 4 + br, 2 * (q % 2), x_parts, *[again] * (q == 0))
                    pe.wait_ge(*full(l, nb))
                    for br, o in enumerate((AQ, BQ, CQ, DZ)):
                        q = 4 * d + br
                        if q >= 2:
                            pe.wait_ge(*br_used.nth(l, q - 2))
                        for k in range(2):
                            for a in range(2):
                                ins = mm(PS[:, 4 + 2 * (q % 2) + a, 0:HALF],
                                         slot(l, nb)[:, 256 * br + 128 * k:256 * br + 128 * k + 128],
                                         F[:, o + k, a * HALF:(a + 1) * HALF], start=k == 0, stop=k == 1)
                        finish(ins, tile_used if br == 3 else br_done)
                def merged(k):
                    pe.wait_ge(*mg_hi.nth(l, k))
                    pe.wait_ge(*mg_lo.nth(l, k))
                for d in range(KD):
                    if d >= 2:
                        pe.wait_ge(*sq_ready.nth(l, 8 + d - 2))
                    else:
                        pe.wait_ge(*g_sig.nth(l, 30 + d))
                    dense_split(l, FIRST["out"] + d, 2 * (d % 2),
                                lambda k: (FR[:, HI_OF[k], :], FR[:, MERGED + k, :]), *[merged] * (d == 0))
                norm_sum(l, 1)
                norm_sum_chunks(l, 2)
                for j in range(2 * JF):
                    if j >= 4:
                        pe.wait_ge(*up_evac.nth(l, j - 4))
                    dense_split(l, FIRST["up"] + j, 2 * (j % 4), x_parts, *[normed(l, 2)] * (j == 0))
                for d in range(KD):
                    if d >= 2:
                        pe.wait_ge(*sq_ready.nth(l, 24 + d - 2))
                    else:
                        pe.wait_ge(*up_evac.nth(l, 2 * JF - 4 + d))
                    for k in range(JF):
                        t, e = divmod(JF * d + k, 8)
                        n = FIRST["down"] + t
                        m = S_DOWN + t
                        q, bank = K_ORDER[k], 2 * (d % 2)
                        if e == 0 or k == 0:
                            pe.wait_ge(*full(l, n))
                            pe.wait_ge(*w_hi.nth(l, m))
                            pe.wait_ge(*lo_ready(l, m))
                        if d == 0:
                            pe.wait_ge(*h_ready.nth(l, q))
                        if q < 2 * KD:
                            if d == 0:
                                pe.wait_ge(*hd_hi.nth(l, q))
                                pe.wait_ge(*hd_lo.nth(l, q))
                            ins = block_split(half(l, m), e, (XH, XL)[q // KD][:, q % KD, :], FR[:, q, :], bank, False,
                                              False)
                        else:
                            for a in range(2):
                                ins = mm(PS[:, bank + a, 0:HALF], slot(l, n)[:, 128 * e:128 * e + 128],
                                         F[:, q, a * HALF:(a + 1) * HALF], start=k == 0, stop=k == JF - 1)
                        if k == JF - 1:
                            ins.then_inc(dn_done.sem, 1)
                            if e == 7:
                                pe.wait_ge(*dn_done.nth(l, d))
                                pe.sem_inc(tile_used.sem, 1)
                        elif e == 7:
                            ins.then_inc(tile_used.sem, 1)
                norm_sum(l, 3)

        @block.scalar
        def _(act):
            A = nc.scalar.activation

            def do(ins, s=act_own):
                ins.then_inc(s.sem, 1)
                s.n += 1
                act.wait_ge(s.sem, s.n)

            def store(dst, src):
                act.dma_start(dst, src).then_inc(stored.sem, 16)

            act.wait_ge(loaded.sem, 48)
            act.wait_ge(pt_loaded.sem, 16)

            def squares(l, j, before):
                for k in range(KD):
                    before(k)
                    if k >= 2:
                        act.wait_ge(*sq_summed.nth(l, 8 * (j // 2) + k - 2))
                    do(A(S[:, k % 2, :], X[:, k, :], ACT.Square), sq_ready)

            def split(l, m):
                if m < NSPLIT:
                    act.wait_ge(*full(l, SPLIT[m]))
                    if m >= 2:
                        act.wait_ge(*tile_done(l, SPLIT[m - 2]))
                    elif l:
                        act.wait_ge(*tile_done(l - 1, SPLIT[NSPLIT - 2 + m]))
                    do(A(WH[:, half(l, m), :], slot(l, SPLIT[m]), ACT.Copy), w_hi)

            def leading(l, half):
                for k in range(KD):
                    act.wait_ge(*xt_ready.nth(l, 8 * half + k))
                    do(A(XH[:, k, :], S[:, k % 2, :], ACT.Copy), xh_ready)

            def root(l, j):
                act.wait_ge(*(sum_ready.nth(l, j // 2) if j % 2 else sq_summed.nth(l, 4 * j + 7)))
                do(A(halves(S[:, 3, :]), pair(4), ACT.Sqrt, bias=eps, scale=1.0 / DM), root_ready)

            for l in range(L):
                if l == 0:
                    squares(l, 0, lambda k: None)
                    split(l, 0)
                    split(l, 1)
                else:
                    squares(l, 0, lambda k: act.wait_ge(*norm_out.nth(l - 1, 24 + k)))
                root(l, 0)
                leading(l, 0)
                def wide(ap):
                    return ap.rearrange("p (a c) -> p a c", a=2)
                for c in range(NPROJ):
                    act.wait_ge(*tile_done(l, proj(c)))
                    if c + 2 < NPROJ and c + 2 not in (CUT, CUT + 1):
                        split(l, c + 2)
                    do(A(halves(F[:, c, :]), pair(2 * (c % 2)), ACT.Copy), proj_out)
                    if c == CUT - 1:
                        for u in range(NU):
                            if by_act(u):
                                cached(act, l, FIRST["K"] + u, u, K_REC, k_c)
                        split(l, CUT)
                        split(l, CUT + 1)
                        act.wait_ge(*sx_done.nth(l, 0))
                        do(A(wide(SF[0:32, 0:1024]), PS[0:32, 4:6, :], ACT.Relu))
                        do(A(SF[0:32, 1024:1025], PS[0:32, 6, 0:1], ACT.Relu))
                        do(A(wide(SF[32:64, 0:1024]), PS[32:64, 4:6, :], ACT.Copy))
                        do(A(SF[32:64, 1024:1025], PS[32:64, 6, 0:1], ACT.Copy))
                        do(A(wide(SF[64:96, 0:1024]), PS[64:96, 4:6, :], ACT.Copy), sb_zc)
                    elif c == CUT:
                        act.wait_ge(*sx_done.nth(l, 1))
                        do(A(wide(T[0:8, 0:1024]), PS[0:8, 4:6, :], ACT.Copy))
                        do(A(T[0:8, 1024:1025], PS[0:8, 7, 0:1], ACT.Copy), sx_score)
                    elif c == CUT + 1:
                        act.wait_ge(*sb_zt.nth(l, 0))
                        do(A(S[:, 3, 0:256], PS[:, 6, 0:256], ACT.Copy))
                        do(A(S[:, 4, 0:256], S[:, 3, 0:256], ACT.Abs))
                        do(A(S[:, 4, 0:256], S[:, 4, 0:256], ACT.Exp, scale=-1.0))
                        do(A(S[:, 4, 0:256], S[:, 4, 0:256], ACT.Ln, bias=one), sb_ln)
                    elif c == CUT + 6:
                        act.wait_ge(*sb_arg.nth(l, 0))
                        do(A(PA[:, 256:512], S[:, 3, 0:256], ACT.Exp), sb_a)
                    elif c == NPROJ - 2:
                        act.wait_ge(*sa_max.nth(l, 0))
                        do(A(SF[32:64, 0:1025], SF[32:64, 0:1025], ACT.Exp, bias=MX[32:64, 8:9], scale=0.125,
                             accum_out=MX[32:64, 9:10]), sa_exp)
                act.wait_ge(*sa_tr.nth(l, 0))
                do(A(PA[:, 0:256], PS[:, 4, 0:256], ACT.Copy), sa_trc)
                if l:
                    act.wait_ge(stored.sem, N_STORES_UPTO[l - 1])

                def token_major(i):
                    act.wait_ge(*tm_done.nth(l, i))
                    src_t = PS[:, 4 + i % 4, :].rearrange("p (t c) -> p t c", c=128)
                    if TO_TM[i][1] == T_SM:
                        do(A(SMT[:, :, 48:64], src_t[:, :, 64:80], ACT.Copy), tm_ready)
                    else:
                        do(A(TM[:, TO_TM[i][1], :, :], src_t, ACT.Copy), tm_ready)
                for c in range(7):
                    if c < 6:
                        if c < 2:
                            act.wait_ge(*rope_done.nth(l, 5))
                        do(A(S[:, c % 2, :], F[:, XX + c, :], ACT.Identity,
                             bias=V[:, l, V_DCB + c:V_DCB + c + 1],
                             scale=V[:, l, V_DCW + 4 * c + 3:V_DCW + 4 * c + 4]), cv_init)
                    if c >= 1:
                        act.wait_ge(*cv_done.nth(l, c - 1))
                        do(A(DO[:, c - 1, :], F[:, XX + c - 1, NPR - 3:TOK], ACT.Copy), cv_saved)
                        do(A(F[:, XX + c - 1, :], S[:, (c - 1) % 2, :], ACT.Silu), xbc_ready)
                    token_major(c)
                for i in range(7, len(TO_TM)):
                    token_major(i)
                act.wait_ge(*sm_v.nth(l, 0))
                do(A(SMT[:, :, 8:16], SMT[:, :, 0:8], ACT.Abs))
                do(A(SMT[:, :, 8:16], SMT[:, :, 8:16], ACT.Exp, scale=-1.0))
                do(A(SMT[:, :, 8:16], SMT[:, :, 8:16], ACT.Ln, bias=one), sm_ln)
                do(A(NEGA[:, 4:8], V[:, l, V_AL:V_AL + 4], ACT.Exp), sm_ln)
                act.wait_ge(*sm_tr.nth(l, 0))
                do(A(SROW[0:96, :], PS[0:96, 5, :], ACT.Copy), sm_row)
                act.wait_ge(*sm_g.nth(l, 0))
                do(A(SROW[0:4, :], SROW[0:4, :], ACT.Copy, scale=-1.0))
                do(A(ML[:, :], MR[:, NPR - 1:NPR], ACT.Copy))
                do(A(MR[:, :], MR[:, :], ACT.Exp, scale=-1.0), sm_em)
                store(pm_o[l], ML[:, :])
                act.wait_ge(*rope_done.nth(l, 5))
                store(ka_o[l], F[:, AK, :])
                store(va_o[l], F[:, AV, :])
                store(ki_o[l], F[0:64, IKD, :])
                store(kb_o[l], F[:, BK:BK + 2, :])
                store(vb_o[l], F[:, BV:BV + 2, :])
                store(dconv_o[l], DO[:, :, :])
                act.wait_ge(st_loaded.sem, 48 * (l + 1))
                store(dconv_s_o[l], ST[:, S_DC:S_DC + 144])
                act.wait_ge(*r_v.nth(l, 0))
                do(A(SS[:, 5:7, :], SS[:, 3:5, :], ACT.Abs))
                do(A(SS[:, 5:7, :], SS[:, 5:7, :], ACT.Exp, scale=-1.0))
                do(A(SS[:, 5:7, :], SS[:, 5:7, :], ACT.Ln, bias=one))
                do(A(SS[:, 17, 0:2], V[:, l, V_SAL:V_SAL + 2], ACT.Exp), r_ln)
                act.wait_ge(*r_arg.nth(l, 0))
                do(A(SS[:, 11:15, :], SS[:, 7:11, :], ACT.Exp), r_exp)
                act.wait_ge(*r_tr.nth(l, 0))
                do(A(S[0:8, 2:4, 0:512], PS[0:8, 0:2, :], ACT.Copy), r_trc)
                for c in range(2):
                    do(A(F[:, CO + c, :], F[:, CO + c, :], ACT.Sigmoid), c_sg)
                for c in range(2):
                    do(A(F[:, DZ + c, :], F[:, DZ + c, :], ACT.Silu), d_sl)
                def decays(v):
                    h, E = v % 4, (B1, B2)[v % 2]
                    act.wait_ge(*bc_done.nth(l, v))
                    if v >= 2:
                        act.wait_ge(*num_done.nth(l, v - 2))
                    for i in range(NT):
                        col = SMT[:, i, 40 + h:41 + h] if v < 4 else RT[:, i, 32 + h:33 + h]
                        do(A(E[:, OFF[i]:OFF[i] + NPR - 128 * i], PS[:, 4, 128 * i:NPR], ACT.Relu, bias=col,
                             scale=-1.0), ex_arg if i == NT - 1 else act_own)
                    do(A(E[:, :], E[:, :], ACT.Exp, scale=-1.0), ex_done)
                act.wait_ge(*sm_ng.nth(l, 0))
                decays(0)
                for v in range(8):
                    if v < 7:
                        decays(v + 1)
                    if v in (1, 3):
                        c = v // 2
                        act.wait_ge(*num_done.nth(l, v))
                        do(A(S[:, 0, 0:NPR], PS[:, 2, :], ACT.Abs), c_abs)
                        act.wait_ge(*c_h.nth(l, c))
                        do(A(S[:, 2, :], S[:, 1, :], ACT.Square), c_sq)
                    elif v in (2, 4):
                        act.wait_ge(*c_sum.nth(l, v // 2 - 1))
                        for a in range(2):
                            do(A(S[:, 3, HALF * a:HALF * (a + 1)], PS[:, 1 + 2 * a, 0:HALF], ACT.Sqrt, bias=eps,
                                 scale=1.0 / HD), c_root if a else act_own)
                for c in range(2):
                    act.wait_ge(*d_y.nth(l, c))
                    do(A(S[:, 2 + c, :], S[:, c, :], ACT.Square), d_sq)
                act.wait_ge(*d_sum.nth(l, 0))
                do(A(halves(S[:, 4, :]), pair(2), ACT.Sqrt, bias=eps, scale=1.0 / 256), d_root)
                do(A(PST[:, :], PS[:, 7, 0:386], ACT.Copy), pst_done)
                store(pc_o[l], PST[:, 0:128])
                store(pn_o[l], PST[:, 128:130])
                store(pssm_o[l], PST[:, 130:386])
                act.wait_ge(*r_out.nth(l, 0))
                store(sc_o[l], CS[:, :, :, :])
                store(sssm_o[l], HS[:, :, :, :])
                store(sn_o[l], SS[:, 22, :])
                store(sm_o[l], SS[:, 21, :])
                act.wait_ge(*d_out.nth(l, 1))
                for t in range(NT):
                    w = 128 * (t + 1)
                    for h in range(4):
                        act.wait_ge(*ix_done.nth(l, 4 * t + h))
                        do(A(S[:, h, 0:w], PS[:, h % 2, 0:w], ACT.Relu), ix_relu)
                    act.wait_ge(*z_done.nth(l, t))
                    for i in range(NT):
                        do(A(B1[:, OFF[i]:OFF[i] + NPR - 128 * i], bblock(i), ACT.Abs))
                    do(A(B1[:, :], B1[:, :], ACT.Exp, scale=-1.0))
                    do(A(B1[:, :], B1[:, :], ACT.Ln, bias=one), z_ln)
                    act.wait_ge(*ac_done.nth(l, t))
                    if t:
                        act.wait_ge(*pv_done.nth(l, t - 1))
                    for i in range(NT):
                        do(A(B2[:, OFF[i]:OFF[i] + NPR - 128 * i], bblock(i), ACT.Exp),
                           a_exp if i == NT - 1 else act_own)
                    if t % 2:
                        act.wait_ge(*pv_done.nth(l, t))
                        do(A(F[:, BQ + t // 2, 0:NPR], PS[:, 7, :], ACT.Copy), b_out)
                    for h in range(4):
                        act.wait_ge(*at_max.nth(l, 4 * t + h))
                        do(A(S[:, h, 0:w], S[:, h, 0:w], ACT.Exp, bias=MX[:, h:h + 1], scale=0.125,
                             accum_out=MX[:, 4 + h:5 + h]), at_exp)
                    for h in range(4):
                        m = 4 * t + h
                        act.wait_ge(*at_tr.nth(l, m))
                        if m >= 2:
                            act.wait_ge(*at_pv.nth(l, m - 2))
                        do(A(PTR[h % 2][:, 0:w], PS[:, h % 2, 0:w], ACT.Copy), at_trc)
                    act.wait_ge(*at_pv.nth(l, 4 * t + 3))
                    do(A(F[:, AQ:AQ + 2, 128 * t:128 * t + 128],
                         PS[:, 2, 0:256].rearrange("p (c q) -> p c q", c=2), ACT.Copy), a_out)
                split(l, NPROJ)
                split(l, NPROJ + 1)

                def merged_leading(k):
                    act.wait_ge(*br_used.nth(l, 4 * k + 3))
                    do(A(FR[:, HI_OF[k], :], F[:, MERGED + k, :], ACT.Copy), mg_hi)
                for q in range(32):
                    act.wait_ge(*tile_done(l, FIRST["gate"] + 5 * (q // 4) + q % 4))
                    if q + 2 < 32:
                        split(l, NPROJ + q + 2)
                    if q >= 4:
                        act.wait_ge(*br_used.nth(l, q - 4))
                    do(A(halves(S[:, q % 4, :]), pair(2 * (q % 2)), ACT.Sigmoid), g_sig)
                    if q % 4 == 1 and q > 4:
                        merged_leading(q // 4 - 1)
                split(l, S_OUT)
                split(l, S_OUT + 1)
                merged_leading(KD - 1)

                def evac(l, j, d, out):
                    do(A(halves(F[:, out + d, :]), pair(2 * (d % 2)), ACT.Copy))
                    if d >= 2:
                        act.wait_ge(*sq_added.nth(l, 8 * (j // 2) + d - 2))
                    else:
                        act.wait_ge(*(br_used.nth(l, 31) if j == 1 else h_ready.nth(l, JF - 1)))
                    do(A(halves(S[:, d % 2, :]), pair(2 * (d % 2)), ACT.Square), sq_ready)

                for d in range(KD):
                    act.wait_ge(*tile_done(l, FIRST["out"] + d))
                    split(l, S_OUT + d + 2)
                    evac(l, 1, d, 0)
                root(l, 1)
                squares(l, 2, lambda k: act.wait_ge(*norm_out.nth(l, 8 + k)))
                root(l, 2)
                leading(l, 1)
                for j in range(JF):
                    for g in range(2):
                        m = 2 * j + g
                        ch = g * JF + j
                        act.wait_ge(*tile_done(l, FIRST["up"] + m))
                        split(l, S_UP + m + 2)
                        if m >= 2:
                            act.wait_ge(*fcv.nth(l, m - 2))
                        else:
                            act.wait_ge(*norm_out.nth(l, 23))
                        do(A(halves(S[:, g, :]), pair(2 * (m % 4)), ACT.Copy))
                        do(A(FO[:, ch, :], S[:, g, NPR - 2:TOK], ACT.Copy))
                        if j:
                            act.wait_ge(*h_ready.nth(l, j - 1))
                        do(A(halves(S[:, 2 + g, :]), pair(2 * (m % 4)), ACT.Identity,
                             bias=V[:, l, V_FCB + ch:V_FCB + ch + 1],
                             scale=V[:, l, V_FCW + 3 * ch + 2:V_FCW + 3 * ch + 3]), up_evac)
                    act.wait_ge(*fcv.nth(l, 2 * j + 1))
                    do(A(S[:, 4, :], S[:, 3, :], ACT.Gelu_apprx_tanh), gl_done)
                store(fconv_o[l], FO[:, :, :])
                store(fconv_s_o[l], ST[:, S_FC:S_FC + 4 * JF * 8])
                for k in range(2 * KD):
                    act.wait_ge(*tile_done(l, FIRST["up"] + 2 * JF - 1))
                    do(A((XH, XL)[k // KD][:, k % KD, :], F[:, k, :], ACT.Copy), hd_hi)
                for t in range(JF):
                    for d in range(KD):
                        if DOWN_END[d] == t:
                            act.wait_ge(*dn_done.nth(l, d))
                            evac(l, 3, d, JF)
                    if t + 2 < JF:
                        split(l, S_DOWN + t + 2)
                    elif l + 1 < L:
                        split(l + 1, t + 2 - JF)
                root(l, 3)

        @block.vector
        def _(dve):
            v_ = nc.vector

            def do(ins, s=dve_own):
                ins.then_inc(s.sem, 1)
                s.n += 1
                dve.wait_ge(s.sem, s.n)

            def tt(out, a, b, op, s=dve_own):
                do(v_.tensor_tensor(out, a, b, op), s)

            def stt(out, a, sc, b, o0, o1, s=dve_own):
                do(v_.scalar_tensor_tensor(out, a, sc, b, o0, o1), s)

            def ts(out, a, s1, s2, o0, o1, s=dve_own):
                do(v_.tensor_scalar(out, a, s1, s2, o0, o1), s)

            for t in (QI, QA, RT):
                do(v_.memset(t[:], 0.0))
            dve.wait_ge(loaded.sem, 48)

            def add_squares(l, j, k):
                    dve.wait_ge(*sq_ready.nth(l, 8 * j + k))
                    if k == 0:
                        do(v_.tensor_copy(S[:, 2, :], S[:, 0, :]), sq_added)
                    else:
                        tt(S[:, 2, :], S[:, 2, :], S[:, k % 2, :], ALU.add, sq_added)

            def split(l, m):
                if m < NSPLIT:
                    dve.wait_ge(*w_hi.nth(l, m))
                    v_.tensor_tensor(WL[:, half(l, m), :], slot(l, SPLIT[m]), WH[:, half(l, m), :].bitcast(f32),
                                     ALU.subtract).then_inc(w_lo.sem, 1)
                    dve.wait_ge(*lo_ready(l, m))

            def pre_norm(l, j, col):
                dve.wait_ge(*root_ready.nth(l, j))
                do(v_.reciprocal(RB[:, :], S[:, 3, :]))

                def rest(k):
                    dve.wait_ge(*xh_ready.nth(l, 4 * j + k))
                    tt(XL[:, k, :], S[:, k % 2, :], XH[:, k, :].bitcast(f32), ALU.subtract, norm_out)
                for k in range(KD):
                    if k >= 2:
                        rest(k - 2)
                    stt(S[:, k % 2, :], X[:, k, :], V[:, l, col + k:col + k + 1], RB[:, :], ALU.mult, ALU.mult,
                        xt_ready)
                rest(6)
                rest(7)

            def post_norm(l, j, col, out):
                if j == 1:
                    for k in range(KD):
                        split(l, S_OUT + k + 2)
                        add_squares(l, j, k)
                else:
                    for t in range(JF):
                        for k in range(KD):
                            if DOWN_END[k] == t:
                                add_squares(l, j, k)
                        if t + 2 < JF:
                            split(l, S_DOWN + t + 2)
                        elif l + 1 < L:
                            split(l + 1, t + 2 - JF)
                dve.wait_ge(*root_ready.nth(l, j))
                do(v_.reciprocal(S[:, 3, :], S[:, 3, :]))
                for k in range(KD):
                    stt(S[:, 4, :], F[:, out + k, :], V[:, l, col + k:col + k + 1], S[:, 3, :], ALU.mult, ALU.mult)
                    tt(X[:, k, :], X[:, k, :], S[:, 4, :], ALU.add, norm_out)

            for l in range(L):
                def vc(col, n=1, p0=0, p1=128):
                    return V[p0:p1, l, col:col + n]

                if l == 0:
                    split(l, 0)
                    split(l, 1)
                pre_norm(l, 0, V_NPRE)
                def rotate(i):
                    dve.wait_ge(*perm_done.nth(l, i))
                    if i < 5:
                        c = [AQ, AQ + 1, AK, IQ, IQ + 1][i]
                        tt(S[:, 0, :], F[:, c, :], kc(C_COS, TOK), ALU.mult)
                        tt(halves(S[:, 1, :]), pair(4 + 2 * (i % 2)), halves(kc(C_SIN, TOK)), ALU.mult, perm_used)
                        tt(F[:, c, :], S[:, 0, :], S[:, 1, :], ALU.add, rope_done)
                    elif i == 5:
                        tt(halves(S[:, 0, :]), pair(6), halves(kc(C_COS, TOK)), ALU.mult, perm_used)
                    else:
                        tt(halves(S[:, 1, :]), pair(4), halves(kc(C_SIN, TOK)), ALU.mult, perm_used)
                        tt(F[:, IKD, :], S[:, 0, :], S[:, 1, :], ALU.add, rope_done)
                for m in range(CUT):
                    if m >= 2:
                        split(l, m)
                    if m >= CUT - 2:
                        for i in range(2 * (m - CUT + 2), 2 * (m - CUT + 2) + 2):
                            rotate(i)
                for i in range(4, 7):
                    rotate(i)
                do(v_.memset(QB[:], 0.0))
                dve.wait_ge(*scaled.nth(l, 0))

                def place(t, h):
                    return t.rearrange("p b c -> p (b c)")[:, h:h + 36 * 7 + 1:36]
                for h in range(4):
                    r0 = 64 * (h % 2)
                    do(v_.tensor_copy(place(QI[:, :, :], h), F[r0:r0 + 64, IQ + h // 2, NPR:TOK]))
                    do(v_.tensor_copy(place(QB[r0:r0 + 64, h // 2, :, :], h), F[r0:r0 + 64, BQ + h // 2, NPR:TOK]))
                    r0 = 64 * (h // 2)
                    do(v_.tensor_copy(place(QA[r0:r0 + 64, :, :], h), F[r0:r0 + 64, AQ + h % 2, NPR:TOK]),
                       q_pad if h == 3 else dve_own)
                split(l, CUT)
                split(l, CUT + 1)
                dve.wait_ge(*sx_done.nth(l, 0))
                stt(IWW[:, :], PS[0:32, 7, 0:8], 1.0 / 16, K[0:32, C_EM:C_EM + 8], ALU.mult, ALU.mult, sx_iw)
                dve.wait_ge(*sx_score.nth(l, 0))
                for k in range(TOPK_S // 8):
                    if k == 4:
                        dve.wait_ge(*sb_ln.nth(l, 0))
                        stt(S[:, 2, 0:256], S[:, 3, 0:256], 0.0, S[:, 4, 0:256], ALU.max, ALU.add, sb_sp)
                    if k == 8:
                        dve.wait_ge(*sb_ac.nth(l, 0))
                        tt(S[:, 3, 0:256], S[:, 3, 0:256], PS[:, 7, 0:256], ALU.add, sb_arg)
                    do(v_.max(M8[0:8, :], T[0:8, 0:PAST + 1]))
                    do(v_.match_replace(T[0:8, 0:PAST + 1], M8[0:8, :], T[0:8, 0:PAST + 1], TAKEN))
                ts(T[0:8, 0:PAST + 1], T[0:8, 0:PAST + 1], TAKEN / 2, None, ALU.is_le, ALU.bypass, sx_sel)
                def wide(ap):
                    return ap.rearrange("p (a c) -> p a c", a=2)
                dve.wait_ge(*sx_bc.nth(l, 0))
                ts(wide(T[32:64, 0:1024]), PS[32:64, 4:6, :], -NEG, NEG, ALU.mult, ALU.add)
                ts(T[32:64, 1024:1025], PS[32:64, 7, 0:1], -NEG, NEG, ALU.mult, ALU.add)
                tt(SF[32:64, 0:1025], SF[32:64, 0:1025], T[32:64, 0:1025], ALU.add)
                do(v_.reduce_max(MX[32:64, 8:9], SF[32:64, 0:1025], AX))
                ts(MX[32:64, 8:9], MX[32:64, 8:9], -0.125, None, ALU.mult, ALU.bypass, sa_max)
                dve.wait_ge(*sa_exp.nth(l, 0))
                do(v_.reciprocal(MX[32:64, 9:10], MX[32:64, 9:10]))
                ts(SF[32:64, 0:1025], SF[32:64, 0:1025], MX[32:64, 9:10], None, ALU.mult, ALU.bypass)
                ts(DG[32:64, :], K[32:64, C_ID + 32:C_ID + 64], SF[32:64, 1024:1025], None, ALU.mult, ALU.bypass,
                   sa_p)
                dve.wait_ge(*sa_tr.nth(l, 0))
                tt(OS[:, :].rearrange("p (b h) -> p b h", h=4), PS[:, 7, 0:32].rearrange("p (b h) -> p b h", h=4),
                   F[:, AV, NPR:TOK].unsqueeze(2).to_broadcast([128, NSM, 4]), ALU.mult, sa_own)
                dve.wait_ge(st_loaded.sem, 48 * (l + 1))
                for c in range(6):
                    dve.wait_ge(*cv_init.nth(l, c))
                    y, x = S[:, c % 2, :], F[:, XX + c, :]
                    for k in range(3):
                        w = vc(V_DCW + 4 * c + k)
                        d = 3 - k
                        stt(y[:, d:NPR], x[:, 0:NPR - d], w, y[:, d:NPR], ALU.mult, ALU.add)
                        o = S_DC + 24 * c + 8 * k
                        stt(y[:, NPR:TOK], ST[:, o:o + 8], w, y[:, NPR:TOK], ALU.mult, ALU.add,
                            cv_done if k == 2 else dve_own)
                dve.wait_ge(*scaled.nth(l, 1))
                dve.wait_ge(*tm_ready.nth(l, 0))
                t0 = SMT[:, :, 48:64]

                def bc3(ap, n, axis_len):
                    return ap.unsqueeze(1).to_broadcast([128, n, axis_len])
                tt(SMT[:, :, 0:8], t0[:, :, 8:16], bc3(vc(V_BFD, 8), NT, 8), ALU.add)
                tt(SMT[:, :, 0:8], SMT[:, :, 0:8], bc3(kc(C_SGN, 8), NT, 8), ALU.mult, sm_v)
                tt(SMT[:, :, 32:36], t0[:, :, 4:8], bc3(vc(V_BI, 4), NT, 4), ALU.add)
                ts(SMT[:, :, 36:40], t0[:, :, 0:4], 1.0 / 16, None, ALU.mult, ALU.bypass)
                dve.wait_ge(*sm_ln.nth(l, 1))
                stt(SMT[:, :, 24:32], SMT[:, :, 0:8], 0.0, SMT[:, :, 8:16], ALU.max, ALU.add)
                do(v_.memset(NEGA[:, 0:4], -1.0))
                ts(NEGA[:, 4:8], NEGA[:, 4:8], -1.0, None, ALU.mult, ALU.bypass)
                tt(SMT[:, :, 16:24], SMT[:, :, 24:32], bc3(NEGA[:, :], NT, 8), ALU.mult, sm_cin)
                dve.wait_ge(*sm_cum.nth(l, 0))
                cum = PS[:, 4, 0:32].rearrange("p (t c) -> p t c", t=NT)
                tt(RT[:, :, 0:4], SMT[:, :, 32:36], cum[:, :, 0:4], ALU.subtract)
                do(v_.tensor_copy(RT[:, :, 32:36], cum[:, :, 4:8]))
                do(v_.tensor_copy(RT[:, :, 64:68], cum[:, :, 0:4]), sm_rt)
                ts(SMT[:, :, 40:44], RT[:, :, 0:4], -1.0, None, ALU.mult, ALU.bypass, sm_ng)
                dve.wait_ge(*sm_row.nth(l, 0))
                do(v_.tensor_tensor_scan(SROW[0:4, :], SROW[0:4, :], SROW[0:4, :], 0.0, ALU.max, ALU.max))
                tt(MR[:, :], SROW[0:4, :], PS[64:68, 5, :], ALU.add, sm_g)
                dve.wait_ge(*tm_ready.nth(l, 9))
                for c in range(2):
                    x4 = TM[:, T_XX + c, :, :].rearrange("p t (h d) -> p t h d", h=2)
                    tt(x4, x4, SMT[:, :, 28 + 2 * c:30 + 2 * c].unsqueeze(3).to_broadcast([128, NT, 2, HD]), ALU.mult)
                def fs(c0):
                    return F[:, c0:c0 + 2, NPR:TOK]

                def ss(i):
                    return SS[:, i, :].rearrange("p (c b) -> p c b", c=2)

                def bb(col):
                    return vc(col, 2).unsqueeze(2).to_broadcast([128, 2, NSM])
                dve.wait_ge(*xbc_ready.nth(l, 5))
                tt(ss(0), fs(CQ), fs(CK), ALU.mult)
                tt(ss(1), fs(CQ), ST[:, S_N:S_N + 16].rearrange("p (c b) -> p c b", c=2), ALU.mult)
                tt(ss(2), fs(XB), fs(XC), ALU.mult, r_prod)
                dve.wait_ge(*r_sel.nth(l, 0))
                sel = PS[:, 6, 0:48].rearrange("p (k c b) -> p k c b", k=3, c=2)
                tt(ss(15), sel[:, 0], bb(V_SBI), ALU.add)
                tt(ss(16), sel[:, 1], bb(V_SBF), ALU.add)
                ts(ss(3), ss(16), -1.0, None, ALU.mult, ALU.bypass)
                tt(ss(4), sel[:, 2], bb(V_SBD), ALU.add, r_v)
                dve.wait_ge(*r_ln.nth(l, 0))
                stt(SS[:, 5:7, :], SS[:, 3:5, :], 0.0, SS[:, 5:7, :], ALU.max, ALU.add)
                tt(ss(16), ST[:, S_M:S_M + 16].rearrange("p (c b) -> p c b", c=2), ss(5), ALU.subtract)
                tt(ss(21), ss(16), ss(15), ALU.max)
                tt(ss(7), ss(16), ss(21), ALU.subtract)
                tt(ss(8), ss(15), ss(21), ALU.subtract)
                ts(ss(9), ss(21), -1.0, None, ALU.mult, ALU.bypass)
                stt(ss(10), ss(6), -1.0, SS[:, 17, 0:2].unsqueeze(2).to_broadcast([128, 2, NSM]),
                    ALU.mult, ALU.mult, r_arg)
                dve.wait_ge(*r_exp.nth(l, 0))
                dve.wait_ge(*r_dot.nth(l, 0))
                dots = PS[:, 7, 0:48].rearrange("p (k c b) -> p k c b", k=3, c=2)
                tt(ss(18), dots[:, 0], ss(12), ALU.mult)
                tt(ss(19), dots[:, 1], ss(11), ALU.mult)
                tt(ss(19), ss(19), ss(18), ALU.add)
                tt(ss(22), ss(11), ST[:, S_N:S_N + 16].rearrange("p (c b) -> p c b", c=2), ALU.mult)
                tt(ss(20), ss(12), fs(CK), ALU.mult)
                tt(ss(22), ss(22), ss(20), ALU.add)
                tt(ss(20), ss(12), fs(CV), ALU.mult)
                tt(ss(23), ss(6), fs(XX), ALU.mult)
                tt(ss(0), dots[:, 2], ss(23), ALU.mult)
                for s in range(8):
                    dve.wait_ge(*r_bc.nth(l, s))
                    bank = 2 * (s % 2)
                    c = s % 2
                    wide = HD if s < 4 else 128
                    if s < 4:
                        p = PS[:, bank, :].rearrange("p (b d) -> p b d", b=NSM)
                        stt_, t = CS[:, c], B3[:, 0:512].rearrange("p (b d) -> p b d", b=NSM)
                    else:
                        p = PS[:, bank:bank + 2, :].rearrange("p a (b d) -> p (a b) d", d=128)
                        stt_, t = HS[:, c], B3[:, 0:1024].rearrange("p (b d) -> p b d", b=NSM)

                    def over(i):
                        return SS[:, i, 8 * c:8 * c + 8].unsqueeze(2).to_broadcast([128, NSM, wide])
                    if s in (0, 1, 4, 5):
                        tt(t, stt_, p, ALU.mult, r_bcu)
                        do(v_.tensor_reduce(SS[:, 1 if s < 4 else 2, 8 * c:8 * c + 8], t, AX, ALU.add))
                    else:
                        tt(t, p, over(20 if s < 4 else 23), ALU.mult, r_bcu)
                        tt(stt_, stt_, over(11 if s < 4 else 14), ALU.mult)
                        tt(stt_, stt_, t, ALU.add)
                tt(ss(1), ss(1), ss(11), ALU.mult)
                tt(ss(3), ss(18), fs(CV), ALU.mult)
                tt(ss(1), ss(1), ss(3), ALU.add)
                ts(ss(4), ss(19), -1.0, None, ALU.mult, ALU.bypass)
                tt(ss(19), ss(19), ss(4), ALU.max)
                tt(ss(19), ss(19), ss(13), ALU.max)
                do(v_.reciprocal(ss(19), ss(19)))
                tt(ss(1), ss(1), ss(19), ALU.mult)
                tt(ss(2), ss(2), ss(14), ALU.mult)
                tt(ss(2), ss(2), ss(0), ALU.add, r_out)
                for v in range(8):
                    h, c, r0 = v % 4, (v % 4) // 2, 64 * (v % 2)
                    E = (B1, B2)[v % 2]
                    dve.wait_ge(*vu_ready.nth(l, v))
                    for i in range(NT):
                        n = NPR - 128 * i
                        m = 4 * v + i
                        dve.wait_ge(*st_block.nth(l, m))
                        tt(E[:, OFF[i]:OFF[i] + n], E[:, OFF[i]:OFF[i] + n], PS[:, 5 + m % 2, 0:n], ALU.mult,
                           w_ready)
                    if v in (1, 3):
                        dve.wait_ge(*c_em.nth(l, c))
                        dve.wait_ge(*c_abs.nth(l, c))
                        tt(S[:, 0, 0:NPR], S[:, 0, 0:NPR], PS[:, 3, :], ALU.max)
                        do(v_.reciprocal(S[:, 0, 0:NPR], S[:, 0, 0:NPR]))
                        do(v_.tensor_copy(S[:, 1, NPR:TOK], SS[:, 1, 8 * c:8 * c + 8]))
                        tt(S[:, 1, 0:NPR], PS[:, 0, :], S[:, 0, 0:NPR], ALU.mult, c_h)
                    elif v in (2, 4):
                        n_ = v // 2 - 1
                        dve.wait_ge(*c_root.nth(l, n_))
                        do(v_.reciprocal(S[:, 3, :], S[:, 3, :]))
                        tt(S[:, 1, :], S[:, 1, :], S[:, 3, :], ALU.mult)
                        dve.wait_ge(*c_sg.nth(l, n_))
                        stt(F[:, CQ + n_, :], S[:, 1, :], vc(V_CN + n_), F[:, CO + n_, :], ALU.mult, ALU.mult, c_out)
                dve.wait_ge(*num_done.nth(l, 7))
                for c in range(2):
                    do(v_.tensor_copy(S[:, 4, NPR:TOK], SS[:, 2, 8 * c:8 * c + 8]))
                    do(v_.tensor_copy(S[:, 4, 0:NPR], PS[:, c, :]))
                    stt(S[:, c, :], F[:, XX + c, :], vc(V_D + c), S[:, 4, :], ALU.mult, ALU.add)
                    dve.wait_ge(*d_sl.nth(l, c))
                    tt(S[:, c, :], S[:, c, :], F[:, DZ + c, :], ALU.mult, d_y)
                dve.wait_ge(*d_root.nth(l, 0))
                do(v_.reciprocal(S[:, 4, :], S[:, 4, :]))
                for c in range(2):
                    stt(F[:, DZ + c, :], S[:, c, :], vc(V_DN + c), S[:, 4, :], ALU.mult, ALU.mult, d_out)
                for t in range(NT):
                    w = 128 * (t + 1)
                    score = B3[:, 0:w]
                    dve.wait_ge(*ix_relu.nth(l, 4 * t))
                    ts(score, S[:, 0, 0:w], SMT[:, t, 36:37], None, ALU.mult, ALU.bypass)
                    for h in range(1, 4):
                        dve.wait_ge(*ix_relu.nth(l, 4 * t + h))
                        stt(score, S[:, h, 0:w], SMT[:, t, 36 + h:37 + h], score, ALU.mult, ALU.add,
                            ix_sum if h == 3 else dve_own)
                    dve.wait_ge(*z_ln.nth(l, t))
                    for i in range(NT):
                        blk = B1[:, OFF[i]:OFF[i] + NPR - 128 * i]
                        stt(blk, bblock(i), 0.0, blk, ALU.max, ALU.add, sp_done if i == NT - 1 else dve_own)
                    dve.wait_ge(*ix_mask.nth(l, t))
                    if w <= TOPK_P:
                        ts(score, score, NEG / 2, NEG, ALU.is_le, ALU.mult, bias_ready)
                    else:
                        for _ in range(TOPK_P // 8):
                            do(v_.max(M8[:, :], score))
                            do(v_.match_replace(score, M8[:, :], score, TAKEN))
                        ts(score, score, TAKEN / 2, NEG, ALU.is_gt, ALU.mult, bias_ready)
                    for h in range(4):
                        dve.wait_ge(*at_qk.nth(l, 4 * t + h))
                        tt(S[:, h, 0:w], PS[:, h % 2, 0:w], score, ALU.add)
                        do(v_.reduce_max(MX[:, h:h + 1], S[:, h, 0:w], AX))
                        ts(MX[:, h:h + 1], MX[:, h:h + 1], -0.125, None, ALU.mult, ALU.bypass, at_max)
                    for h in range(4):
                        dve.wait_ge(*at_exp.nth(l, 4 * t + h))
                        do(v_.reciprocal(MX[:, 4 + h:5 + h], MX[:, 4 + h:5 + h]))
                        ts(S[:, h, 0:w], S[:, h, 0:w], MX[:, 4 + h:5 + h], None, ALU.mult, ALU.bypass, at_norm)
                dve.wait_ge(*at_pv.nth(l, 15))
                split(l, NPROJ)
                split(l, NPROJ + 1)
                dve.wait_ge(*tile_done(l, FIRST["V"] + NU - 1))
                tt(OS[:, :], OS[:, :], PS[:, 3, 0:32], ALU.add)
                for h in range(4):
                    r0 = 64 * (h // 2)
                    do(v_.tensor_copy(F[r0:r0 + 64, AQ + h % 2, NPR:TOK], OS[r0:r0 + 64, h:32:4]))
                for h in range(4):
                    r0, c = 64 * (h % 2), h // 2
                    do(v_.tensor_copy(F[r0:r0 + 64, BQ + c, NPR:TOK], PS[r0:r0 + 64, 3, 32 + 16 * c + h % 2:48 + 16 * c:2]),
                       sa_out if h == 3 else dve_own)
                for k in range(4, KD):
                    stt(S[:, k % 2, :], X[:, k, :], V[:, l, V_NPRE + k:V_NPRE + k + 1], RB[:, :], ALU.mult, ALU.mult)
                    tt(XL[:, k, :], S[:, k % 2, :], XH[:, k, :].bitcast(f32), ALU.subtract, xl_again)
                dve.wait_ge(stored.sem, N_STORES_MID[l])

                def merged_rest(k):
                    dve.wait_ge(*mg_hi.nth(l, k))
                    tt(FR[:, MERGED + k, :], F[:, MERGED + k, :], FR[:, HI_OF[k], :].bitcast(f32), ALU.subtract, mg_lo)
                for d in range(KD):
                    for m in range(4 * d + 2, 4 * d + 6):
                        split(l, NPROJ + m)
                        if m == 4 * d + 3 and d:
                            merged_rest(d - 1)
                    for br in range(4):
                        q = 4 * d + br
                        dve.wait_ge(*g_sig.nth(l, q))
                        dve.wait_ge(*(tile_done(l, FIRST["gate"] + 5 * d + 4) if br == 3
                                      else br_done.nth(l, 3 * d + br)))
                        p = pair(4 + 2 * (q % 2))
                        if br == 0:
                            tt(halves(F[:, MERGED + d, :]), halves(S[:, q % 4, :]), p, ALU.mult, br_used)
                        else:
                            tt(halves(S[:, 4, :]), halves(S[:, q % 4, :]), p, ALU.mult)
                            tt(F[:, MERGED + d, :], F[:, MERGED + d, :], S[:, 4, :], ALU.add, br_used)
                merged_rest(KD - 1)
                post_norm(l, 1, V_NPOST, 0)
                pre_norm(l, 2, V_FPRE)
                for j in range(JF):
                    for g in range(2):
                        m, ch = 2 * j + g, g * JF + j
                        split(l, S_UP + m + 2)
                        dve.wait_ge(*up_evac.nth(l, m))
                        u, y = S[:, g, :], S[:, 2 + g, :]
                        for k in range(2):
                            w = vc(V_FCW + 3 * ch + k)
                            d = 2 - k
                            stt(y[:, d:NPR], u[:, 0:NPR - d], w, y[:, d:NPR], ALU.mult, ALU.add)
                            o = S_FC + 16 * ch + 8 * k
                            stt(y[:, NPR:TOK], ST[:, o:o + 8], w, y[:, NPR:TOK], ALU.mult, ALU.add,
                                fcv if k == 1 else dve_own)
                    dve.wait_ge(*gl_done.nth(l, j))
                    tt(F[:, j, :], S[:, 2, :], S[:, 4, :], ALU.mult, h_ready)
                for k in range(2 * KD):
                    dve.wait_ge(*hd_hi.nth(l, k))
                    tt(FR[:, k, :], F[:, k, :], (XH, XL)[k // KD][:, k % KD, :].bitcast(f32), ALU.subtract, hd_lo)
                post_norm(l, 3, V_FPOST, JF)

        @block.gpsimd
        def _(pool):
            g_ = nc.gpsimd

            def do(ins, s=pool_own):
                ins.then_inc(s.sem, 1)
                s.n += 1
                pool.wait_ge(s.sem, s.n)

            def diagonal(buf, i, base):
                return g_.affine_select(out=buf[:, OFF[i]:OFF[i] + 128], in_=buf[:, OFF[i]:OFF[i] + 128],
                                        pattern=[[1, 128]], compare_op=ALU.is_ge, fill=0.0, base=base,
                                        channel_multiplier=-1)
            pool.wait_ge(loaded.sem, 48)
            for l in range(L):
                pool.wait_ge(*proj_out.nth(l, BQ + 1))
                do(g_.tensor_scalar(F[:, BQ:BQ + 2, :], F[:, BQ:BQ + 2, :], 0.125, None, ALU.mult), scaled)
                for m in range(CUT + 2, NPROJ):
                    pool.wait_ge(*w_hi.nth(l, m))
                    g_.tensor_tensor(WL[:, half(l, m), :], slot(l, SPLIT[m]), WH[:, half(l, m), :].bitcast(f32),
                                     ALU.subtract).then_inc(w_lo_p.sem, 1)
                    pool.wait_ge(*lo_ready(l, m))
                pool.wait_ge(*proj_out.nth(l, CK + 1))
                do(g_.tensor_scalar(F[:, CK:CK + 2, :], F[:, CK:CK + 2, :], 0.125, None, ALU.mult), scaled)
                pool.wait_ge(*r_trc.nth(l, 0))
                for s in range(8):
                    if s >= 2:
                        pool.wait_ge(*r_bc.nth(l, s - 2))
                    md = (B1, B2)[s % 2]
                    id8 = K[0:8, C_ID:C_ID + 8]
                    if s < 4:
                        out = md[0:8, 0:1024].rearrange("p (h b d) -> p h b d", h=2, b=NSM)
                        for hh in range(2):
                            do(g_.tensor_tensor(out[:, hh], STM[:, s // 4, s % 4, 64 * hh:64 * hh + 64].unsqueeze(1)
                                                .to_broadcast([8, NSM, HD]),
                                                id8.unsqueeze(2).to_broadcast([8, NSM, HD]), ALU.mult),
                               r_md if hh else pool_own)
                    else:
                        out = md[0:8, 0:1024].rearrange("p (b d) -> p b d", b=NSM)
                        do(g_.tensor_tensor(out, STM[:, s // 4, s % 4, :].unsqueeze(1).to_broadcast([8, NSM, 128]),
                                            id8.unsqueeze(2).to_broadcast([8, NSM, 128]), ALU.mult), r_md)
                for v in range(8):
                    h, c, r0, E = v % 4, (v % 4) // 2, 64 * (v % 2), (B1, B2)[v % 2]
                    pool.wait_ge(*ex_done.nth(l, v))
                    for i in range(NT):
                        do(diagonal(E, i, 0))
                    if v >= 2:
                        pool.wait_ge(*num_done.nth(l, v - 2))
                    src = TM[:, T_CV + c, :, r0:r0 + 64] if v < 4 else TM[:, T_XX + c, :, r0:r0 + 64]
                    for i in range(NT):
                        last = OFF[i] + NPR - 128 * i - 1
                        do(g_.tensor_copy(U4[:, v % 2, i:i + 1], E[:, last:last + 1]))
                    for i in range(NT):
                        do(g_.tensor_scalar(VU[:, v % 2, i, :], src[:, i, :], U4[:, v % 2, i:i + 1], None, ALU.mult),
                           vu_ready if i == NT - 1 else pool_own)
                for t in range(NT):
                    pool.wait_ge(*ix_sum.nth(l, t))
                    blk = B3[:, 128 * t:128 * t + 128]
                    do(g_.affine_select(out=blk, in_=blk, pattern=[[-1, 128]], compare_op=ALU.is_ge, fill=NEG,
                                        base=0, channel_multiplier=1), ix_mask)
                    pool.wait_ge(*sp_done.nth(l, t))
                    for i in range(NT):
                        do(diagonal(B1, i, -1), sp_mask if i == NT - 1 else pool_own)
                    pool.wait_ge(*a_exp.nth(l, t))
                    for i in range(NT):
                        do(diagonal(B2, i, -1), a_mask if i == NT - 1 else pool_own)
                pool.wait_ge(*pv_done.nth(l, 3))
                for k in range(4):
                    rest = T[:, 0:TOK]
                    do(g_.tensor_scalar(rest, X[:, k, :], V[:, l, V_NPRE + k:V_NPRE + k + 1], None, ALU.mult))
                    do(g_.tensor_tensor(rest, rest, RB[:, :], ALU.mult))
                    do(g_.tensor_tensor(XL[:, k, :], rest, XH[:, k, :].bitcast(f32), ALU.subtract), xl_first)


N_MID, N_END, N_ALL = 15, 17, 17
N_STORES_MID = [16 * (N_ALL * l + N_MID) for l in range(L)]
N_STORES_UPTO = [16 * N_ALL * (l + 1) for l in range(L)] + [16 * (N_ALL * L + 1)]


def kernel(**inputs):
    import numpy as np
    import concourse.bacc as bacc
    from concourse.bass_utils import run_bass_kernel_spmd

    g = {k: np.asarray(v) for k, v in inputs.items()}
    x = np.concatenate([g["x_prompt"][0], g["x_sample"][:, 0]], 0)
    arr = {}
    arr["x"] = x.T.reshape(KD, 128, TOK).transpose(1, 0, 2)
    arr["pages"] = g["page_table"].reshape(1, -1)
    offs = np.cumsum([0, 256, 128, 128, 256, 64, 4, 256, 256, 256, 256, 256, 256, 4, 4, 256, 256, 768, 4, 4096])
    (o_aq, o_ak, o_av, o_iq, o_ik, o_iw, o_bq, o_bk, o_bv, o_cq, o_ck, o_cv, o_ci, o_cf, o_co, o_dz, o_x, o_dt,
     o_g) = offs[:19]
    w = g["w_in"]
    r = np.arange
    zero = np.zeros((L, DM, 48), w.dtype)
    aq = np.concatenate([o_aq + 64 * h + r(64) for h in (0, 2, 1, 3)])
    cols = [w[:, :, aq], w[:, :, o_ak:o_ak + 128], w[:, :, o_av:o_av + 128], w[:, :, o_iq:o_iq + 256],
            w[:, :, o_ik:o_ik + 64], w[:, :, o_iw:o_iw + 4], w[:, :, o_ci:o_ci + 4], w[:, :, o_cf:o_cf + 4],
            w[:, :, o_dt:o_dt + 4], zero, w[:, :, o_bq:o_bq + 768], w[:, :, o_cq:o_cq + 768],
            w[:, :, o_co:o_co + 256], w[:, :, o_dz:o_dz + 256], w[:, :, o_x:o_x + 768]]
    wp = np.concatenate(cols, 2)

    def tiles(m, kk, nn):
        return m.reshape(L, kk, 128, nn, 128).transpose(0, 3, 2, 1, 4).reshape(L, nn, 128, kk * 128)
    arr["w_proj"] = tiles(wp, KD, NPROJ)
    wg = tiles(w[:, :, o_g:], KD, 32).reshape(L, 4, 8, 128, 1024).transpose(0, 2, 1, 3, 4)
    arr["w_gate"] = wg.reshape(L, 32, 128, 1024)
    ra = np.concatenate([64 * h + r(64) for h in (0, 2, 1, 3)])
    brs = [tiles(m, 2, KD) for m in (g["w_br_a"][:, ra], g["w_br_b"], g["w_br_c"], g["w_br_d"])]
    arr["w_br"] = np.concatenate(brs, 3)
    arr["w_out"] = tiles(g["w_out"], KD, KD)
    up = tiles(g["ffn_up"], KD, 2 * JF).reshape(L, 2, JF, 128, 1024).transpose(0, 2, 1, 3, 4)
    arr["w_up"] = up.reshape(L, 2 * JF, 128, 1024)
    dn = tiles(g["ffn_down"], JF, KD).reshape(L, KD, 128, JF, 128).transpose(0, 1, 3, 2, 4)[:, :, K_ORDER]
    arr["w_down"] = dn.reshape(L, JF, 8, 128, 128).transpose(0, 1, 3, 2, 4).reshape(L, JF, 128, SLOT)

    def fm(v, n):
        return v.reshape(L, n, 128).transpose(0, 2, 1)

    def bcast(v):
        return np.broadcast_to(v[:, None, :], (L, 128, v.shape[1]))

    def heads(v):
        return np.repeat(v.reshape(L, 2, 2), 64, 2).transpose(0, 2, 1)
    packs = [fm(g["norm_mix_pre"], 8), fm(g["norm_mix_post"], 8), fm(g["norm_ffn_pre"], 8),
             fm(g["norm_ffn_post"], 8), fm(g["c_norm"], 2), fm(g["d_norm"], 2),
             g["d_conv_w"].reshape(L, 4, 6, 128).transpose(0, 3, 2, 1).reshape(L, 128, 24), fm(g["d_conv_b"], 6),
             g["ffn_conv_w"].reshape(L, 3, 44, 128).transpose(0, 3, 2, 1).reshape(L, 128, 132),
             fm(g["ffn_conv_b"], 44), heads(g["d_D"]), bcast(g["c_b_i"]), bcast(g["c_b_f"]),
             bcast(g["d_dt_bias"]), bcast(g["d_A_log"]), heads(g["c_b_i"]), heads(g["c_b_f"]),
             heads(g["d_dt_bias"]), heads(g["d_A_log"])]
    vec = np.concatenate(packs, 2)
    assert vec.shape[2] == NV
    arr["vecs"] = vec.transpose(1, 0, 2)
    n_ = g["state_c_n"].reshape(L, 8, 2, 128).transpose(0, 3, 2, 1).reshape(L, 128, 16)
    m_ = np.repeat(g["state_c_m"].reshape(L, 8, 2, 2), 64, 3).transpose(0, 3, 2, 1).reshape(L, 128, 16)
    dc = g["state_d_conv"].reshape(L, 8, 3, 6, 128).transpose(0, 4, 3, 2, 1).reshape(L, 128, 144)
    fc = g["state_ffn_conv"].reshape(L, 8, 2, 44, 128).transpose(0, 4, 3, 2, 1).reshape(L, 128, 704)
    arr["states"] = np.concatenate([n_, m_, dc, fc], 2)
    arr["c_state"] = g["state_c_C"].reshape(L, 8, 2, 128, 64).transpose(0, 3, 2, 1, 4)
    arr["d_state"] = g["state_d_ssm"].reshape(L, 8, 2, 128, 128).transpose(0, 3, 2, 1, 4)
    ki = g["cache_a_kidx"].transpose(0, 1, 3, 2)
    ka = g["cache_a_k"].reshape(L, POOL, 128, 128).transpose(0, 1, 3, 2)
    kb = g["cache_b_k"].reshape(L, POOL, 128, 2, 128).transpose(3, 0, 1, 4, 2)
    arr["k_c"] = np.concatenate([ka, kb[0], kb[1], np.concatenate([ki, np.zeros_like(ki)], 2)], 3)
    arr["v_c"] = np.concatenate([g["cache_a_v"].reshape(L, POOL, 128, 128),
                                 g["cache_b_v"].reshape(L, POOL, 128, 256)], 3)

    k_ = np.zeros((128, NC_), np.float32)
    i = r(128)
    k_[:, C_ID:C_ID + 128] = np.eye(128)
    k_[:, C_ONE:C_ONE + 128] = 1
    k_[:, C_TRI:C_TRI + 128] = i[:, None] <= i[None]
    k_[:, C_NTRI:C_NTRI + 128] = -1.0 * (i[:, None] >= i[None])
    k_[:, C_NONE:C_NONE + 128] = -1
    swap = (i // 64) * 64 + (i % 64 + 32) % 64
    k_[swap, C_PERM + i] = 1
    k_[i % 64, C_DUP1 + i] = 1
    k_[(i % 64 + 32) % 64, C_DUP2 + i] = 1
    k_[:, C_BLK:C_BLK + 128] = (i[:, None] // 64) == (i[None] // 64)
    for h in range(4):
        k_[[h, 32 + h], C_SEL + 128 * h:C_SEL + 128 * h + 128] = 1
        k_[h, C_SELP + 128 * (h // 2) + 64 * (h % 2):C_SELP + 128 * (h // 2) + 64 * (h % 2) + 64] = 1
        for what in range(3):
            col = C_SELS + 128 * (2 * what + h // 2) + 64 * (h % 2)
            k_[64 + 4 * (what + 1) + h, col:col + 64] = 1
        k_[64 + h, C_AIW + h:C_AIW + 32:4] = 1
    for b in range(8):
        k_[4 * b:4 * b + 4, C_EM + b] = 1
        k_[b, C_EB + 4 * b:C_EB + 4 * b + 4] = 1
    k_[:, C_SGN:C_SGN + 4] = -1
    k_[:, C_SGN + 4:C_SGN + 8] = 1
    k_[:, C_EPS] = EPS
    inv = (10000.0 ** (-r(32) / 32)).astype(np.float32)
    pos = np.concatenate([r(NPR), np.full(NSM, PAST)]).astype(np.float32)
    ang = (inv[i % 32][:, None] * pos[None]).astype(np.float32)
    k_[:, C_COS:C_COS + TOK] = np.cos(ang)
    k_[:, C_SIN:C_SIN + TOK] = np.sin(ang) * np.where(i % 64 < 32, -1.0, 1.0)[:, None]
    arr["consts"] = k_

    nc = bacc.Bacc("TRN2", target_bir_lowering=False, num_devices=1)
    dt_of = mybir.dt.from_np

    def dram(name):
        arr[name] = np.ascontiguousarray(arr[name])
        return nc.dram_tensor(name, arr[name].shape, dt_of(arr[name].dtype), kind="ExternalInput").ap()
    shapes = {"y_o": (128, KD, TOK), "ka_o": (L, 128, TOK), "va_o": (L, 128, TOK), "ki_o": (L, 64, TOK),
              "kb_o": (L, 128, 2, TOK), "vb_o": (L, 128, 2, TOK), "pc_o": (L, 128, 128), "pn_o": (L, 128, 2),
              "pm_o": (L, 4, 1), "dconv_o": (L, 128, 6, 11), "dconv_s_o": (L, 128, 144), "pssm_o": (L, 128, 256),
              "fconv_o": (L, 128, 44, 10), "fconv_s_o": (L, 128, 704), "sc_o": (L, 128, 2, 8, 64),
              "sn_o": (L, 128, 16), "sm_o": (L, 128, 16), "sssm_o": (L, 128, 2, 8, 128)}
    outs = {n: nc.dram_tensor(n, s, mybir.dt.float32, kind="ExternalOutput").ap() for n, s in shapes.items()}
    trunk_kernel(nc, *[dram(n) for n in ("x", "pages", "consts", "vecs", "states", "c_state", "d_state",
                                         "k_c", "v_c", "w_proj", "w_gate", "w_br", "w_out", "w_up", "w_down")],
                 *outs.values())
    res = run_bass_kernel_spmd(nc, [arr], core_ids=[0]).results[0]
    o = {n: np.asarray(res[n]) for n in shapes}

    y = o["y_o"].transpose(2, 1, 0).reshape(TOK, DM)

    def rows(t, c):
        return t.reshape(L, -1, c, TOK).transpose(0, 3, 2, 1).reshape(L, TOK, -1)
    both = {}
    for name, t, c, tail in (("a_k", o["ka_o"], 1, (2, 64)), ("a_v", o["va_o"], 1, (2, 64)),
                             ("kidx", o["ki_o"], 1, (64,)), ("b_k", o["kb_o"], 2, (4, 64)),
                             ("b_v", o["vb_o"], 2, (4, 64))):
        t = rows(t, c)
        both["p_" + name] = t[:, None, :NPR].reshape((L, 1, NPR) + tail)
        both["s_" + name] = t[:, NPR:, None].reshape((L, NSM, 1) + tail)
    p_c = o["pc_o"].reshape(L, 2, 64, 2, 64).transpose(0, 3, 1, 2, 4).reshape(L, 1, 4, 64, 64)
    p_n = o["pn_o"].reshape(L, 2, 64, 2).transpose(0, 3, 1, 2).reshape(L, 1, 4, 64)
    p_m = o["pm_o"].reshape(L, 1, 4)
    dco = o["dconv_o"]
    p_dc = dco[..., :3].transpose(0, 3, 2, 1).reshape(L, 1, 3, 768)
    s_old = o["dconv_s_o"].reshape(L, 128, 6, 3, 8)[:, :, :, 1:]
    s_dc = np.concatenate([s_old, dco[:, :, :, None, 3:]], 3).transpose(0, 4, 3, 2, 1).reshape(L, 8, 3, 768)
    p_h = o["pssm_o"].reshape(L, 2, 64, 2, 128).transpose(0, 3, 1, 2, 4).reshape(L, 1, 4, 64, 128)
    fco = o["fconv_o"]
    p_fc = fco[..., :2].transpose(0, 3, 2, 1).reshape(L, 1, 2, 2 * DFF)
    f_old = o["fconv_s_o"].reshape(L, 128, 44, 2, 8)[:, :, :, 1:]
    s_fc = np.concatenate([f_old, fco[:, :, :, None, 2:]], 3).transpose(0, 4, 3, 2, 1).reshape(L, 8, 2, 2 * DFF)
    s_c = o["sc_o"].reshape(L, 2, 64, 2, 8, 64).transpose(0, 4, 3, 1, 2, 5).reshape(L, 8, 4, 64, 64)
    s_n = o["sn_o"].reshape(L, 2, 64, 2, 8).transpose(0, 4, 3, 1, 2).reshape(L, 8, 4, 64)
    s_m = o["sm_o"].reshape(L, 2, 64, 2, 8)[:, :, 0].transpose(0, 3, 2, 1).reshape(L, 8, 4)
    s_h = o["sssm_o"].reshape(L, 2, 64, 2, 8, 128).transpose(0, 4, 3, 1, 2, 5).reshape(L, 8, 4, 64, 128)
    out = (y[None, :NPR], y[NPR:, None], both["p_a_k"], both["p_a_v"], both["p_kidx"], both["p_b_k"],
           both["p_b_v"], p_c, p_n, p_m, p_dc, p_h, p_fc, both["s_a_k"], both["s_a_v"], both["s_kidx"],
           both["s_b_k"], both["s_b_v"], s_c, s_n, s_m, s_dc, s_h, s_fc)
    return tuple(np.ascontiguousarray(t) for t in out)
```
